# Optimizing a Trainium2 kernel written in Bass

```python
import math
import jax
import jax.numpy as jnp
from jax import lax
import numpy as np

D_MODEL = 2048
BATCH = 1
SEQ = 256
DEPTH = 2

N_A_LAYERS = DEPTH // 2
N_B_LAYERS = DEPTH - N_A_LAYERS
Q_BLOCK = 128
ROPE_THETA = 10000.0
NORM_EPS = 1e-6

MLA_HEADS = 12
MLA_NOPE_DIM = 128
MLA_ROPE_DIM = 64
MLA_V_DIM = 128
Q_LORA_RANK = 512
KV_LORA_RANK = 512

DIFF_HEADS = 6
DIFF_HEAD_DIM = 128
DIFF_V_DIM = 2 * DIFF_HEAD_DIM

MEM_TOKENS = 256
MEM_HEADS = 4
MEM_HEAD_DIM = 128

D_FF = 5632
CONV_WIDTH = 3

A_IN_WIDTH = Q_LORA_RANK + KV_LORA_RANK + MLA_ROPE_DIM + MEM_HEADS * MEM_HEAD_DIM
B_IN_WIDTH = DIFF_HEADS * 2 * DIFF_HEAD_DIM + MEM_HEADS * MEM_HEAD_DIM
A_OUT_WIDTH = MLA_HEADS * MLA_V_DIM + MEM_HEADS * MEM_HEAD_DIM
B_OUT_WIDTH = DIFF_HEADS * DIFF_V_DIM + MEM_HEADS * MEM_HEAD_DIM
SHARED_KV_WIDTH = DIFF_HEADS * (2 * DIFF_HEAD_DIM + DIFF_V_DIM)

kernel_name = 'hybrid_mla_diffattn_yoco_convffn'

def rms_norm(x, gain):
    xf = x.astype(jnp.float32)
    xf = xf * lax.rsqrt(jnp.mean(xf * xf, axis=-1, keepdims=True) + NORM_EPS)
    return xf.astype(x.dtype) * gain

def rope(x, pos):
    dh = x.shape[-1]
    half = dh // 2
    inv_freq = jnp.exp(-math.log(ROPE_THETA) * jnp.arange(half, dtype=jnp.float32) * (2.0 / dh))
    ang = pos.astype(jnp.float32)[..., None] * inv_freq
    cos = jnp.cos(ang)[:, :, None, :]
    sin = jnp.sin(ang)[:, :, None, :]
    xf = x.astype(jnp.float32)
    x1, x2 = xf[..., :half], xf[..., half:]
    return jnp.concatenate([x1 * cos - x2 * sin, x2 * cos + x1 * sin], axis=-1).astype(x.dtype)

def _to_blocks(q):
    b, s = q.shape[:2]
    return jnp.moveaxis(q.reshape((b, s // Q_BLOCK, Q_BLOCK) + q.shape[2:]), 1, 0)

def _from_blocks(o):
    nb, b = o.shape[:2]
    return jnp.moveaxis(o, 0, 1).reshape((b, nb * Q_BLOCK) + o.shape[3:])

def _causal_mask(blk, s):
    q_pos = blk * Q_BLOCK + jnp.arange(Q_BLOCK)
    return jnp.arange(s)[None, :] <= q_pos[:, None]

def causal_attention(q, k, v, scale):
    s = k.shape[1]

    def one_block(args):
        blk, q_blk = args
        sc = jnp.einsum('bqhd,bkhd->bhqk', q_blk, k).astype(jnp.float32) * scale
        sc = jnp.where(_causal_mask(blk, s), sc, -jnp.inf)
        p = jax.nn.softmax(sc, axis=-1).astype(v.dtype)
        return jnp.einsum('bhqk,bkhd->bqhd', p, v)

    nb = s // Q_BLOCK
    return _from_blocks(lax.map(one_block, (jnp.arange(nb), _to_blocks(q))))

def differential_attention(q1, q2, k1, k2, v, lam, scale):
    s = k1.shape[1]

    def one_block(args):
        blk, q1_blk, q2_blk = args
        mask = _causal_mask(blk, s)
        s1 = jnp.einsum('bqhd,bkhd->bhqk', q1_blk, k1).astype(jnp.float32) * scale
        s2 = jnp.einsum('bqhd,bkhd->bhqk', q2_blk, k2).astype(jnp.float32) * scale
        p = (jax.nn.softmax(jnp.where(mask, s1, -jnp.inf), axis=-1)
             - lam * jax.nn.softmax(jnp.where(mask, s2, -jnp.inf), axis=-1))
        return jnp.einsum('bhqk,bkhd->bqhd', p.astype(v.dtype), v)

    nb = s // Q_BLOCK
    return _from_blocks(lax.map(one_block, (jnp.arange(nb), _to_blocks(q1), _to_blocks(q2))))

def memory_attention(q_mem, mem, mem_gain, w_mem_kv):
    b, s = q_mem.shape[:2]
    m = mem.shape[1]
    q = q_mem.reshape(b, s, MEM_HEADS, MEM_HEAD_DIM)
    kv = (rms_norm(mem, mem_gain) @ w_mem_kv).reshape(b, m, MEM_HEADS, 2 * MEM_HEAD_DIM)
    k, v = kv[..., :MEM_HEAD_DIM], kv[..., MEM_HEAD_DIM:]
    sc = jnp.einsum('bshd,bmhd->bhsm', q, k).astype(jnp.float32) * (MEM_HEAD_DIM ** -0.5)
    p = jax.nn.softmax(sc, axis=-1).astype(v.dtype)
    return jnp.einsum('bhsm,bmhd->bshd', p, v).reshape(b, s, MEM_HEADS * MEM_HEAD_DIM)

def mla_mixer(h, positions, mem, w_in, q_norm, w_uq, kv_norm, w_ukv, mem_norm, w_mem_kv, w_o):
    b, s = h.shape[:2]
    proj = h @ w_in
    i0 = Q_LORA_RANK
    i1 = i0 + KV_LORA_RANK
    i2 = i1 + MLA_ROPE_DIM
    q_lat, kv_lat, k_pe, q_mem = proj[..., :i0], proj[..., i0:i1], proj[..., i1:i2], proj[..., i2:]
    q = (rms_norm(q_lat, q_norm) @ w_uq).reshape(b, s, MLA_HEADS, MLA_NOPE_DIM + MLA_ROPE_DIM)
    q = jnp.concatenate([q[..., :MLA_NOPE_DIM], rope(q[..., MLA_NOPE_DIM:], positions)], axis=-1)
    kv = (rms_norm(kv_lat, kv_norm) @ w_ukv).reshape(b, s, MLA_HEADS, MLA_NOPE_DIM + MLA_V_DIM)
    k_pe = rope(k_pe[:, :, None, :], positions)
    k = jnp.concatenate([kv[..., :MLA_NOPE_DIM],
                         jnp.broadcast_to(k_pe, (b, s, MLA_HEADS, MLA_ROPE_DIM))], axis=-1)
    v = kv[..., MLA_NOPE_DIM:]
    o_main = causal_attention(q, k, v, (MLA_NOPE_DIM + MLA_ROPE_DIM) ** -0.5)
    o_main = o_main.reshape(b, s, MLA_HEADS * MLA_V_DIM)
    o_mem = memory_attention(q_mem, mem, mem_norm, w_mem_kv)
    return jnp.concatenate([o_main, o_mem], axis=-1) @ w_o

def shared_kv(x, positions, gain, w_kv):
    b, s = x.shape[:2]
    kv = (rms_norm(x, gain) @ w_kv).reshape(b, s, DIFF_HEADS, 2 * DIFF_HEAD_DIM + DIFF_V_DIM)
    k1 = rope(kv[..., :DIFF_HEAD_DIM], positions)
    k2 = rope(kv[..., DIFF_HEAD_DIM:2 * DIFF_HEAD_DIM], positions)
    v = kv[..., 2 * DIFF_HEAD_DIM:]
    return k1, k2, v

def diff_mixer(h, positions, mem, k1, k2, v, w_in, lq1, lk1, lq2, lk2, subln,
               mem_norm, w_mem_kv, w_o, lambda_init):
    b, s = h.shape[:2]
    proj = h @ w_in
    nq = DIFF_HEADS * 2 * DIFF_HEAD_DIM
    q = proj[..., :nq].reshape(b, s, DIFF_HEADS, 2 * DIFF_HEAD_DIM)
    q1 = rope(q[..., :DIFF_HEAD_DIM], positions)
    q2 = rope(q[..., DIFF_HEAD_DIM:], positions)
    lam = (jnp.exp(jnp.sum(lq1.astype(jnp.float32) * lk1.astype(jnp.float32)))
           - jnp.exp(jnp.sum(lq2.astype(jnp.float32) * lk2.astype(jnp.float32)))
           + lambda_init)
    o = differential_attention(q1, q2, k1, k2, v, lam, DIFF_HEAD_DIM ** -0.5)
    o = (rms_norm(o, subln) * (1.0 - lambda_init)).reshape(b, s, DIFF_HEADS * DIFF_V_DIM)
    o_mem = memory_attention(proj[..., nq:], mem, mem_norm, w_mem_kv)
    return jnp.concatenate([o, o_mem], axis=-1) @ w_o

def conv_ffn(h, w_in, conv_w, conv_b, w_out):
    s = h.shape[1]
    u = h @ w_in
    up = jnp.pad(u, ((0, 0), (CONV_WIDTH - 1, 0), (0, 0)))
    c = conv_b
    for j in range(CONV_WIDTH):
        c = c + conv_w[j] * up[:, j:j + s]
    g, val = c[..., :D_FF], c[..., D_FF:]
    return (jax.nn.gelu(g, approximate=True) * val) @ w_out

def setup_inputs(seed: int = 0) -> dict:
    key = jax.random.key(seed)
    keys = list(jax.random.split(key, 48))
    f32 = jnp.float32

    def nxt():
        return keys.pop()

    def dense(shape, fan_in):
        return jax.random.normal(nxt(), shape, f32) * (fan_in ** -0.5)

    def gain(shape):
        return 1.0 + 0.05 * jax.random.normal(nxt(), shape, f32)

    def small(shape, scale):
        return scale * jax.random.normal(nxt(), shape, f32)

    na, nb = N_A_LAYERS, N_B_LAYERS
    x = jax.random.normal(nxt(), (BATCH, SEQ, D_MODEL), f32)
    mem = jax.random.normal(nxt(), (BATCH, MEM_TOKENS, D_MODEL), f32)
    offsets = jax.random.randint(nxt(), (BATCH, 1), 0, 4096, dtype=jnp.int32)
    positions = (offsets + jnp.arange(SEQ, dtype=jnp.int32)[None, :]).astype(jnp.int32)
    return {
        'x': x,
        'mem': mem,
        'positions': positions,
        'a_attn_norm_pre': gain((na, D_MODEL)),
        'a_w_in': dense((na, D_MODEL, A_IN_WIDTH), D_MODEL),
        'a_q_norm': gain((na, Q_LORA_RANK)),
        'a_w_uq': dense((na, Q_LORA_RANK, MLA_HEADS * (MLA_NOPE_DIM + MLA_ROPE_DIM)), Q_LORA_RANK),
        'a_kv_norm': gain((na, KV_LORA_RANK)),
        'a_w_ukv': dense((na, KV_LORA_RANK, MLA_HEADS * (MLA_NOPE_DIM + MLA_V_DIM)), KV_LORA_RANK),
        'a_mem_norm': gain((na, D_MODEL)),
        'a_w_mem_kv': dense((na, D_MODEL, MEM_HEADS * 2 * MEM_HEAD_DIM), D_MODEL),
        'a_w_o': dense((na, A_OUT_WIDTH, D_MODEL), A_OUT_WIDTH),
        'a_attn_norm_post': gain((na, D_MODEL)),
        'shared_kv_norm': gain((D_MODEL,)),
        'shared_w_kv': dense((D_MODEL, SHARED_KV_WIDTH), D_MODEL),
        'b_attn_norm_pre': gain((nb, D_MODEL)),
        'b_w_in': dense((nb, D_MODEL, B_IN_WIDTH), D_MODEL),
        'b_lambda_q1': small((nb, DIFF_HEAD_DIM), 0.1),
        'b_lambda_k1': small((nb, DIFF_HEAD_DIM), 0.1),
        'b_lambda_q2': small((nb, DIFF_HEAD_DIM), 0.1),
        'b_lambda_k2': small((nb, DIFF_HEAD_DIM), 0.1),
        'b_subln': gain((nb, DIFF_V_DIM)),
        'b_mem_norm': gain((nb, D_MODEL)),
        'b_w_mem_kv': dense((nb, D_MODEL, MEM_HEADS * 2 * MEM_HEAD_DIM), D_MODEL),
        'b_w_o': dense((nb, B_OUT_WIDTH, D_MODEL), B_OUT_WIDTH),
        'b_attn_norm_post': gain((nb, D_MODEL)),
        'ffn_norm_pre': gain((DEPTH, D_MODEL)),
        'ffn_w_in': dense((DEPTH, D_MODEL, 2 * D_FF), D_MODEL),
        'ffn_conv_w': dense((DEPTH, CONV_WIDTH, 2 * D_FF), CONV_WIDTH),
        'ffn_conv_b': small((DEPTH, 2 * D_FF), 0.01),
        'ffn_w_out': dense((DEPTH, D_FF, D_MODEL), D_FF),
        'ffn_norm_post': gain((DEPTH, D_MODEL)),
    }

def reference(x, mem, positions,
              a_attn_norm_pre, a_w_in, a_q_norm, a_w_uq, a_kv_norm, a_w_ukv,
              a_mem_norm, a_w_mem_kv, a_w_o, a_attn_norm_post,
              shared_kv_norm, shared_w_kv,
              b_attn_norm_pre, b_w_in, b_lambda_q1, b_lambda_k1, b_lambda_q2, b_lambda_k2,
              b_subln, b_mem_norm, b_w_mem_kv, b_w_o, b_attn_norm_post,
              ffn_norm_pre, ffn_w_in, ffn_conv_w, ffn_conv_b, ffn_w_out, ffn_norm_post):
    k1 = k2 = v = None
    for layer in range(DEPTH):
        if layer < N_A_LAYERS:
            i = layer
            mix = mla_mixer(rms_norm(x, a_attn_norm_pre[i]), positions, mem,
                            a_w_in[i], a_q_norm[i], a_w_uq[i], a_kv_norm[i], a_w_ukv[i],
                            a_mem_norm[i], a_w_mem_kv[i], a_w_o[i])
            x = x + rms_norm(mix, a_attn_norm_post[i])
        else:
            j = layer - N_A_LAYERS
            if j == 0:
                k1, k2, v = shared_kv(x, positions, shared_kv_norm, shared_w_kv)
            lambda_init = 0.8 - 0.6 * math.exp(-0.3 * layer)
            mix = diff_mixer(rms_norm(x, b_attn_norm_pre[j]), positions, mem, k1, k2, v,
                             b_w_in[j], b_lambda_q1[j], b_lambda_k1[j], b_lambda_q2[j], b_lambda_k2[j],
                             b_subln[j], b_mem_norm[j], b_w_mem_kv[j], b_w_o[j], lambda_init)
            x = x + rms_norm(mix, b_attn_norm_post[j])
        f = conv_ffn(rms_norm(x, ffn_norm_pre[layer]), ffn_w_in[layer], ffn_conv_w[layer],
                     ffn_conv_b[layer], ffn_w_out[layer])
        x = x + rms_norm(f, ffn_norm_post[layer])
    return x


_drawn_inputs = setup_inputs


def setup_inputs(seed=0):
    import zlib

    import numpy as np

    out = dict(_drawn_inputs(seed))
    spreads = {}
    factors = {'b_attn_norm_pre': 3.885,
     'b_lambda_k2': 22.491,
     'b_mem_norm': 8.0,
     'ffn_conv_b': 4.755,
     'shared_kv_norm': 7.012,
     'b_lambda_q1': 7.459,
     'b_lambda_k1': 3.29,
     'b_subln': 23.281}
    for name, (base, spread) in spreads.items():
        noise = np.random.default_rng([zlib.crc32(name.encode()), seed]).standard_normal(out[name].shape)
        drawn = base * np.exp(spread * noise) if base else spread * noise
        out[name] = jnp.asarray(drawn.astype(out[name].dtype))
    for name, factor in factors.items():
        out[name] = (out[name] * factor).astype(out[name].dtype)
    return out
```

```python
import math
from contextlib import ExitStack

import numpy as np

import concourse.bass as bass
from concourse import mybir

P = 128
F32 = mybir.dt.float32
F32R = mybir.dt.float32r
BF16 = mybir.dt.bfloat16
I32 = mybir.dt.int32
ALU = mybir.AluOpType
ACT = mybir.ActivationFunctionType
AX = mybir.AxisListType.X

S = 256
M = 256
TT = S // P
D = 2048
KC = D // P
AH, NOPE, RD = 12, 128, 64
LORA = 512
BH, HD, VD = 6, 128, 256
MH = 4
F = 5632
FC = F // P
EPS = 1e-6
LAMBDA_INIT = 0.8 - 0.6 * math.exp(-0.3)
THETA = 10000.0
SCALE_A = float(NOPE + RD) ** -0.5
SCALE_B = float(HD) ** -0.5
NEG = -3.0e38

R = 4
AHEAD = 3
DSTEPS = KC // 2
LSTEPS = LORA // P // 2
FSTEPS = FC // 2
FJ = F // 512

MEMA, MEMA_T = 0, 0
MEMB, MEMB_T = MEMA + 2 * DSTEPS, MEMA_T + 2
QLAT, QLAT_T = MEMB + 2 * DSTEPS, MEMB_T + 2
KVLAT, KVLAT_T = QLAT + DSTEPS, QLAT_T + 1
KPE, KPE_T = KVLAT + DSTEPS, KVLAT_T + 1
QMEM, QMEM_T = KPE + 1, KPE_T + 1
UQ, UQ_T = QMEM + DSTEPS, QMEM_T + 1
UKV, UKV_T = UQ + 6 * LSTEPS, UQ_T + 6
OA, OA_T = UKV + 6 * LSTEPS, UKV_T + 6
IN0, IN0_T = OA + 4 * DSTEPS, OA_T + 4
OUT0, OUT0_T = IN0 + 2 * FJ * DSTEPS, IN0_T + 2 * FJ
SKV, SKV_T = OUT0 + 4 * FSTEPS, OUT0_T + 4
BQ, BQ_T = SKV + BH * DSTEPS, SKV_T + BH
OB, OB_T = BQ + 4 * DSTEPS, BQ_T + 4
IN1, IN1_T = OB + 4 * DSTEPS, OB_T + 4
OUT1, OUT1_T = IN1 + 2 * FJ * DSTEPS, IN1_T + 2 * FJ
STEPS, TILES = OUT1 + 4 * FSTEPS, OUT1_T + 4

GROUPS = [("C", 3), ("N", 8), ("N", 8), ("N", 2), ("N", 2), ("C", 1), ("C", 6), ("N", 8),
          ("N", 8), ("C", 6), ("C", 6), ("N", 6), ("N", 8)]
(T_SETUP, T_MEM, T_X, T_QLAT, T_KVLAT, T_KPE, T_QPE, T_FFN0, T_B, T_KB, T_QB, T_SUB,
 T_FFN1) = range(len(GROUPS))

GAIN_ROWS = {}
_row = 0
for _name, _n in (("a_pre", KC), ("a_mem", KC), ("b_mem", KC), ("b_pre", KC), ("shared", KC),
                  ("ffn_pre", 2 * KC), ("q_norm", 4), ("kv_norm", 4), ("subln", 2)):
    GAIN_ROWS[_name] = _row
    _row += _n
N_GAIN = _row


N_SMALL = 9 + 4 + 4 + 1 + TT
ROUND = 1.5 * 2.0 ** 23
TWO_PI = (6.28125, float(np.float32(np.round((2 * math.pi - 6.28125) * 2 ** 20) / 2 ** 20)), None)
TWO_PI = TWO_PI[:2] + (2 * math.pi - TWO_PI[0] - TWO_PI[1],)
SIN_MAX = 3.1415925


def groups_before(phase, kind=None):
    return sum(n for k, n in GROUPS[:phase] if kind in (None, k))


def val(const, per, i):
    return const if i is None else i * per + const


def program(nc, x_in, mem_in, positions, inv_freq, w, vec, out):
    with ExitStack() as ctx:
        sem = lambda name: ctx.enter_context(nc.semaphore(name))
        base = 16512

        def at(name, shape, dt, offset):
            return nc.alloc_sbuf_tensor_at(name, shape, dt, offset=base + offset)

        KB = 1024
        X0, XT0, RING0, KVB0, H0, M0 = 0, 16 * KB, 48 * KB, 96 * KB, 104 * KB, 192 * KB
        x = at("x", [P, TT, D], F32, X0)
        xT_hi = at("xT_hi", [P, KC, S], F32R, XT0)
        xT_lo = at("xT_lo", [P, KC, S], F32R, XT0 + 16 * KB)
        w_raw = at("w_raw", [P, R, 1024], F32, RING0)
        w_hi = at("w_hi", [P, R, 1024], F32R, RING0 + 16 * KB)
        w_lo = at("w_lo", [P, R, 1024], F32R, RING0 + 32 * KB)
        y_f = at("y_f", [P, TT, D], F32, XT0)
        gain_f = at("gain_f", [P, D], F32, XT0 + 16 * KB)
        kmT_b = at("kmT_b", [P, MH, M], F32, KVB0)
        vm_b = at("vm_b", [P, 2, MH, P], F32, KVB0 + 4 * KB)
        mTa_hi = at("mTa_hi", [P, KC, M], F32R, H0)
        mTa_lo = at("mTa_lo", [P, KC, M], F32R, H0 + 16 * KB)
        mTb_hi = at("mTb_hi", [P, KC, M], F32R, H0 + 32 * KB)
        mTb_lo = at("mTb_lo", [P, KC, M], F32R, H0 + 48 * KB)
        mem = at("mem", [P, 2, D], F32, H0 + 64 * KB)
        gain_rows = at("gain_rows", [P, P], F32, H0 + 80 * KB)
        conv_rows = at("conv_rows", [2 * FC, 2, 4, P], F32, H0 + 81 * KB)
        lam_rows = at("lam_rows", [P, 4, P], F32, H0 + 85 * KB)
        freq = at("freq", [P, 96], F32, H0 + 87 * KB)
        angle = at("angle", [P, TT, 96], F32, KVB0)
        turns = at("turns", [P, 2, TT, 96], F32, KVB0 + KB)
        rope_k = at("rope_k", [P, 2, TT, 96], F32, KVB0 + 3 * KB)
        latq_hi = at("latq_hi", [P, 4, S], F32R, H0)
        latq_lo = at("latq_lo", [P, 4, S], F32R, H0 + 4 * KB)
        latk_hi = at("latk_hi", [P, 4, S], F32R, H0 + 8 * KB)
        latk_lo = at("latk_lo", [P, 4, S], F32R, H0 + 12 * KB)
        lat = at("lat", [P, 2, TT, LORA], F32, H0 + 16 * KB)
        qnT = at("qnT", [P, AH, S], F32, H0 + 24 * KB)
        kT_a = at("kT_a", [P, AH, S], F32, H0 + 36 * KB)
        v_a = at("v_a", [P, TT, AH, P], F32, H0 + 48 * KB)
        qmT_a = at("qmT_a", [P, MH, S], F32, H0 + 60 * KB)
        kmT_a = at("kmT_a", [P, MH, M], F32, H0 + 64 * KB)
        vm_a = at("vm_a", [P, 2, MH, P], F32, H0 + 68 * KB)
        qpT = at("qpT", [P, AH // 2, S], F32, H0 + 72 * KB)
        kpT = at("kpT", [P, S], F32, H0 + 78 * KB)
        diag_kv = at("diag_kv", [P, TT, P], F32, H0 + 79 * KB)
        xbT_hi = at("xbT_hi", [P, KC, S], F32R, H0)
        xbT_lo = at("xbT_lo", [P, KC, S], F32R, H0 + 16 * KB)
        kT_b = at("kT_b", [P, 2 * BH, S], F32, H0 + 32 * KB)
        v_b = at("v_b", [P, TT, BH, VD], F32, H0 + 44 * KB)
        qT_b = at("qT_b", [P, 2 * BH, S], F32, H0 + 56 * KB)
        qmT_b = at("qmT_b", [P, MH, S], F32, H0 + 68 * KB)
        o_nat = at("o_nat", [P, BH, TT, VD], F32, H0)
        probs = at("probs", [P, 2, 2, 512], F32, H0 + 12 * KB)
        pT = at("pT", [P, 2, 512], F32, H0 + 20 * KB)
        y_o = at("y_o", [P, TT, D], F32, H0 + 24 * KB)
        gain_o = at("gain_o", [P, D], F32, H0 + 80 * KB)
        hT_hi = at("hT_hi", [P, FC, S], F32R, H0)
        hT_lo = at("hT_lo", [P, FC, S], F32R, H0 + 44 * KB)
        scratch = at("scratch", [P, 2, 4, S], F32, M0)
        conv = at("conv", [P, 2, 4, 2 * FC], F32, M0 + 8 * KB)
        m = M0 + 8 * KB + 2816
        gcol = at("gcol", [P, P], F32, m)
        ident = at("ident", [P, P], F32, m + 512)
        diag = at("diag", [P, TT, P], F32, m + 1024)
        cosine = at("cosine", [P, TT, 96], F32, m + 2048)
        sine = at("sine", [P, TT, 96], F32, m + 2816)
        ident_b = at("ident_b", [P, P], BF16, m + 3584)
        mask_b = at("mask_b", [P, P], BF16, m + 3840)
        stat = at("stat", [P, 4, 8], F32, m + 4096)
        ssp = at("ssp", [P, 2, 8], F32, m + 4224)
        nrm = at("nrm", [P, 8], F32, m + 4288)
        osum = at("osum", [P, 3, 12], F32, m + 4320)
        neglam = at("neglam", [P, 4], F32, m + 4480)
        eps = at("eps", [P, 1], F32, m + 4512)
        pos_i = at("pos_i", [P, TT], I32, m + 4544)
        pos_f = at("pos_f", [P, TT], F32, m + 4576)
        assert m + 4608 + base <= 229344

        ps = ctx.enter_context(nc.psum_tensor("ps", [P, 8, 512], F32))

        w_landed = [sem(f"w_landed{k}") for k in range(R)]
        small_landed = sem("small_landed")
        mem_landed = [sem(f"mem_landed{t}") for t in range(2)]
        x_landed = [sem(f"x_landed{t}") for t in range(TT)]
        gain_landed = sem("gain_landed")
        out_stored = sem("out_stored")
        hi_ready = sem("hi_ready")
        lo_ready = sem("lo_ready")
        step_used = sem("step_used")
        pair_act = sem("pair_act")
        pair_dve = sem("pair_dve")
        consts_ready = sem("consts_ready")
        pool_step = sem("pool_step")
        tr_ready = sem("tr_ready")
        tr_copied = sem("tr_copied")
        tr_hi = sem("tr_hi")
        tr_lo = sem("tr_lo")
        sq_ready = sem("sq_ready")
        ss_ready = sem("ss_ready")
        std_ready = sem("std_ready")
        diag_ready = sem("diag_ready")
        x_piece = sem("x_piece")
        rope_ready = sem("rope_ready")
        range_ready = sem("range_ready")
        trig_ready = sem("trig_ready")
        lam_prod = sem("lam_prod")
        lam_exp = sem("lam_exp")
        s_ready = sem("s_ready")
        max_ready = sem("max_ready")
        e_ready = sem("e_ready")
        p_ready = sem("p_ready")
        pT_ready = sem("pT_ready")
        pT_copied = sem("pT_copied")
        o_ready = sem("o_ready")
        o_hi = sem("o_hi")
        o_lo = sem("o_lo")
        on_scaled = sem("on_scaled")
        dve_link = sem("dve_link")
        gate_ready = sem("gate_ready")
        h_ready = sem("h_ready")
        h_hi = sem("h_hi")
        h_lo = sem("h_lo")
        ostd_ready = sem("ostd_ready")

        ITEMS_A = [("mla", h) for h in range(AH)] + [("mem", h) for h in range(MH)]
        ITEMS_B = [("diff", h) for h in range(BH)] + [("mem", h) for h in range(MH)]

        view = {k: v.rearrange("(c p) n -> p c n", p=P) for k, v in w.items()}

        blk = ctx.enter_context(nc.Block())

        @blk.sync
        def _(sp):
            def load(s, src, per=0, i=None, width=1024):
                if s >= R:
                    sp.wait_ge(lo_ready, val(s - R + 1, per, i))
                dst = w_raw[:, s % R, 0:width]
                sp.dma_start(dst.rearrange("p (c n) -> p c n", c=src.shape[1]), src)\
                    .then_inc(w_landed[s % R], 16)

            def tile(s0, name, steps, n0, per=0, i=None, width=512):
                cols = slice(n0, n0 + width) if i is None else bass.ds(n0, width)
                for k in range(steps):
                    load(s0 + k, view[name][:, 2 * k:2 * k + 2, cols], per, i, 2 * width)

            for t in range(2):
                sp.dma_start(mem[:, t, :], mem_in[t * P:(t + 1) * P, :]).then_inc(mem_landed[t], 16)
            for j in range(2):
                tile(MEMA + j * DSTEPS, "a_w_mem_kv", DSTEPS, 512 * j)
            for j in range(2):
                tile(MEMB + j * DSTEPS, "b_w_mem_kv", DSTEPS, 512 * j)
            tile(QLAT, "a_w_in", DSTEPS, 0)
            tile(KVLAT, "a_w_in", DSTEPS, LORA)
            load(KPE, view["a_w_in"][:, :, 2 * LORA:2 * LORA + RD])
            tile(QMEM, "a_w_in", DSTEPS, 2 * LORA + RD)
            for j in range(6):
                tile(UQ + j * LSTEPS, "a_w_uq", LSTEPS, 384 * j, width=384)
            for j in range(6):
                tile(UKV + j * LSTEPS, "a_w_ukv", LSTEPS, 512 * j)
            with sp.Fori(0, 2) as i:
                for j in range(2):
                    tile(OA + j * DSTEPS, "a_w_o", DSTEPS, i * 1024 + 512 * j, 2 * DSTEPS, i)
            for layer, s_in, s_out in ((0, IN0, OUT0), (1, IN1, OUT1)):
                if layer == 1:
                    with sp.Fori(0, BH // 2) as i:
                        for j in range(2):
                            tile(SKV + j * DSTEPS, "shared_w_kv", DSTEPS, i * 1024 + 512 * j,
                                 2 * DSTEPS, i)
                    with sp.Fori(0, 2) as i:
                        for j in range(2):
                            tile(BQ + j * DSTEPS, "b_w_in", DSTEPS, i * 1024 + 512 * j,
                                 2 * DSTEPS, i)
                    with sp.Fori(0, 2) as i:
                        for j in range(2):
                            tile(OB + j * DSTEPS, "b_w_o", DSTEPS, i * 1024 + 512 * j,
                                 2 * DSTEPS, i)
                with sp.Fori(0, FJ) as i:
                    tile(s_in, f"ffn_w_in{layer}", DSTEPS, i * 512, 2 * DSTEPS, i)
                    tile(s_in + DSTEPS, f"ffn_w_in{layer}", DSTEPS, i * 512 + F, 2 * DSTEPS, i)
                with sp.Fori(0, 2) as i:
                    for j in range(2):
                        tile(s_out + j * FSTEPS, f"ffn_w_out{layer}", FSTEPS,
                             i * 1024 + 512 * j, 2 * FSTEPS, i)
            for q in range(4):
                sp.wait_ge(x_piece, 12 + q + 1)
                t, half = q // 2, q % 2
                sp.dma_start(out[t * P:(t + 1) * P, half * 1024:(half + 1) * 1024],
                             x[:, t, half * 1024:(half + 1) * 1024]).then_inc(out_stored, 16)
            sp.wait_ge(out_stored, 64)

        @blk.gpsimd
        def _(pool):
            for name, rows in vec["rows"]:
                r0 = GAIN_ROWS[name]
                pool.dma_start(gain_rows[r0:r0 + rows.shape[0], :], rows).then_inc(small_landed, 16)
            for layer in range(2):
                pool.dma_start(conv_rows[:, layer, 0:3, :],
                               vec["conv_w"][layer].rearrange("j (c p) -> c j p", p=P))\
                    .then_inc(small_landed, 16)
                pool.dma_start(conv_rows[:, layer, 3, :],
                               vec["conv_b"][layer].rearrange("(c p) -> c p", p=P))\
                    .then_inc(small_landed, 16)
            for k in range(4):
                pool.dma_start(lam_rows[:, k, :], vec["lambda"][k].partition_broadcast(P))\
                    .then_inc(small_landed, 16)
            pool.dma_start(freq[:, :], inv_freq.partition_broadcast(P)).then_inc(small_landed, 16)
            for t in range(TT):
                pool.dma_start(pos_i[:, t:t + 1],
                               positions[t * P:(t + 1) * P].rearrange("(p a) -> p a", a=1))\
                    .then_inc(small_landed, 16)
            nc.gpsimd.memset(ident[:, :], 0.0).then_inc(pool_step, 1)
            nc.gpsimd.memset(ident_b[:, :], 0.0).then_inc(pool_step, 1)
            nc.gpsimd.memset(mask_b[:, :], 0.0).then_inc(pool_step, 1)
            pool.wait_ge(pool_step, 3)
            for t in (ident, ident_b):
                nc.gpsimd.affine_select(out=t[:, :], in_=t[:, :], compare_op=ALU.not_equal,
                                        fill=1.0, base=0, pattern=[[-1, P]], channel_multiplier=1)\
                    .then_inc(consts_ready, 1)
            nc.gpsimd.affine_select(out=mask_b[:, :], in_=mask_b[:, :], compare_op=ALU.is_ge,
                                    fill=NEG, base=0, pattern=[[-1, P]], channel_multiplier=1)\
                .then_inc(consts_ready, 1)
            nc.gpsimd.memset(eps[:, :], EPS).then_inc(consts_ready, 1)
            pool.wait_ge(tr_copied, 3)
            pool.wait_ge(trig_ready, 1)
            pool.wait_ge(lam_prod, 1)
            pool.dma_start(gain_o[:, :], vec["a_post"].partition_broadcast(P))\
                .then_inc(gain_landed, 16)
            for k, (name, dst, step) in enumerate((("ffn_post0", gain_f, OUT0),
                                                   ("b_post", gain_o, OUT0),
                                                   ("ffn_post1", gain_f, OUT1))):
                if dst is gain_f:
                    pool.wait_ge(step_used, step)
                else:
                    pool.wait_ge(step_used, SKV)
                pool.dma_start(dst[:, :], vec[name].partition_broadcast(P)).then_inc(gain_landed, 16)

        @blk.tensor
        def _(pe):
            def release(tile_no, per=0, i=None):
                if tile_no >= 2:
                    pe.wait_ge(pair_act, val(tile_no - 1, per, i))
                    pe.wait_ge(pair_dve, val(tile_no - 1, per, i))

            def product(s0, steps, tile_no, xhi, xlo, parts, width=512, chunks=2, per=0, i=None,
                        per_t=0):
                release(tile_no, per_t, i)
                pair = 2 * (tile_no % 2)
                for k in range(steps):
                    pe.wait_ge(lo_ready, val(s0 + k + 1, per, i))
                    slot = (s0 + k) % R
                    for c in range(chunks):
                        wh = w_hi[:, slot, c * width:(c + 1) * width]
                        wl = w_lo[:, slot, c * width:(c + 1) * width]
                        ch = k * chunks + c
                        seen = set()
                        for mode, bank, o0, on, tok, cols in parts:
                            dst = ps[:, pair + bank, o0:o0 + on]
                            first = ch == 0 and bank not in seen
                            seen.add(bank)
                            last = ch == steps * chunks - 1
                            a_hi, a_lo = xhi[:, ch, tok], xlo[:, ch, tok]
                            pairs = [(a_hi, cols(wh)), (a_hi, cols(wl)), (a_lo, cols(wh))]
                            if mode == "T":
                                pairs = [(b, a) for a, b in (pairs[0], pairs[2], pairs[1])]
                            for q, (st, mv) in enumerate(pairs):
                                mm = nc.tensor.matmul(dst, st, mv, start=first and q == 0,
                                                      stop=last and q == 2, skip_group_check=True)
                    mm.then_inc(step_used, 1)

            whole = lambda n: (lambda a: a[:, 0:n])
            every = slice(0, S)
            tok_t = [slice(0, P), slice(P, S)]

            def n_parts(width=512):
                return [("N", t, 0, width, tok_t[t], whole(width)) for t in range(TT)]

            def t_parts():
                return [("T", k // 2, 256 * (k % 2), 256, every,
                         (lambda a, k=k: a[:, k * P:(k + 1) * P])) for k in range(4)]

            def kv_parts():
                ks = [("T", 0, 256 * h, 256, every,
                       (lambda a, h=h: a[:, 256 * h:256 * h + P])) for h in range(2)]
                pick = lambda a: a.rearrange("p (h n) -> p h n", h=2)[:, :, P:2 * P]
                return ks + [("N", 1, 256 * t, 256, tok_t[t], pick) for t in range(TT)]

            def uq_parts():
                qs = [("T", 0, 256 * h, 256, every,
                       (lambda a, h=h: a[:, 192 * h:192 * h + P])) for h in range(2)]
                pick = lambda a: a.rearrange("p (h n) -> p h n", h=2)[:, :, P:P + RD]
                return qs + [("N", 1, 128 * t, 128, tok_t[t], pick) for t in range(TT)]

            done = {"C": 0, "N": 0}
            items_done = [0]

            def phase_free():
                if done["N"]:
                    pe.wait_ge(tr_lo, done["N"])
                if done["C"]:
                    pe.wait_ge(tr_copied, done["C"])
                if items_done[0]:
                    pe.wait_ge(o_lo, items_done[0])

            def norm_transpose(src, chunks, diag_no, diag=diag):
                phase_free()
                pe.wait_ge(diag_ready, diag_no)
                for g in range(chunks // 2):
                    if g >= 4:
                        pe.wait_ge(tr_lo, done["N"] + g - 3)
                    for c in range(2):
                        for t in range(TT):
                            f0 = (2 * g + c) * P
                            mm = nc.tensor.matmul(ps[:, 4 + g % 4, 256 * c + P * t:256 * c + P * t + P],
                                                  src[:, t, f0:f0 + P], diag[:, t, :],
                                                  start=True, stop=True)
                    mm.then_inc(tr_ready, 1)
                done["N"] += chunks // 2

            def rope_transpose(bank, blocks, rope_no):
                pe.wait_ge(rope_ready, rope_no)
                for k, src in enumerate(blocks):
                    mm = nc.tensor.transpose(ps[:, bank, P * k:P * (k + 1)], src, ident[:, :])
                mm.then_inc(tr_ready, 1)
                done["C"] += 1

            rot = scratch[:, 0].rearrange("p a b -> p (a b)")

            def attend(items, km, vm, first_item):
                phase_free()
                pe.wait_ge(pair_act, pair_count[0])
                pe.wait_ge(pair_dve, pair_count[0])
                t0 = first_item

                def scores(t):
                    kind, h = items[t]
                    lag = 2 if is_b else 4
                    if t >= lag:
                        pe.wait_ge(e_ready, t0 + t - lag + 1)
                    if kind == "mem":
                        b = 2 * (t % 2) if is_b else t % 4
                        for q in range(TT):
                            mm = nc.tensor.matmul(ps[:, b, 256 * q:256 * q + M],
                                                  qm[:, h, q * P:(q + 1) * P], km[:, h, :],
                                                  start=q == 0, stop=True, skip_group_check=True)
                    else:
                        for j in range(2 if kind == "diff" else 1):
                            b = 2 * (t % 2) + j if is_b else t % 4
                            for q in range(TT):
                                dst = ps[:, b, P * q:P * q + (q + 1) * P]
                                n = (q + 1) * P
                                if kind == "diff":
                                    g = 2 * h + j
                                    nc.tensor.matmul(dst, qT_b[:, g, q * P:(q + 1) * P],
                                                     kT_b[:, g, 0:n], start=q == 0, stop=False,
                                                     skip_group_check=True)
                                else:
                                    nc.tensor.matmul(dst, qnT[:, h, q * P:(q + 1) * P],
                                                     kT_a[:, h, 0:n], start=q == 0, stop=False,
                                                     skip_group_check=True)
                                    r0 = RD * (h % 2)
                                    nc.tensor.matmul(dst, qpT[r0:r0 + RD, h // 2, q * P:(q + 1) * P],
                                                     kpT[r0:r0 + RD, 0:n], start=False, stop=False,
                                                     skip_group_check=True)
                                mm = nc.tensor.matmul(ps[:, b, P * 2 * q:P * 2 * q + P],
                                                      ident_b[:, :], mask_b[:, :], start=False,
                                                      stop=True, skip_group_check=True)
                    mm.then_inc(s_ready, 1)

                def transposes(t):
                    kind, h = items[t]
                    pe.wait_ge(p_ready, t0 + t + 1)
                    if t >= 2:
                        pe.wait_ge(pT_copied, t0 + t - 1)
                    src = probs[:, t % 2, 0, :]
                    dst = ps[:, 4 + t % 2, :]
                    if kind == "mem":
                        moves = [(256 * q + P * k, 256 * k + P * q) for q in range(2) for k in range(2)]
                    else:
                        moves = [(0, 0), (P, P), (2 * P, 2 * P)]
                    for a, b in moves:
                        mm = nc.tensor.transpose(dst[:, b:b + P], src[:, a:a + P], ident[:, :])
                    mm.then_inc(pT_ready, 1)

                def outputs(t):
                    kind, h = items[t]
                    pe.wait_ge(pT_copied, t0 + t + 1)
                    if t >= 2:
                        pe.wait_ge(o_lo, t0 + t - 1)
                    p = pT[:, t % 2, :]
                    dst = ps[:, 6 + t % 2, :]
                    if kind == "mem":
                        for k in range(2):
                            mm = nc.tensor.matmul(dst[:, 0:S], vm[:, k, h, :],
                                                  p[:, 256 * k:256 * k + S], start=k == 0, stop=k == 1)
                    elif kind == "mla":
                        nc.tensor.matmul(dst[:, 0:S], v_a[:, 0, h, :], p[:, 0:S], start=True,
                                         stop=False, skip_group_check=True)
                        mm = nc.tensor.matmul(dst[:, P:S], v_a[:, 1, h, :], p[:, 2 * P:3 * P],
                                              start=False, stop=True, skip_group_check=True)
                    else:
                        nc.tensor.matmul(dst[:, 0:VD], p[:, 0:P], v_b[:, 0, h, :], start=True,
                                         stop=True, skip_group_check=True)
                        nc.tensor.matmul(dst[:, VD:2 * VD], p[:, P:2 * P], v_b[:, 0, h, :],
                                         start=False, stop=False, skip_group_check=True)
                        mm = nc.tensor.matmul(dst[:, VD:2 * VD], p[:, 2 * P:3 * P], v_b[:, 1, h, :],
                                              start=False, stop=True, skip_group_check=True)
                    mm.then_inc(o_ready, 1)

                is_b = first_item > 0
                qm = qmT_b if is_b else qmT_a
                n = len(items)
                lead = 1 if is_b else 3
                for t in range(lead):
                    scores(t)
                for t in range(n + 1):
                    if t + lead < n:
                        scores(t + lead)
                    if t < n:
                        transposes(t)
                    if t >= 1:
                        outputs(t - 1)
                items_done[0] += n

            pair_count = [0]

            pe.wait_ge(small_landed, 16 * N_SMALL)
            pe.wait_ge(consts_ready, 4)
            nc.tensor.transpose(ps[:, 4, 0:N_GAIN], gain_rows[0:N_GAIN, :],
                                ident[0:N_GAIN, 0:N_GAIN]).then_inc(tr_ready, 1)
            for layer in range(2):
                for k in range(4):
                    mm = nc.tensor.transpose(ps[:, 5 + layer, 88 * k:88 * (k + 1)],
                                             conv_rows[:, layer, k, :], ident[0:2 * FC, 0:2 * FC])
                mm.then_inc(tr_ready, 1)
            done["C"] = 3

            norm_transpose(mem, KC, 1)
            for j in range(2):
                pe.wait_ge(tr_lo, 8)
                product(MEMA + j * DSTEPS, DSTEPS, MEMA_T + j, mTa_hi, mTa_lo, kv_parts())
            norm_transpose(x, KC, 2)
            for j in range(2):
                product(MEMB + j * DSTEPS, DSTEPS, MEMB_T + j, mTb_hi, mTb_lo, kv_parts())
            pe.wait_ge(tr_lo, done["N"])
            product(QLAT, DSTEPS, QLAT_T, xT_hi, xT_lo, n_parts())
            product(KVLAT, DSTEPS, KVLAT_T, xT_hi, xT_lo, n_parts())
            product(KPE, 1, KPE_T, xT_hi, xT_lo, n_parts(RD), width=RD, chunks=KC)
            product(QMEM, DSTEPS, QMEM_T, xT_hi, xT_lo, t_parts())
            norm_transpose(lat[:, 0], 4, 3)
            norm_transpose(lat[:, 1], 4, 4, diag_kv)
            phase_free()
            rope_transpose(4, [rot[:, P * t:P * (t + 1)] for t in range(TT)], 1)
            qpe_blocks = [rot[:, P * t:P * (t + 1)] for t in range(TT)]
            for j in range(6):
                product(UQ + j * LSTEPS, LSTEPS, UQ_T + j, latq_hi, latq_lo, uq_parts(), width=384)
                if j == 0:
                    phase_free()
                else:
                    if j >= 3:
                        pe.wait_ge(tr_copied, groups_before(T_QPE, "C") + j - 2)
                    rope_transpose(4 + (j - 1) % 2, qpe_blocks, 1 + j)
            for j in range(6):
                product(UKV + j * LSTEPS, LSTEPS, UKV_T + j, latk_hi, latk_lo, kv_parts())
                if j == 0:
                    pe.wait_ge(tr_copied, groups_before(T_QPE, "C") + 4)
                    rope_transpose(5, qpe_blocks, 7)
            pair_count[0] = OA_T
            attend(ITEMS_A, kmT_a, vm_a, 0)

            def wide_product(s0, t0, steps, xhi, xlo):
                with pe.Fori(0, 2) as i:
                    for j in range(2):
                        product(s0 + j * steps, steps, t0 + j, xhi, xlo, n_parts(),
                                per=2 * steps, i=i, per_t=2)

            def ffn(s_in, t_in, s_out, t_out, diag_no):
                norm_transpose(x, KC, diag_no)
                pe.wait_ge(tr_lo, done["N"])
                with pe.Fori(0, FJ) as i:
                    for j in range(2):
                        product(s_in + j * DSTEPS, DSTEPS, t_in + j, xT_hi, xT_lo, t_parts(),
                                per=2 * DSTEPS, i=i, per_t=2)
                pe.wait_ge(h_lo, h_count[0] + FJ)
                h_count[0] += FJ
                wide_product(s_out, t_out, FSTEPS, hT_hi, hT_lo)

            h_count = [0]
            pe.wait_ge(o_lo, items_done[0])
            wide_product(OA, OA_T, DSTEPS, xT_hi, xT_lo)
            ffn(IN0, IN0_T, OUT0, OUT0_T, 5)

            norm_transpose(x, KC, 6)
            pe.wait_ge(tr_lo, done["N"])
            pe.wait_ge(tr_copied, done["C"])
            kb_blocks = [rot[:, 512 * t + P * g:512 * t + P * (g + 1)]
                         for g in range(2) for t in range(TT)]
            skv_tile = lambda j, **kw: product(SKV + j * DSTEPS, DSTEPS, SKV_T + j, xT_hi, xT_lo,
                                               n_parts(), **kw)
            c0 = groups_before(T_KB, "C")
            skv_tile(0)
            for j in range(1, BH):
                skv_tile(j)
                if j >= 3:
                    pe.wait_ge(tr_copied, c0 + j - 2)
                rope_transpose(4 + (j - 1) % 2, kb_blocks, 7 + j)
            qb_blocks = [[rot[:, 512 * t + P * g:512 * t + P * (g + 1)]
                          for g in (2 * q, 2 * q + 1) for t in range(TT)] for q in range(2)]
            c1 = groups_before(T_QB, "C")
            for j in range(3):
                product(BQ + j * DSTEPS, DSTEPS, BQ_T + j, xbT_hi, xbT_lo, n_parts())
                if j == 0:
                    pe.wait_ge(tr_copied, c0 + 4)
                    rope_transpose(5, kb_blocks, 13)
                else:
                    pe.wait_ge(tr_copied, c1 + 2 * (j - 1))
                    for q in range(2):
                        rope_transpose(6 + q, qb_blocks[q], 13 + j)
            product(BQ + 3 * DSTEPS, DSTEPS, BQ_T + 3, xbT_hi, xbT_lo, t_parts())
            pe.wait_ge(tr_copied, c1 + 4)
            for q in range(2):
                rope_transpose(6 + q, qb_blocks[q], 16)
            pair_count[0] = OB_T
            attend(ITEMS_B, kmT_b, vm_b, len(ITEMS_A))
            pe.wait_ge(o_lo, items_done[0])
            for h in range(BH):
                pe.wait_ge(on_scaled, h + 1)
                if h >= 4:
                    pe.wait_ge(tr_lo, done["N"] + h - 3)
                for c in range(2):
                    for t in range(TT):
                        mm = nc.tensor.transpose(ps[:, 4 + h % 4, 256 * c + P * t:256 * c + P * t + P],
                                                 o_nat[:, h, t, P * c:P * (c + 1)], ident[:, :])
                mm.then_inc(tr_ready, 1)
            done["N"] += BH
            pe.wait_ge(tr_lo, done["N"])
            wide_product(OB, OB_T, DSTEPS, xT_hi, xT_lo)
            ffn(IN1, IN1_T, OUT1, OUT1_T, 7)

        @blk.scalar
        def _(act):
            for t in range(TT):
                act.dma_start(x[:, t, :], x_in[t * P:(t + 1) * P, :]).then_inc(x_landed[t], 16)

            n_split = [0]
            count = {"C": 0, "N": 0, "tr": 0, "sq": 0, "std": 0}

            def split(s, per=0, i=None):
                width = 768 if UQ <= s < UKV and i is None else 1024
                act.wait_ge(w_landed[s % R], val(16 * (s // R + 1), 16 * per // R, i))
                if s >= R:
                    act.wait_ge(step_used, val(s - R + 1, per, i))
                nc.scalar.activation(w_hi[:, s % R, 0:width], w_raw[:, s % R, 0:width], ACT.Copy)\
                    .then_inc(hi_ready, 1)

            def splits_to(s):
                for k in range(n_split[0], min(s, STEPS)):
                    split(k)
                n_split[0] = min(s, STEPS)

            def root(n, width):
                count["std"] += 1
                act.wait_ge(ss_ready, count["std"])
                nc.scalar.activation(nrm[:, 2:4], nrm[:, 0:2], ACT.Sqrt, bias=eps[:, :],
                                     scale=1.0 / width).then_inc(std_ready, 1)

            squared = scratch[:, :, :, :].rearrange("p a b c -> p (a b c)").bitcast(BF16)
            unused = lambda k, n: squared[:, 1024 * k:1024 * k + n]

            def squares(pieces):
                for k, (src, col) in enumerate(pieces):
                    a = nc.scalar.activation(unused(2 * k, src.free_size()), src, ACT.Square,
                                             accum_out=col)
                a.then_inc(sq_ready, 1)
                count["sq"] += 1

            def split_transposes(chunks, targets):
                for g in range(chunks // 2):
                    count["tr"] += 1
                    act.wait_ge(tr_ready, count["tr"])
                    for g0, hi in targets:
                        for c in range(2):
                            ch = 2 * g + c
                            a = nc.scalar.activation(hi[:, ch, :], ps[:, 4 + g % 4, 256 * c:256 * c + S],
                                                     ACT.Copy, scale=gcol[:, g0 + ch:g0 + ch + 1])
                    a.then_inc(tr_hi, 1)

            def copy_transposed(dst, bank):
                count["tr"] += 1
                act.wait_ge(tr_ready, count["tr"])
                nc.scalar.activation(dst, ps[:, bank, 0:dst.free_size()], ACT.Copy)\
                    .then_inc(tr_copied, 1)

            act.wait_ge(consts_ready, 4)
            copy_transposed(gcol[:, 0:N_GAIN], 4)
            for layer in range(2):
                copy_transposed(conv[:, layer].rearrange("p j c -> p (j c)"), 5 + layer)
            for t in range(2):
                act.wait_ge(mem_landed[t], 16)
            squares([(mem[:, t, :], ssp[:, t, 0:1]) for t in range(2)])
            root(1, D)
            split_transposes(KC, [(GAIN_ROWS["a_mem"], mTa_hi), (GAIN_ROWS["b_mem"], mTb_hi)])

            def kv_epilogue(t, kT, heads, s_end):
                act.wait_ge(step_used, s_end)
                nc.scalar.activation(kT[:, heads, :].rearrange("p h s -> p (h s)"),
                                     ps[:, 2 * (t % 2), :], ACT.Copy).then_inc(pair_act, 1)

            splits_to(MEMA + DSTEPS + AHEAD)
            kv_epilogue(MEMA_T, kmT_a, slice(0, 2), MEMA + DSTEPS)
            act.wait_ge(range_ready, 1)
            nc.scalar.activation(cosine[:, :, :], rope_k[:, 0], ACT.Sin)
            nc.scalar.activation(sine[:, :, :], rope_k[:, 1], ACT.Sin).then_inc(trig_ready, 1)
            act.wait_ge(lam_prod, 1)
            nc.scalar.activation(neglam[:, 2:4], neglam[:, 0:2], ACT.Exp).then_inc(lam_exp, 1)
            for t in range(TT):
                act.wait_ge(x_landed[t], 16)
            squares([(x[:, t, :], ssp[:, t, 0:1]) for t in range(TT)])
            root(1, D)
            splits_to(MEMB + AHEAD)
            kv_epilogue(MEMA_T + 1, kmT_a, slice(2, 4), MEMB)
            split_transposes(KC, [(GAIN_ROWS["a_pre"], xT_hi)])
            splits_to(MEMB + DSTEPS + AHEAD)
            kv_epilogue(MEMB_T, kmT_b, slice(0, 2), MEMB + DSTEPS)
            splits_to(QLAT + AHEAD)
            kv_epilogue(MEMB_T + 1, kmT_b, slice(2, 4), QLAT)

            def latent_epilogue(k, t, s_end):
                act.wait_ge(step_used, s_end)
                pr = 2 * (t % 2)
                nc.scalar.activation(lat[:, k, 0, :], ps[:, pr, :], ACT.Copy).then_inc(pair_act, 1)
                act.wait_ge(pair_act, t + 1)
                act.wait_ge(pair_dve, t + 1)
                squares([(lat[:, k, u, :], ssp[:, u, 0:1]) for u in range(TT)])
                root(1, LORA)

            def raw_epilogue(t, width, s_end):
                act.wait_ge(step_used, s_end)
                pr = 2 * (t % 2)
                nc.scalar.activation(rawv[:, :, 0:width], ps[:, pr:pr + 2, 0:width], ACT.Copy)\
                    .then_inc(pair_act, 1)

            rawv = scratch[:, 0].rearrange("p a b -> p (a b)").rearrange("p (t n) -> p t n", t=TT)
            raw_a = scratch[:, 0].rearrange("p a b -> p (a b)")[:, 0:256]\
                .rearrange("p (t n) -> p t n", t=TT)

            splits_to(KVLAT + AHEAD)
            latent_epilogue(0, QLAT_T, KVLAT)
            splits_to(KPE + AHEAD)
            latent_epilogue(1, KVLAT_T, KPE)
            splits_to(QMEM + AHEAD)
            act.wait_ge(step_used, QMEM)
            pr = 2 * (KPE_T % 2)
            nc.scalar.activation(raw_a[:, :, 0:RD], ps[:, pr:pr + 2, 0:RD], ACT.Copy)\
                .then_inc(pair_act, 1)
            splits_to(UQ + AHEAD)
            act.wait_ge(step_used, UQ)
            nc.scalar.activation(qmT_a[:, 0:2, :].rearrange("p h s -> p (h s)"),
                                 ps[:, 2 * (QMEM_T % 2), :], ACT.Copy).then_inc(pair_act, 1)
            split_transposes(4, [(GAIN_ROWS["q_norm"], latq_hi)])
            split_transposes(4, [(GAIN_ROWS["kv_norm"], latk_hi)])
            copy_transposed(kpT[:, :], 4)
            for j in range(6):
                splits_to(UQ + (j + 1) * LSTEPS + AHEAD)
                if j:
                    copy_transposed(qpT[:, j - 1, :], 4 + (j - 1) % 2)
                act.wait_ge(step_used, UQ + (j + 1) * LSTEPS)
                pr = 2 * ((UQ_T + j) % 2)
                nc.scalar.activation(raw_a, ps[:, pr + 1, 0:256].rearrange("p (t n) -> p t n", t=TT),
                                     ACT.Copy)
                nc.scalar.activation(qnT[:, 2 * j:2 * j + 2, :].rearrange("p h s -> p (h s)"),
                                     ps[:, pr, :], ACT.Copy).then_inc(pair_act, 1)
            for j in range(6):
                splits_to(UKV + (j + 1) * LSTEPS + AHEAD)
                if j == 0:
                    copy_transposed(qpT[:, 5, :], 5)
                kv_epilogue(UKV_T + j, kT_a, slice(2 * j, 2 * j + 2), UKV + (j + 1) * LSTEPS)

            def attend(items, first_item, scale):
                t0 = first_item
                is_b = first_item > 0

                def exps(t):
                    kind, h = items[t]
                    act.wait_ge(max_ready, t0 + t + 1)
                    if t >= 2:
                        act.wait_ge(pT_ready, t0 + t - 1)
                    sc = scale if kind != "mem" else SCALE_B
                    for j in range(2 if kind == "diff" else 1):
                        b = 2 * (t % 2) + j if is_b else t % 4
                        cuts = ((0, 256), (256, 512)) if kind == "mem" else ((0, P), (P, 3 * P))
                        for q, (a, z) in enumerate(cuts):
                            e = nc.scalar.activation(
                                probs[:, t % 2, j, a:z], ps[:, b, a:z], ACT.Exp, scale=sc,
                                bias=stat[:, t % 4, 2 * j + q:2 * j + q + 1],
                                accum_out=sums[:, t % 4, 2 * j + q:2 * j + q + 1])
                    e.then_inc(e_ready, 1)

                def copy_pT(t):
                    kind, h = items[t]
                    act.wait_ge(pT_ready, t0 + t + 1)
                    if t >= 2:
                        act.wait_ge(o_ready, t0 + t - 1)
                    n = 512 if kind == "mem" else 3 * P
                    nc.scalar.activation(pT[:, t % 2, 0:n], ps[:, 4 + t % 2, 0:n], ACT.Copy)\
                        .then_inc(pT_copied, 1)

                def output(t):
                    kind, h = items[t]
                    act.wait_ge(o_ready, t0 + t + 1)
                    src = ps[:, 6 + t % 2, :]
                    if kind == "diff":
                        for q in range(TT):
                            a = nc.scalar.activation(
                                unused(2 * (t % 2) + q, VD), src[:, VD * q:VD * (q + 1)], ACT.Square,
                                accum_out=osum[:, 0, 2 * h + q:2 * h + q + 1])
                        a.then_inc(o_hi, 1)
                    else:
                        ch = h if kind == "mla" else 12 + h
                        nc.scalar.activation(xT_hi[:, ch, :], src[:, 0:S], ACT.Copy).then_inc(o_hi, 1)

                for t in range(len(items) + 2):
                    if t < len(items):
                        exps(t)
                    if 1 <= t <= len(items):
                        copy_pT(t - 1)
                    if t >= 2:
                        output(t - 2)

            sums = stat[:, :, 4:8]
            attend(ITEMS_A, 0, SCALE_A)

            def wide_epilogue(s0, t0, steps):
                assert n_split[0] == s0 + AHEAD

                def turn(i):
                    for j in range(2):
                        for k in range(steps):
                            if s0 + (2 * i + j) * steps + k + AHEAD < STEPS if s0 == OUT1 else True:
                                split(s0 + j * steps + k + AHEAD, 2 * steps, i)
                        act.wait_ge(step_used, val(s0 + (j + 1) * steps, 2 * steps, i))
                        for u in range(TT):
                            a = nc.scalar.activation(
                                unused(2 * j + u, 512), ps[:, 2 * ((t0 + j) % 2) + u, :], ACT.Square,
                                accum_out=ssp[:, u, bass.ds(i * 2 + j, 1)])
                        a.then_inc(pair_act, 1)

                if s0 == OUT1:
                    for i in range(2):
                        turn(i)
                else:
                    with act.Fori(0, 2) as i:
                        turn(i)
                n_split[0] = s0 + 4 * steps + AHEAD

            pieces = [0]

            def residual_norm(last=False):
                root(4, D)
                if last:
                    return
                cols = []
                for q in range(4):
                    pieces[0] += 1
                    act.wait_ge(x_piece, pieces[0])
                    t, half = q // 2, q % 2
                    a = nc.scalar.activation(unused(q, 1024), x[:, t, half * 1024:(half + 1) * 1024], ACT.Square,
                                             accum_out=ssp[:, t, half:half + 1])
                a.then_inc(sq_ready, 1)
                root(2, D)

            def ffn_epilogues(layer, s_in, t_in, g_count):
                assert n_split[0] == s_in + AHEAD
                with act.Fori(0, FJ) as i:
                    for j in range(2):
                        for k in range(DSTEPS):
                            split(s_in + j * DSTEPS + k + AHEAD, 2 * DSTEPS, i)
                        act.wait_ge(step_used, val(s_in + (j + 1) * DSTEPS, 2 * DSTEPS, i))
                        for m4 in range(4):
                            ch = i * 4 + (m4 + j * FC)
                            a = nc.scalar.activation(
                                scratch[:, j, m4, :],
                                ps[:, 2 * ((t_in + j) % 2) + m4 // 2, 256 * (m4 % 2):256 * (m4 % 2) + S],
                                ACT.Identity, scale=conv[:, layer, 2, bass.ds(ch, 1)],
                                bias=conv[:, layer, 3, bass.ds(ch, 1)])
                        a.then_inc(pair_act, 1)
                        if j == 0:
                            act.wait_ge(pair_dve, val(t_in + 1, 2, i))
                            nc.scalar.activation(scratch[:, 0], scratch[:, 0],
                                                 ACT.Gelu_apprx_tanh).then_inc(gate_ready, 1)
                        else:
                            act.wait_ge(h_ready, val(g_count + 1, 1, i))
                            nc.scalar.activation(hT_hi[:, bass.ds(i * 4, 4), :], scratch[:, 1],
                                                 ACT.Copy).then_inc(h_hi, 1)
                n_split[0] = s_in + 2 * FJ * DSTEPS + AHEAD

            wide_epilogue(OA, OA_T, DSTEPS)
            residual_norm()
            split_transposes(KC, [(GAIN_ROWS["ffn_pre"], xT_hi)])
            ffn_epilogues(0, IN0, IN0_T, 0)
            wide_epilogue(OUT0, OUT0_T, FSTEPS)
            residual_norm()
            split_transposes(KC, [(GAIN_ROWS["shared"], xT_hi), (GAIN_ROWS["b_pre"], xbT_hi)])
            for j in range(BH):
                splits_to(SKV + (j + 1) * DSTEPS + AHEAD)
                if j:
                    copy_transposed(kT_b[:, 2 * j - 2:2 * j, :].rearrange("p h s -> p (h s)"),
                                    4 + (j - 1) % 2)
                raw_epilogue(SKV_T + j, 256, SKV + (j + 1) * DSTEPS)
            for j in range(3):
                splits_to(BQ + (j + 1) * DSTEPS + AHEAD)
                if j == 0:
                    copy_transposed(kT_b[:, 10:12, :].rearrange("p h s -> p (h s)"), 5)
                else:
                    for q in range(2):
                        h0 = 4 * (j - 1) + 2 * q
                        copy_transposed(qT_b[:, h0:h0 + 2, :].rearrange("p h s -> p (h s)"), 6 + q)
                raw_epilogue(BQ_T + j, 512, BQ + (j + 1) * DSTEPS)
            splits_to(OB + AHEAD)
            act.wait_ge(step_used, OB)
            nc.scalar.activation(qmT_b[:, 0:2, :].rearrange("p h s -> p (h s)"),
                                 ps[:, 2 * ((BQ_T + 3) % 2), :], ACT.Copy).then_inc(pair_act, 1)
            for q in range(2):
                copy_transposed(qT_b[:, 8 + 2 * q:10 + 2 * q, :].rearrange("p h s -> p (h s)"), 6 + q)
            attend(ITEMS_B, len(ITEMS_A), SCALE_B)
            act.wait_ge(o_hi, len(ITEMS_A) + BH)
            nc.scalar.activation(osum[:, 1, :], osum[:, 0, :], ACT.Sqrt, bias=eps[:, :],
                                 scale=1.0 / VD).then_inc(ostd_ready, 1)
            for h in range(BH):
                count["tr"] += 1
                act.wait_ge(tr_ready, count["tr"])
                for c in range(2):
                    g0 = GAIN_ROWS["subln"] + c
                    a = nc.scalar.activation(xT_hi[:, 2 * h + c, :], ps[:, 4 + h % 4, 256 * c:256 * c + S],
                                             ACT.Copy, scale=gcol[:, g0:g0 + 1])
                a.then_inc(tr_hi, 1)
            wide_epilogue(OB, OB_T, DSTEPS)
            residual_norm()
            split_transposes(KC, [(GAIN_ROWS["ffn_pre"] + KC, xT_hi)])
            ffn_epilogues(1, IN1, IN1_T, FJ)
            wide_epilogue(OUT1, OUT1_T, FSTEPS)
            residual_norm(last=True)

        @blk.vector
        def _(dve):
            linked = [0]

            def link(ins, base=0):
                linked[0] += 1
                ins.then_inc(dve_link, 1)
                dve.wait_ge(dve_link, base + linked[0])

            n_split = [0]
            count = {"N": 0, "sq": 0, "std": 0, "gain": 0, "rope": 0}

            def split(s, per=0, i=None):
                width = 768 if UQ <= s < UKV and i is None else 1024
                dve.wait_ge(hi_ready, val(s + 1, per, i))
                nc.vector.tensor_tensor(w_lo[:, s % R, 0:width], w_raw[:, s % R, 0:width],
                                        w_hi[:, s % R, 0:width].bitcast(F32), ALU.subtract)\
                    .then_inc(lo_ready, 1)

            def splits_to(s):
                for k in range(n_split[0], min(s, STEPS)):
                    split(k)
                n_split[0] = min(s, STEPS)

            def sums(parts):
                nc.vector.reduce_sum(nrm[:, 0:2], ssp[:, :, 0:parts], axis=AX).then_inc(ss_ready, 1)

            def inverse_std():
                count["std"] += 1
                dve.wait_ge(std_ready, count["std"])
                link(nc.vector.reciprocal(nrm[:, 4:6], nrm[:, 2:4]))

            def diagonal(dst):
                for t in range(TT):
                    d = nc.vector.tensor_scalar(dst[:, t, :], ident[:, :], nrm[:, 4 + t:5 + t], None,
                                                ALU.mult)
                d.then_inc(diag_ready, 1)

            def norm(parts, dst=diag):
                count["sq"] += 1
                dve.wait_ge(sq_ready, count["sq"])
                sums(parts)
                inverse_std()
                diagonal(dst)

            def split_transposes(chunks, targets):
                for g in range(chunks // 2):
                    count["N"] += 1
                    dve.wait_ge(tr_hi, count["N"])
                    for g0, hi, lo in targets:
                        for c in range(2):
                            ch = 2 * g + c
                            d = nc.vector.scalar_tensor_tensor(
                                out=lo[:, ch, :], in0=ps[:, 4 + g % 4, 256 * c:256 * c + S],
                                scalar=gcol[:, g0 + ch:g0 + ch + 1], in1=hi[:, ch, :].bitcast(F32),
                                op0=ALU.mult, op1=ALU.subtract)
                    d.then_inc(tr_lo, 1)

            dve.wait_ge(small_landed, 16 * N_SMALL)
            link(nc.vector.tensor_copy(pos_f[:, :], pos_i[:, :]))
            for t in range(TT):
                d = nc.vector.tensor_scalar(angle[:, t, :], freq[:, :], pos_f[:, t:t + 1], None,
                                            ALU.mult)
            link(d)
            for k, quarter in ((0, 0.25), (1, 0.0)):
                d = nc.vector.tensor_scalar(turns[:, k], angle[:, :, :], 1.0 / (2 * math.pi), quarter,
                                            ALU.mult, ALU.add)
            link(d)
            link(nc.vector.tensor_scalar(turns[:, :], turns[:, :], ROUND, ROUND, ALU.add,
                                         ALU.subtract))
            for k in range(2):
                d = nc.vector.scalar_tensor_tensor(
                    out=rope_k[:, k], in0=turns[:, k], scalar=-TWO_PI[0], in1=angle[:, :, :],
                    op0=ALU.mult, op1=ALU.add)
            link(d)
            for part in TWO_PI[1:]:
                link(nc.vector.scalar_tensor_tensor(
                    out=rope_k[:, :], in0=turns[:, :], scalar=-part, in1=rope_k[:, :],
                    op0=ALU.mult, op1=ALU.add))
            link(nc.vector.tensor_scalar_add(rope_k[:, 0], rope_k[:, 0], math.pi / 2))
            nc.vector.tensor_scalar(rope_k[:, :], rope_k[:, :], SIN_MAX, -SIN_MAX, ALU.min, ALU.max)\
                .then_inc(range_ready, 1)
            lr = lam_rows[:, :, :].rearrange("p (a b) n -> p a b n", a=2)
            link(nc.vector.tensor_tensor(lr[:, :, 0, :], lr[:, :, 0, :], lr[:, :, 1, :], ALU.mult))
            nc.vector.reduce_sum(neglam[:, 0:2], lr[:, :, 0, :], axis=AX).then_inc(lam_prod, 1)
            dve.wait_ge(tr_copied, 3)
            g0 = GAIN_ROWS["subln"]
            link(nc.vector.tensor_scalar(gcol[:, g0:g0 + 2], gcol[:, g0:g0 + 2], 1.0 - LAMBDA_INIT,
                                         None, ALU.mult))
            norm(1)
            split_transposes(KC, [(GAIN_ROWS["a_mem"], mTa_hi, mTa_lo),
                                  (GAIN_ROWS["b_mem"], mTb_hi, mTb_lo)])

            def v_epilogue(t, v, heads, s_end):
                dve.wait_ge(step_used, s_end)
                nc.vector.tensor_copy(v[:, :, heads, :].rearrange("p t h n -> p t (h n)"),
                                      ps[:, 2 * (t % 2) + 1, :].rearrange("p (t n) -> p t n", t=2))\
                    .then_inc(pair_dve, 1)

            splits_to(MEMA + DSTEPS + AHEAD)
            v_epilogue(MEMA_T, vm_a, slice(0, 2), MEMA + DSTEPS)
            dve.wait_ge(lam_exp, 1)
            link(nc.vector.tensor_tensor(neglam[:, 0:1], neglam[:, 3:4], neglam[:, 2:3], ALU.subtract))
            link(nc.vector.tensor_scalar_add(neglam[:, 0:1], neglam[:, 0:1], -LAMBDA_INIT))
            norm(1)
            splits_to(MEMB + AHEAD)
            v_epilogue(MEMA_T + 1, vm_a, slice(2, 4), MEMB)
            split_transposes(KC, [(GAIN_ROWS["a_pre"], xT_hi, xT_lo)])
            splits_to(MEMB + DSTEPS + AHEAD)
            v_epilogue(MEMB_T, vm_b, slice(0, 2), MEMB + DSTEPS)
            splits_to(QLAT + AHEAD)
            v_epilogue(MEMB_T + 1, vm_b, slice(2, 4), QLAT)

            raw = scratch[:, 0].rearrange("p a b -> p (a b)")
            tmp = scratch[:, 1].rearrange("p a b -> p (a b)")

            def rotate(tile_no, row, width, c0, half, twice=False):
                dve.wait_ge(pair_act, tile_no + 1)
                shape = dict(t=TT)
                v4 = lambda a: a[:, 0:TT * row].rearrange("p (t n) -> p t n", t=TT)[:, :, 0:width]\
                    .rearrange("p t (g d) -> p t g d", d=2 * half)
                xr, tr = v4(raw), v4(tmp)
                g = width // (2 * half)
                wide = [P, TT, g, half]
                cos = cosine[:, :, c0:c0 + half].unsqueeze(2).to_broadcast(wide)
                sin = sine[:, :, c0:c0 + half].unsqueeze(2).to_broadcast(wide)
                a, b = (slice(0, half), slice(half, 2 * half))
                nc.vector.tensor_tensor(tr[:, :, :, a], xr[:, :, :, b], sin, ALU.mult)\
                    .then_inc(pair_dve, 1)
                nc.vector.tensor_tensor(tr[:, :, :, b], xr[:, :, :, a], sin, ALU.mult)
                nc.vector.tensor_tensor(xr[:, :, :, a], xr[:, :, :, a], cos, ALU.mult)
                link(nc.vector.tensor_tensor(xr[:, :, :, b], xr[:, :, :, b], cos, ALU.mult))
                nc.vector.tensor_tensor(xr[:, :, :, a], xr[:, :, :, a], tr[:, :, :, a], ALU.subtract)
                d = nc.vector.tensor_tensor(xr[:, :, :, b], xr[:, :, :, b], tr[:, :, :, b], ALU.add)
                if twice:
                    link(d)
                    rows = raw[:, 0:TT * row].rearrange("p (t n) -> p t n", t=TT)
                    d = nc.vector.tensor_copy(rows[:, :, width:2 * width], rows[:, :, 0:width])
                d.then_inc(rope_ready, 1)

            def latent_epilogue(k, t, s_end, dst):
                dve.wait_ge(step_used, s_end)
                nc.vector.tensor_copy(lat[:, k, 1, :], ps[:, 2 * (t % 2) + 1, :]).then_inc(pair_dve, 1)
                norm(1, dst)

            splits_to(KVLAT + AHEAD)
            latent_epilogue(0, QLAT_T, KVLAT, diag)
            splits_to(KPE + AHEAD)
            latent_epilogue(1, KVLAT_T, KPE, diag_kv)
            splits_to(QMEM + AHEAD)
            rotate(KPE_T, P, RD, 0, RD // 2, twice=True)
            splits_to(UQ + AHEAD)
            dve.wait_ge(step_used, UQ)
            nc.vector.tensor_copy(qmT_a[:, 2:4, :].rearrange("p h s -> p (h s)"),
                                  ps[:, 2 * (QMEM_T % 2) + 1, :]).then_inc(pair_dve, 1)
            split_transposes(4, [(GAIN_ROWS["q_norm"], latq_hi, latq_lo)])
            split_transposes(4, [(GAIN_ROWS["kv_norm"], latk_hi, latk_lo)])
            for j in range(6):
                splits_to(UQ + (j + 1) * LSTEPS + AHEAD)
                rotate(UQ_T + j, P, P, 0, RD // 2)
            for j in range(6):
                splits_to(UKV + (j + 1) * LSTEPS + AHEAD)
                v_epilogue(UKV_T + j, v_a, slice(2 * j, 2 * j + 2), UKV + (j + 1) * LSTEPS)

            def attend(items, first_item, scale):
                t0 = first_item
                is_b = first_item > 0

                def maxima(t):
                    kind, h = items[t]
                    dve.wait_ge(s_ready, t0 + t + 1)
                    m4 = stat[:, t % 4, :]
                    if kind == "mem":
                        b = 2 * (t % 2) if is_b else t % 4
                        n = 2
                        d = nc.vector.reduce_max(
                            m4[:, 0:2], ps[:, b, :].rearrange("p (q n) -> p q n", q=2), axis=AX)
                    else:
                        n = 4 if kind == "diff" else 2
                        for j in range(n // 2):
                            b = 2 * (t % 2) + j if is_b else t % 4
                            for q, (a, z) in enumerate(((0, P), (P, 3 * P))):
                                d = nc.vector.reduce_max(m4[:, 2 * j + q:2 * j + q + 1],
                                                         ps[:, b, a:z], axis=AX)
                    link(d)
                    sc = SCALE_B if kind == "mem" else scale
                    nc.vector.tensor_scalar(m4[:, 0:n], m4[:, 0:n], -sc, None, ALU.mult)\
                        .then_inc(max_ready, 1)

                def normalise(t):
                    kind, h = items[t]
                    dve.wait_ge(e_ready, t0 + t + 1)
                    m4 = stat[:, t % 4, :]
                    n = 4 if kind == "diff" else 2
                    link(nc.vector.reciprocal(m4[:, 4:4 + n], m4[:, 4:4 + n]))
                    p = probs[:, t % 2]
                    cuts = ((0, 256), (256, 512)) if kind == "mem" else ((0, P), (P, 3 * P))
                    if kind == "diff":
                        nc.vector.tensor_scalar(m4[:, 6:8], m4[:, 6:8], neglam[:, 0:1], None, ALU.mult)
                    for q, (a, z) in enumerate(cuts):
                        d = nc.vector.tensor_scalar(p[:, 0, a:z], p[:, 0, a:z], m4[:, 4 + q:5 + q],
                                                    None, ALU.mult)
                    if kind == "diff":
                        link(d)
                        for q, (a, z) in enumerate(cuts):
                            d = nc.vector.scalar_tensor_tensor(
                                out=p[:, 0, a:z], in0=p[:, 1, a:z], scalar=m4[:, 6 + q:7 + q],
                                in1=p[:, 0, a:z], op0=ALU.mult, op1=ALU.add)
                    d.then_inc(p_ready, 1)

                def output(t):
                    kind, h = items[t]
                    dve.wait_ge(o_hi, t0 + t + 1)
                    src = ps[:, 6 + t % 2, :]
                    if kind == "diff":
                        nc.vector.tensor_copy(o_nat[:, h].rearrange("p t n -> p (t n)"), src)\
                            .then_inc(o_lo, 1)
                    else:
                        ch = h if kind == "mla" else 12 + h
                        nc.vector.tensor_tensor(xT_lo[:, ch, :], src[:, 0:S],
                                                xT_hi[:, ch, :].bitcast(F32), ALU.subtract)\
                            .then_inc(o_lo, 1)

                for t in range(len(items) + 3):
                    if t < len(items):
                        maxima(t)
                    if 1 <= t <= len(items):
                        normalise(t - 1)
                    if t >= 3:
                        output(t - 3)

            attend(ITEMS_A, 0, SCALE_A)

            def wide_epilogue(s0, t0, steps, y, gain):
                assert n_split[0] == s0 + AHEAD
                count["gain"] += 1

                def turn(i):
                    for j in range(2):
                        for k in range(steps):
                            if s0 + (2 * i + j) * steps + k + AHEAD < STEPS if s0 == OUT1 else True:
                                split(s0 + j * steps + k + AHEAD, 2 * steps, i)
                        if j == 0:
                            dve.wait_ge(gain_landed, 16 * count["gain"])
                        dve.wait_ge(pair_act, val(t0 + j + 1, 2, i))
                        pr = 2 * ((t0 + j) % 2)
                        cols = bass.ds(i * 1024 + 512 * j, 512)
                        nc.vector.tensor_tensor(
                            y[:, :, cols], ps[:, pr:pr + 2, :],
                            gain[:, cols].unsqueeze(1).to_broadcast([P, TT, 512]), ALU.mult)\
                            .then_inc(pair_dve, 1)

                if s0 == OUT1:
                    for i in range(2):
                        turn(i)
                else:
                    with dve.Fori(0, 2) as i:
                        turn(i)
                n_split[0] = s0 + 4 * steps + AHEAD

            def residual(y, t_end):
                dve.wait_ge(pair_dve, t_end)
                sums(4)
                inverse_std()
                for q in range(4):
                    t, half = q // 2, q % 2
                    cols = slice(half * 1024, (half + 1) * 1024)
                    nc.vector.scalar_tensor_tensor(
                        out=x[:, t, cols], in0=y[:, t, cols], scalar=nrm[:, 4 + t:5 + t],
                        in1=x[:, t, cols], op0=ALU.mult, op1=ALU.add).then_inc(x_piece, 1)

            def ffn_epilogues(layer, s_in, t_in, g_count):
                assert n_split[0] == s_in + AHEAD
                before = linked[0]
                with dve.Fori(0, FJ) as i:
                    for j in range(2):
                        for k in range(DSTEPS):
                            split(s_in + j * DSTEPS + k + AHEAD, 2 * DSTEPS, i)
                        dve.wait_ge(pair_act, val(t_in + j + 1, 2, i))
                        for shift in (1, 2):
                            for m4 in range(4):
                                ch = i * 4 + (m4 + j * FC)
                                u = ps[:, 2 * ((t_in + j) % 2) + m4 // 2,
                                       256 * (m4 % 2):256 * (m4 % 2) + S - shift]
                                c = scratch[:, j, m4, shift:S]
                                d = nc.vector.scalar_tensor_tensor(
                                    out=c, in0=u, scalar=conv[:, layer, 2 - shift, bass.ds(ch, 1)],
                                    in1=c, op0=ALU.mult, op1=ALU.add)
                            if shift == 1:
                                link(d, i * 2)
                        d.then_inc(pair_dve, 1)
                    dve.wait_ge(pair_dve, val(t_in + 2, 2, i))
                    dve.wait_ge(gate_ready, val(g_count + 1, 1, i))
                    nc.vector.tensor_tensor(scratch[:, 1], scratch[:, 0], scratch[:, 1], ALU.mult)\
                        .then_inc(h_ready, 1)
                    dve.wait_ge(h_hi, val(g_count + 1, 1, i))
                    hs = bass.ds(i * 4, 4)
                    nc.vector.tensor_tensor(hT_lo[:, hs, :], scratch[:, 1], hT_hi[:, hs, :].bitcast(F32),
                                            ALU.subtract).then_inc(h_lo, 1)
                assert linked[0] - before == 2
                linked[0] = before + 2 * FJ
                n_split[0] = s_in + 2 * FJ * DSTEPS + AHEAD

            wide_epilogue(OA, OA_T, DSTEPS, y_o, gain_o)
            residual(y_o, OA_T + 4)
            norm(2)
            split_transposes(KC, [(GAIN_ROWS["ffn_pre"], xT_hi, xT_lo)])
            ffn_epilogues(0, IN0, IN0_T, 0)
            wide_epilogue(OUT0, OUT0_T, FSTEPS, y_f, gain_f)
            residual(y_f, OUT0_T + 4)
            norm(2)
            split_transposes(KC, [(GAIN_ROWS["shared"], xT_hi, xT_lo),
                                  (GAIN_ROWS["b_pre"], xbT_hi, xbT_lo)])
            for j in range(BH):
                splits_to(SKV + (j + 1) * DSTEPS + AHEAD)
                dve.wait_ge(pair_act, SKV_T + j + 1)
                pr = 2 * ((SKV_T + j) % 2)
                nc.vector.tensor_copy(v_b[:, :, j, :], ps[:, pr:pr + 2, 256:512])
                rotate(SKV_T + j, 512, 256, 32, HD // 2)
            for j in range(3):
                splits_to(BQ + (j + 1) * DSTEPS + AHEAD)
                rotate(BQ_T + j, 512, 512, 32, HD // 2)
            splits_to(OB + AHEAD)
            dve.wait_ge(step_used, OB)
            nc.vector.tensor_copy(qmT_b[:, 2:4, :].rearrange("p h s -> p (h s)"),
                                  ps[:, 2 * ((BQ_T + 3) % 2) + 1, :]).then_inc(pair_dve, 1)
            attend(ITEMS_B, len(ITEMS_A), SCALE_B)
            dve.wait_ge(ostd_ready, 1)
            link(nc.vector.reciprocal(osum[:, 2, :], osum[:, 1, :]))
            for h in range(BH):
                nc.vector.tensor_tensor(
                    o_nat[:, h], o_nat[:, h],
                    osum[:, 2, 2 * h:2 * h + 2].unsqueeze(2).to_broadcast([P, TT, VD]), ALU.mult)\
                    .then_inc(on_scaled, 1)
            for h in range(BH):
                count["N"] += 1
                dve.wait_ge(tr_hi, count["N"])
                for c in range(2):
                    g0 = GAIN_ROWS["subln"] + c
                    d = nc.vector.scalar_tensor_tensor(
                        out=xT_lo[:, 2 * h + c, :], in0=ps[:, 4 + h % 4, 256 * c:256 * c + S],
                        scalar=gcol[:, g0:g0 + 1], in1=xT_hi[:, 2 * h + c, :].bitcast(F32),
                        op0=ALU.mult, op1=ALU.subtract)
                d.then_inc(tr_lo, 1)
            wide_epilogue(OB, OB_T, DSTEPS, y_o, gain_o)
            residual(y_o, OB_T + 4)
            norm(2)
            split_transposes(KC, [(GAIN_ROWS["ffn_pre"] + KC, xT_hi, xT_lo)])
            ffn_epilogues(1, IN1, IN1_T, FJ)
            wide_epilogue(OUT1, OUT1_T, FSTEPS, y_f, gain_f)
            residual(y_f, OUT1_T + 4)


_INS = ["x", "mem", "positions", "a_attn_norm_pre", "a_w_in", "a_q_norm", "a_w_uq", "a_kv_norm",
        "a_w_ukv", "a_mem_norm", "a_w_mem_kv", "a_w_o", "a_attn_norm_post", "shared_kv_norm",
        "shared_w_kv", "b_attn_norm_pre", "b_w_in", "b_lambda_q1", "b_lambda_k1", "b_lambda_q2",
        "b_lambda_k2", "b_subln", "b_mem_norm", "b_w_mem_kv", "b_w_o", "b_attn_norm_post",
        "ffn_norm_pre", "ffn_w_in", "ffn_conv_w", "ffn_conv_b", "ffn_w_out", "ffn_norm_post"]


def build(nc, a, inv_freq, out):
    w = {n: a[n][0] for n in ("a_w_in", "a_w_uq", "a_w_ukv", "a_w_mem_kv", "a_w_o", "b_w_in",
                              "b_w_mem_kv", "b_w_o")}
    w["shared_w_kv"] = a["shared_w_kv"]
    for layer in range(2):
        w[f"ffn_w_in{layer}"] = a["ffn_w_in"][layer]
        w[f"ffn_w_out{layer}"] = a["ffn_w_out"][layer]
    rows = lambda v: v.rearrange("(c p) -> c p", p=P)
    vec = {
        "rows": [("a_pre", rows(a["a_attn_norm_pre"][0])), ("a_mem", rows(a["a_mem_norm"][0])),
                 ("b_mem", rows(a["b_mem_norm"][0])), ("b_pre", rows(a["b_attn_norm_pre"][0])),
                 ("shared", rows(a["shared_kv_norm"])),
                 ("ffn_pre", a["ffn_norm_pre"].rearrange("l (c p) -> (l c) p", p=P)),
                 ("q_norm", rows(a["a_q_norm"][0])), ("kv_norm", rows(a["a_kv_norm"][0])),
                 ("subln", rows(a["b_subln"][0]))],
        "conv_w": [a["ffn_conv_w"][layer] for layer in range(2)],
        "conv_b": [a["ffn_conv_b"][layer] for layer in range(2)],
        "lambda": [a[n][0] for n in ("b_lambda_q1", "b_lambda_k1", "b_lambda_q2", "b_lambda_k2")],
        "a_post": a["a_attn_norm_post"][0], "b_post": a["b_attn_norm_post"][0],
        "ffn_post0": a["ffn_norm_post"][0], "ffn_post1": a["ffn_norm_post"][1],
    }
    program(nc, a["x"][0], a["mem"][0], a["positions"][0], inv_freq, w, vec, out[0])


def kernel(**inputs):
    import concourse.bacc as bacc
    from concourse.bass_utils import run_bass_kernel_spmd

    nc = bacc.Bacc("TRN2", target_bir_lowering=False, num_devices=1)
    arrays, aps = {}, {}
    for name in _INS:
        v = np.ascontiguousarray(inputs[name])
        arrays[f"in_{name}"] = v
        aps[name] = nc.dram_tensor(f"in_{name}", v.shape, mybir.dt.from_np(v.dtype),
                                   kind="ExternalInput").ap()
    freq = np.concatenate([np.exp(np.float32(-math.log(THETA)) * np.arange(n, dtype=np.float32)
                                  * np.float32(1.0 / n)).astype(np.float32)
                           for n in (RD // 2, HD // 2)])
    arrays["in_freq"] = freq
    f = nc.dram_tensor("in_freq", freq.shape, F32, kind="ExternalInput").ap()
    out = nc.dram_tensor("out_0", (1, S, D), F32, kind="ExternalOutput").ap()
    build(nc, aps, f, out)
    r = run_bass_kernel_spmd(nc, [arrays], core_ids=[0])
    return r.results[0]["out_0"]
```

```python
import math
from contextlib import ExitStack

import numpy as np

import concourse.bass as bass
from concourse import mybir

P = 128
F32 = mybir.dt.float32
F32R = mybir.dt.float32r
BF16 = mybir.dt.bfloat16
I32 = mybir.dt.int32
ALU = mybir.AluOpType
ACT = mybir.ActivationFunctionType
AX = mybir.AxisListType.X

S = 256
M = 256
TT = S // P
D = 2048
KC = D // P
AH, NOPE, RD = 12, 128, 64
LORA = 512
BH, HD, VD = 6, 128, 256
MH = 4
F = 5632
FC = F // P
EPS = 1e-6
LAMBDA_INIT = 0.8 - 0.6 * math.exp(-0.3)
THETA = 10000.0
SCALE_A = float(NOPE + RD) ** -0.5
SCALE_B = float(HD) ** -0.5
NEG = -3.0e38

R = 4
AHEAD = 3
CUT = 7
DSTEPS = KC // 2
LSTEPS = LORA // P // 2
FSTEPS = FC // 2
FJ = F // 512

MEMA, MEMA_T = 0, 0
MEMB, MEMB_T = MEMA + 2 * DSTEPS, MEMA_T + 2
QLAT, QLAT_T = MEMB + 2 * DSTEPS, MEMB_T + 2
KVLAT, KVLAT_T = QLAT + DSTEPS, QLAT_T + 1
KVW = LORA + RD
QMEM, QMEM_T = KVLAT + KC, KVLAT_T + 1
UQ, UQ_T = QMEM + DSTEPS, QMEM_T + 1
UKV, UKV_T = UQ + 6 * LSTEPS, UQ_T + 6
OA, OA_T = UKV + 6 * LSTEPS, UKV_T + 6
IN0, IN0_T = OA + 4 * DSTEPS, OA_T + 4
OUT0, OUT0_T = IN0 + 2 * FJ * DSTEPS, IN0_T + 2 * FJ
SKV, SKV_T = OUT0 + 4 * FSTEPS, OUT0_T + 4
BQ, BQ_T = SKV + BH * DSTEPS, SKV_T + BH
OB, OB_T = BQ + 4 * DSTEPS, BQ_T + 4
IN1, IN1_T = OB + 4 * DSTEPS, OB_T + 4
OUT1, OUT1_T = IN1 + 2 * FJ * DSTEPS, IN1_T + 2 * FJ
STEPS, TILES = OUT1 + 4 * FSTEPS, OUT1_T + 4

GROUPS = [("C", 3), ("N", 8), ("N", 8), ("N", 2), ("N", 2), ("C", 1), ("C", 6), ("N", 8),
          ("N", 8), ("C", 6), ("C", 6), ("N", 6), ("N", 8)]
(T_SETUP, T_MEM, T_X, T_QLAT, T_KVLAT, T_KPE, T_QPE, T_FFN0, T_B, T_KB, T_QB, T_SUB,
 T_FFN1) = range(len(GROUPS))

GAIN_ROWS = {}
_row = 0
for _name, _n in (("a_pre", KC), ("a_mem", KC), ("b_mem", KC), ("b_pre", KC), ("shared", KC),
                  ("ffn_pre", 2 * KC), ("q_norm", 4), ("kv_norm", 4), ("subln", 2)):
    GAIN_ROWS[_name] = _row
    _row += _n
N_GAIN = _row


MEM_CHUNK = KC - MH
N_SMALL, N_ROPE = 2, 2 + TT
ROUND = 1.5 * 2.0 ** 23
TWO_PI = (6.28125, float(np.float32(np.round((2 * math.pi - 6.28125) * 2 ** 20) / 2 ** 20)), None)
TWO_PI = TWO_PI[:2] + (2 * math.pi - TWO_PI[0] - TWO_PI[1],)
SIN_MAX = 3.1415925


SUB_BANKS = (4, 5, 2 - 2 * (OB_T % 2), 3 - 2 * (OB_T % 2), 6, 7)


def groups_before(phase, kind=None):
    return sum(n for k, n in GROUPS[:phase] if kind in (None, k))


def val(const, per, i):
    return const if i is None else i * per + const


def program(nc, x_in, mem_in, positions, inv_freq, w, vec, out):
    with ExitStack() as ctx:
        sem = lambda name: ctx.enter_context(nc.semaphore(name))
        base = 16512

        def at(name, shape, dt, offset):
            return nc.alloc_sbuf_tensor_at(name, shape, dt, offset=base + offset)

        KB = 1024
        X0, XT0, RING0, KVB0, H0, M0 = 0, 16 * KB, 48 * KB, 96 * KB, 104 * KB, 192 * KB
        x = at("x", [P, TT, D], F32, X0)
        xT_hi = at("xT_hi", [P, KC, S], F32R, XT0)
        xT_lo = at("xT_lo", [P, KC, S], F32R, XT0 + 16 * KB)
        w_raw = at("w_raw", [P, R, 1024], F32, RING0)
        w_hi = at("w_hi", [P, R, 1024], F32R, RING0 + 16 * KB)
        w_lo = at("w_lo", [P, R, 1024], F32R, RING0 + 32 * KB)
        y_f = at("y_f", [P, TT, D], F32, XT0)
        gain_f = at("gain_f", [P, D], F32, XT0 + 16 * KB)
        kmT_b = at("kmT_b", [P, MH, M], F32, KVB0)
        vm_b = at("vm_b", [P, 2, MH, P], F32, KVB0 + 4 * KB)
        mTa_hi = at("mTa_hi", [P, KC, M], F32R, H0)
        mTa_lo = at("mTa_lo", [P, KC, M], F32R, H0 + 16 * KB)
        mTb_hi = at("mTb_hi", [P, KC, M], F32R, H0 + 32 * KB)
        mTb_lo = at("mTb_lo", [P, KC, M], F32R, H0 + 48 * KB)
        mem = at("mem", [P, 2, D], F32, H0 + 64 * KB)
        gain_rows = at("gain_rows", [P, P], F32, H0 + 80 * KB)
        conv_rows = at("conv_rows", [2 * FC, 2, 4, P], F32, H0 + 81 * KB)
        lam_rows = at("lam_rows", [P, 4, P], F32, H0 + 85 * KB)
        freq = at("freq", [P, 96], F32, H0 + 87 * KB)
        angle = at("angle", [P, TT, 96], F32, KVB0)
        turns = at("turns", [P, 2, TT, 96], F32, KVB0 + KB)
        rope_k = at("rope_k", [P, 2, TT, 96], F32, KVB0 + 3 * KB)
        latq_hi = at("latq_hi", [P, 4, S], F32R, H0)
        latq_lo = at("latq_lo", [P, 4, S], F32R, H0 + 4 * KB)
        latk_hi = at("latk_hi", [P, 4, S], F32R, H0 + 8 * KB)
        latk_lo = at("latk_lo", [P, 4, S], F32R, H0 + 12 * KB)
        lat = at("lat", [P, 2, TT, LORA], F32, H0 + 16 * KB)
        qnT = at("qnT", [P, AH, S], F32, H0 + 24 * KB)
        kT_a = at("kT_a", [P, AH, S], F32, H0 + 36 * KB)
        v_a = at("v_a", [P, TT, AH, P], F32, H0 + 48 * KB)
        qmT_a = at("qmT_a", [P, MH, S], F32, H0 + 60 * KB)
        kmT_a = at("kmT_a", [P, MH, M], F32, H0 + 64 * KB)
        vm_a = at("vm_a", [P, 2, MH, P], F32, H0 + 68 * KB)
        qpT = at("qpT", [P, AH // 2, S], F32, H0 + 72 * KB)
        kpT = at("kpT", [P, S], F32, H0 + 78 * KB)
        diag_kv = at("diag_kv", [P, TT, P], F32, H0 + 79 * KB)
        xbT_hi = at("xbT_hi", [P, KC, S], F32R, H0)
        xbT_lo = at("xbT_lo", [P, KC, S], F32R, H0 + 16 * KB)
        kT_b = at("kT_b", [P, 2 * BH, S], F32, H0 + 32 * KB)
        v_b = at("v_b", [P, TT, BH, VD], F32, H0 + 44 * KB)
        qT_b = at("qT_b", [P, 2 * BH, S], F32, H0 + 56 * KB)
        qmT_b = at("qmT_b", [P, MH, S], F32, H0 + 68 * KB)
        o_nat = at("o_nat", [P, BH, TT, VD], F32, H0)
        probs = at("probs", [P, 2, 2, 512], F32, H0 + 12 * KB)
        pT = at("pT", [P, 2, 512], F32, H0 + 20 * KB)
        y_o = at("y_o", [P, TT, D], F32, H0 + 24 * KB)
        gain_o = at("gain_o", [P, D], F32, H0 + 80 * KB)
        hT_hi = at("hT_hi", [P, FC, S], F32R, H0)
        hT_lo = at("hT_lo", [P, FC, S], F32R, H0 + 44 * KB)
        scratch = at("scratch", [P, 2, 4, S], F32, M0)
        conv = at("conv", [P, 2, 4, 2 * FC], F32, M0 + 8 * KB)
        m = M0 + 8 * KB + 2816
        gcol = at("gcol", [P, P], F32, m)
        ident = at("ident", [P, P], F32, m + 512)
        diag = at("diag", [P, TT, P], F32, m + 1024)
        cosine = at("cosine", [P, TT, 96], F32, m + 2048)
        sine = at("sine", [P, TT, 96], F32, m + 2816)
        ident_b = at("ident_b", [P, P], BF16, m + 3584)
        mask_b = at("mask_b", [P, P], BF16, m + 3840)
        stat = at("stat", [P, 4, 8], F32, m + 4096)
        ssp = at("ssp", [P, 2, 8], F32, m + 4224)
        nrm = at("nrm", [P, 8], F32, m + 4288)
        osum = at("osum", [P, 3, 12], F32, m + 4320)
        neglam = at("neglam", [P, 4], F32, m + 4480)
        eps = at("eps", [P, 1], F32, m + 4512)
        pos_i = at("pos_i", [P, TT], I32, m + 4544)
        pos_f = at("pos_f", [P, TT], F32, m + 4576)
        assert m + 4608 + base <= 229344

        ps = ctx.enter_context(nc.psum_tensor("ps", [P, 8, 512], F32))

        w_landed = [sem(f"w_landed{k}") for k in range(R)]
        small_landed = sem("small_landed")
        rope_landed = sem("rope_landed")
        mem_landed = [sem(f"mem_landed{t}") for t in range(2)]
        x_landed = [sem(f"x_landed{t}") for t in range(TT)]
        gain_landed = sem("gain_landed")
        out_stored = sem("out_stored")
        hi_ready = sem("hi_ready")
        lo_ready = sem("lo_ready")
        step_used = sem("step_used")
        pair_act = sem("pair_act")
        pair_dve = sem("pair_dve")
        consts_ready = sem("consts_ready")
        pool_step = sem("pool_step")
        tr_ready = sem("tr_ready")
        tr_copied = sem("tr_copied")
        tr_hi = sem("tr_hi")
        tr_lo = sem("tr_lo")
        sq_ready = sem("sq_ready")
        sq_dve = sem("sq_dve")
        ss_ready = sem("ss_ready")
        std_ready = sem("std_ready")
        diag_ready = sem("diag_ready")
        x_piece = sem("x_piece")
        raw_ready = sem("raw_ready")
        rope_ready = sem("rope_ready")
        range_ready = sem("range_ready")
        trig_ready = sem("trig_ready")
        lam_prod = sem("lam_prod")
        lam_exp = sem("lam_exp")
        s_ready = sem("s_ready")
        max_ready = sem("max_ready")
        e_ready = sem("e_ready")
        p_ready = sem("p_ready")
        pT_ready = sem("pT_ready")
        pT_copied = sem("pT_copied")
        o_ready = sem("o_ready")
        o_hi = sem("o_hi")
        o_lo = sem("o_lo")
        on_scaled = sem("on_scaled")
        dve_link = sem("dve_link")
        gate_ready = sem("gate_ready")
        h_ready = sem("h_ready")
        h_hi = sem("h_hi")
        h_lo = sem("h_lo")
        ostd_ready = sem("ostd_ready")

        ITEMS_A = [("mla", h) for h in range(AH)] + [("mem", h) for h in range(MH)]
        ITEMS_B = [("diff", h) for h in range(BH)] + [("mem", h) for h in range(MH)]

        view = {k: v.rearrange("(c p) n -> p c n", p=P) for k, v in w.items()}

        blk = ctx.enter_context(nc.Block())

        @blk.sync
        def _(sp):
            def load(s, src, per=0, i=None, width=1024):
                if s >= R:
                    sp.wait_ge(lo_ready, val(s - R + 1, per, i))
                dst = w_raw[:, s % R, 0:width]
                sp.dma_start(dst.rearrange("p (c n) -> p c n", c=src.shape[1]), src)\
                    .then_inc(w_landed[s % R], 16)

            def tile(s0, name, steps, n0, per=0, i=None, width=512, first=0):
                cols = slice(n0, n0 + width) if i is None else bass.ds(n0, width)
                for k in range(steps):
                    c = (first + 2 * k) % (2 * steps)
                    load(s0 + k, view[name][:, c:c + 2, cols], per, i, 2 * width)
                    if s0 + k == MEMA + R - 1:
                        for t in range(TT):
                            sp.dma_start(x[:, t, :], x_in[t * P:(t + 1) * P, :])\
                                .then_inc(x_landed[t], 16)

            for t in range(2):
                sp.dma_start(mem[:, t, :], mem_in[t * P:(t + 1) * P, :]).then_inc(mem_landed[t], 16)
            for j in range(2):
                tile(MEMA + j * DSTEPS, "a_w_mem_kv", DSTEPS, 512 * j)
            for j in range(2):
                tile(MEMB + j * DSTEPS, "b_w_mem_kv", DSTEPS, 512 * j)
            tile(QLAT, "a_w_in", DSTEPS, 0)
            for c in range(KC):
                load(KVLAT + c, view["a_w_in"][:, c:c + 1, LORA:LORA + KVW], width=KVW)
            tile(QMEM, "a_w_in", DSTEPS, 2 * LORA + RD)
            for j in range(6):
                tile(UQ + j * LSTEPS, "a_w_uq", LSTEPS, 384 * j, width=384)
            for j in range(6):
                tile(UKV + j * LSTEPS, "a_w_ukv", LSTEPS, 512 * j)
            with sp.Fori(0, 2) as i:
                for j in range(2):
                    tile(OA + j * DSTEPS, "a_w_o", DSTEPS, i * 1024 + 512 * j, 2 * DSTEPS, i)
            for layer, s_in, s_out in ((0, IN0, OUT0), (1, IN1, OUT1)):
                if layer == 1:
                    with sp.Fori(0, BH // 2) as i:
                        for j in range(2):
                            tile(SKV + j * DSTEPS, "shared_w_kv", DSTEPS, i * 1024 + 512 * j,
                                 2 * DSTEPS, i)
                    with sp.Fori(0, 2) as i:
                        for j in range(2):
                            tile(BQ + j * DSTEPS, "b_w_in", DSTEPS, i * 1024 + 512 * j,
                                 2 * DSTEPS, i)
                    for j in range(4):
                        tile(OB + j * DSTEPS, "b_w_o", DSTEPS, 512 * j, first=MEM_CHUNK)
                with sp.Fori(0, FJ) as i:
                    tile(s_in, f"ffn_w_in{layer}", DSTEPS, i * 512, 2 * DSTEPS, i)
                    tile(s_in + DSTEPS, f"ffn_w_in{layer}", DSTEPS, i * 512 + F, 2 * DSTEPS, i)
                with sp.Fori(0, 2) as i:
                    for j in range(2):
                        tile(s_out + j * FSTEPS, f"ffn_w_out{layer}", FSTEPS,
                             i * 1024 + 512 * j, 2 * FSTEPS, i)
            for q in range(4):
                sp.wait_ge(x_piece, 12 + q + 1)
                t, half = q // 2, q % 2
                sp.dma_start(out[t * P:(t + 1) * P, half * 1024:(half + 1) * 1024],
                             x[:, t, half * 1024:(half + 1) * 1024]).then_inc(out_stored, 16)
            sp.wait_ge(out_stored, 64)

        @blk.gpsimd
        def _(pool):
            nc.gpsimd.memset(ident[:, :], 0.0).then_inc(pool_step, 1)
            nc.gpsimd.memset(ident_b[:, :], 0.0).then_inc(pool_step, 1)
            nc.gpsimd.memset(mask_b[:, :], 0.0).then_inc(pool_step, 1)
            pool.wait_ge(pool_step, 3)
            for t in (ident, ident_b):
                nc.gpsimd.affine_select(out=t[:, :], in_=t[:, :], compare_op=ALU.not_equal,
                                        fill=1.0, base=0, pattern=[[-1, P]], channel_multiplier=1)\
                    .then_inc(consts_ready, 1)
            nc.gpsimd.affine_select(out=mask_b[:, :], in_=mask_b[:, :], compare_op=ALU.is_ge,
                                    fill=NEG, base=0, pattern=[[-1, P]], channel_multiplier=1)\
                .then_inc(consts_ready, 1)
            nc.gpsimd.memset(eps[:, :], EPS).then_inc(consts_ready, 1)
            pool.wait_ge(tr_copied, 3)
            pool.wait_ge(trig_ready, 1)
            pool.wait_ge(lam_prod, 1)
            pool.dma_start(gain_o[:, :], vec["a_post"].partition_broadcast(P))\
                .then_inc(gain_landed, 16)
            for k, (name, dst, step) in enumerate((("ffn_post0", gain_f, OUT0),
                                                   ("b_post", gain_o, OUT0),
                                                   ("ffn_post1", gain_f, OUT1))):
                if dst is gain_f:
                    pool.wait_ge(step_used, step)
                else:
                    pool.wait_ge(step_used, SKV)
                pool.dma_start(dst[:, :], vec[name].partition_broadcast(P)).then_inc(gain_landed, 16)

        @blk.tensor
        def _(pe):
            def release(tile_no, per=0, i=None):
                if tile_no >= 2:
                    pe.wait_ge(pair_act, val(tile_no - 1, per, i))
                    pe.wait_ge(pair_dve, val(tile_no - 1, per, i))

            def product(s0, steps, tile_no, xhi, xlo, parts, width=512, chunks=2, per=0, i=None,
                        per_t=0, first_chunk=0, late=(), after=None):
                release(tile_no, per_t, i)
                pair = 2 * (tile_no % 2)
                for k in range(steps):
                    pe.wait_ge(lo_ready, val(s0 + k + 1, per, i))
                    for step, semaphore, value in late:
                        if k == step:
                            pe.wait_ge(semaphore, value)
                    slot = (s0 + k) % R
                    for c in range(chunks):
                        wh = w_hi[:, slot, c * width:(c + 1) * width]
                        wl = w_lo[:, slot, c * width:(c + 1) * width]
                        n_ch = k * chunks + c
                        ch = (first_chunk + n_ch) % (steps * chunks)
                        seen = set()
                        for mode, bank, o0, on, tok, cols in parts:
                            dst = ps[:, bank if bank >= 4 else pair + bank, o0:o0 + on]
                            first = n_ch == 0 and bank not in seen
                            seen.add(bank)
                            last = n_ch == steps * chunks - 1
                            a_hi, a_lo = xhi[:, ch, tok], xlo[:, ch, tok]
                            pairs = [(a_hi, cols(wh)), (a_hi, cols(wl)), (a_lo, cols(wh))]
                            if mode == "T":
                                pairs = [(b, a) for a, b in (pairs[0], pairs[2], pairs[1])]
                            for q, (st, mv) in enumerate(pairs):
                                mm = nc.tensor.matmul(dst, st, mv, start=first and q == 0,
                                                      stop=last and q == 2, skip_group_check=True)
                    mm.then_inc(step_used, 1)
                    if after:
                        after(k)

            whole = lambda n: (lambda a: a[:, 0:n])
            every = slice(0, S)
            tok_t = [slice(0, P), slice(P, S)]

            def n_parts(width=512):
                return [("N", t, 0, width, tok_t[t], whole(width)) for t in range(TT)]

            def t_parts():
                return [("T", k // 2, 256 * (k % 2), 256, every,
                         (lambda a, k=k: a[:, k * P:(k + 1) * P])) for k in range(4)]

            def kv_parts():
                ks = [("T", 0, 256 * h, 256, every,
                       (lambda a, h=h: a[:, 256 * h:256 * h + P])) for h in range(2)]
                pick = lambda a: a.rearrange("p (h n) -> p h n", h=2)[:, :, P:2 * P]
                return ks + [("N", 1, 256 * t, 256, tok_t[t], pick) for t in range(TT)]

            def uq_parts():
                qs = [("T", 0, 256 * h, 256, every,
                       (lambda a, h=h: a[:, 192 * h:192 * h + P])) for h in range(2)]
                pick = lambda a: a.rearrange("p (h n) -> p h n", h=2)[:, :, P:P + RD]
                return qs + [("N", 1, 128 * t, 128, tok_t[t], pick) for t in range(TT)]

            done = {"C": 0, "N": 0}
            items_done = [0]

            def phase_free():
                if done["N"]:
                    pe.wait_ge(tr_lo, done["N"])
                if done["C"]:
                    pe.wait_ge(tr_copied, done["C"])
                if items_done[0]:
                    pe.wait_ge(o_lo, items_done[0])

            def norm_group(src, g, diag=diag):
                for c in range(2):
                    for t in range(TT):
                        f0 = (2 * g + c) * P
                        mm = nc.tensor.matmul(ps[:, 4 + g % 4, 256 * c + P * t:256 * c + P * t + P],
                                              src[:, t, f0:f0 + P], diag[:, t, :],
                                              start=True, stop=True)
                mm.then_inc(tr_ready, 1)

            def norm_transpose(src, chunks, diag_no, diag=diag):
                phase_free()
                pe.wait_ge(diag_ready, diag_no)
                for g in range(chunks // 2):
                    if g >= 4:
                        pe.wait_ge(tr_lo, done["N"] + g - 3)
                    norm_group(src, g, diag)
                done["N"] += chunks // 2

            def norm_product(src, diag_no, *args):
                phase_free()
                pe.wait_ge(diag_ready, diag_no)
                for g in range(4):
                    norm_group(src, g)
                base_n = done["N"]
                late = [(k, tr_lo, base_n + k + 1) for k in range(DSTEPS)]
                product(*args, late=late, after=lambda k: k < 4 and norm_group(src, 4 + k))
                done["N"] += DSTEPS

            def rope_transpose(bank, blocks, rope_no):
                pe.wait_ge(rope_ready, rope_no)
                for k, src in enumerate(blocks):
                    mm = nc.tensor.transpose(ps[:, bank, P * k:P * (k + 1)], src, ident[:, :])
                mm.then_inc(tr_ready, 1)
                done["C"] += 1

            rot = scratch[:, 0].rearrange("p a b -> p (a b)")

            def attend(items, km, vm, first_item):
                phase_free()
                pe.wait_ge(pair_act, pair_count[0])
                pe.wait_ge(pair_dve, pair_count[0])
                t0 = first_item

                def scores(t):
                    kind, h = items[t]
                    lag = 2 if is_b else 4
                    if t >= lag:
                        pe.wait_ge(e_ready, t0 + t - lag + 1)
                    if kind == "mem":
                        b = 2 * (t % 2) if is_b else t % 4
                        for q in range(TT):
                            mm = nc.tensor.matmul(ps[:, b, 256 * q:256 * q + M],
                                                  qm[:, h, q * P:(q + 1) * P], km[:, h, :],
                                                  start=q == 0, stop=True, skip_group_check=True)
                    else:
                        for j in range(2 if kind == "diff" else 1):
                            b = 2 * (t % 2) + j if is_b else t % 4
                            for q in range(TT):
                                dst = ps[:, b, P * q:P * q + (q + 1) * P]
                                n = (q + 1) * P
                                if kind == "diff":
                                    g = 2 * h + j
                                    nc.tensor.matmul(dst, qT_b[:, g, q * P:(q + 1) * P],
                                                     kT_b[:, g, 0:n], start=q == 0, stop=False,
                                                     skip_group_check=True)
                                else:
                                    nc.tensor.matmul(dst, qnT[:, h, q * P:(q + 1) * P],
                                                     kT_a[:, h, 0:n], start=q == 0, stop=False,
                                                     skip_group_check=True)
                                    r0 = RD * (h % 2)
                                    nc.tensor.matmul(dst, qpT[r0:r0 + RD, h // 2, q * P:(q + 1) * P],
                                                     kpT[r0:r0 + RD, 0:n], start=False, stop=False,
                                                     skip_group_check=True)
                                mm = nc.tensor.matmul(ps[:, b, P * 2 * q:P * 2 * q + P],
                                                      ident_b[:, :], mask_b[:, :], start=False,
                                                      stop=True, skip_group_check=True)
                    mm.then_inc(s_ready, 1)

                def transposes(t):
                    kind, h = items[t]
                    pe.wait_ge(p_ready, t0 + t + 1)
                    if t >= 2:
                        pe.wait_ge(pT_copied, t0 + t - 1)
                    src = probs[:, t % 2, 0, :]
                    dst = ps[:, 4 + t % 2, :]
                    if kind == "mem":
                        moves = [(256 * q + P * k, 256 * k + P * q) for q in range(2) for k in range(2)]
                    else:
                        moves = [(0, 0), (P, P), (2 * P, 2 * P)]
                    for a, b in moves:
                        mm = nc.tensor.transpose(dst[:, b:b + P], src[:, a:a + P], ident[:, :])
                    mm.then_inc(pT_ready, 1)

                def outputs(t):
                    kind, h = items[t]
                    pe.wait_ge(pT_copied, t0 + t + 1)
                    if t >= 2:
                        pe.wait_ge(o_lo, t0 + t - 1)
                    p = pT[:, t % 2, :]
                    dst = ps[:, 6 + t % 2, :]
                    if kind == "mem":
                        for k in range(2):
                            mm = nc.tensor.matmul(dst[:, 0:S], vm[:, k, h, :],
                                                  p[:, 256 * k:256 * k + S], start=k == 0, stop=k == 1)
                    elif kind == "mla":
                        nc.tensor.matmul(dst[:, 0:S], v_a[:, 0, h, :], p[:, 0:S], start=True,
                                         stop=False, skip_group_check=True)
                        mm = nc.tensor.matmul(dst[:, P:S], v_a[:, 1, h, :], p[:, 2 * P:3 * P],
                                              start=False, stop=True, skip_group_check=True)
                    else:
                        nc.tensor.matmul(dst[:, 0:VD], p[:, 0:P], v_b[:, 0, h, :], start=True,
                                         stop=True, skip_group_check=True)
                        nc.tensor.matmul(dst[:, VD:2 * VD], p[:, P:2 * P], v_b[:, 0, h, :],
                                         start=False, stop=False, skip_group_check=True)
                        mm = nc.tensor.matmul(dst[:, VD:2 * VD], p[:, 2 * P:3 * P], v_b[:, 1, h, :],
                                              start=False, stop=True, skip_group_check=True)
                    mm.then_inc(o_ready, 1)

                is_b = first_item > 0
                qm = qmT_b if is_b else qmT_a
                n = len(items)
                lead = 2 if is_b else 3
                for t in range(lead):
                    scores(t)
                for t in range(n + 1):
                    if t + lead < n:
                        scores(t + lead)
                    if t < n:
                        transposes(t)
                    if t >= 1:
                        outputs(t - 1)
                items_done[0] += n

            pair_count = [0]

            pe.wait_ge(small_landed, 16 * N_SMALL)
            pe.wait_ge(consts_ready, 4)
            nc.tensor.transpose(ps[:, 4, 0:N_GAIN], gain_rows[0:N_GAIN, :],
                                ident[0:N_GAIN, 0:N_GAIN]).then_inc(tr_ready, 1)
            for layer in range(2):
                for k in range(4):
                    mm = nc.tensor.transpose(ps[:, 5 + layer, 88 * k:88 * (k + 1)],
                                             conv_rows[:, layer, k, :], ident[0:2 * FC, 0:2 * FC])
                mm.then_inc(tr_ready, 1)
            done["C"] = 3

            norm_product(mem, 1, MEMA, DSTEPS, MEMA_T, mTa_hi, mTa_lo, kv_parts())
            product(MEMA + DSTEPS, DSTEPS, MEMA_T + 1, mTa_hi, mTa_lo, kv_parts())
            norm_transpose(x, KC, 2)
            for j in range(2):
                product(MEMB + j * DSTEPS, DSTEPS, MEMB_T + j, mTb_hi, mTb_lo, kv_parts())
            pe.wait_ge(tr_lo, done["N"])
            product(QLAT, DSTEPS, QLAT_T, xT_hi, xT_lo, n_parts())
            kpe_parts = [("N", 7, RD * t, RD, tok_t[t], (lambda a: a[:, LORA:KVW]))
                         for t in range(TT)]
            product(KVLAT, KC, KVLAT_T, xT_hi, xT_lo, n_parts() + kpe_parts, width=KVW, chunks=1)
            norm_transpose(lat[:, 0], 4, 3)
            product(QMEM, DSTEPS, QMEM_T, xT_hi, xT_lo, t_parts())
            norm_transpose(lat[:, 1], 4, 4, diag_kv)
            rope_transpose(6, [rot[:, P * t:P * (t + 1)] for t in range(TT)], 1)
            qpe_blocks = [rot[:, P * t:P * (t + 1)] for t in range(TT)]
            for j in range(6):
                product(UQ + j * LSTEPS, LSTEPS, UQ_T + j, latq_hi, latq_lo, uq_parts(), width=384)
                if j == 0:
                    phase_free()
                else:
                    if j >= 3:
                        pe.wait_ge(tr_copied, groups_before(T_QPE, "C") + j - 2)
                    rope_transpose(4 + (j - 1) % 2, qpe_blocks, 1 + j)
            for j in range(6):
                product(UKV + j * LSTEPS, LSTEPS, UKV_T + j, latk_hi, latk_lo, kv_parts())
                if j == 0:
                    pe.wait_ge(tr_copied, groups_before(T_QPE, "C") + 4)
                    rope_transpose(5, qpe_blocks, 7)
            pe.wait_ge(tr_lo, done["N"])
            pair_count[0] = OA_T
            attend(ITEMS_A, kmT_a, vm_a, 0)

            def wide_product(s0, t0, steps, xhi, xlo, late=(), first_chunk=0):
                with pe.Fori(0, 2) as i:
                    for j in range(2):
                        product(s0 + j * steps, steps, t0 + j, xhi, xlo, n_parts(),
                                per=2 * steps, i=i, per_t=2, late=late if j == 0 else (),
                                first_chunk=first_chunk)

            def ffn(s_in, t_in, s_out, t_out, diag_no):
                tiles = lambda j, **kw: product(s_in + j * DSTEPS, DSTEPS, t_in + j, xT_hi, xT_lo,
                                                t_parts(), **kw)
                norm_product(x, diag_no, s_in, DSTEPS, t_in, xT_hi, xT_lo, t_parts())
                with pe.Fori(0, FJ - 1) as i:
                    for j in (1, 2):
                        tiles(j, per=2 * DSTEPS, i=i, per_t=2)
                tiles(2 * FJ - 1)
                h_count[0] += FJ
                pe.wait_ge(h_lo, h_count[0] - 1)
                wide_product(s_out, t_out, FSTEPS, hT_hi, hT_lo, [(FSTEPS - 2, h_lo, h_count[0])])

            h_count = [0]
            pe.wait_ge(o_lo, items_done[0] - 2)
            wide_product(OA, OA_T, DSTEPS, xT_hi, xT_lo, [(DSTEPS - 1, o_lo, items_done[0])])
            ffn(IN0, IN0_T, OUT0, OUT0_T, 5)

            kb_blocks = [rot[:, 512 * t + P * g:512 * t + P * (g + 1)]
                         for g in range(2) for t in range(TT)]
            skv_tile = lambda j, **kw: product(SKV + j * DSTEPS, DSTEPS, SKV_T + j, xT_hi, xT_lo,
                                               n_parts(), **kw)
            c0 = groups_before(T_KB, "C")
            norm_product(x, 6, SKV, DSTEPS, SKV_T, xT_hi, xT_lo, n_parts())
            for j in range(1, BH):
                skv_tile(j)
                if j >= 3:
                    pe.wait_ge(tr_copied, c0 + j - 2)
                rope_transpose(4 + (j - 1) % 2, kb_blocks, 7 + j)
            qb_blocks = [[rot[:, 512 * t + P * g:512 * t + P * (g + 1)]
                          for g in (2 * q, 2 * q + 1) for t in range(TT)] for q in range(2)]
            c1 = groups_before(T_QB, "C")
            for j in range(3):
                product(BQ + j * DSTEPS, DSTEPS, BQ_T + j, xbT_hi, xbT_lo, n_parts())
                if j == 0:
                    pe.wait_ge(tr_copied, c0 + 4)
                    rope_transpose(5, kb_blocks, 13)
                else:
                    pe.wait_ge(tr_copied, c1 + 2 * (j - 1))
                    for q in range(2):
                        rope_transpose(6 + q, qb_blocks[q], 13 + j)
            product(BQ + 3 * DSTEPS, DSTEPS, BQ_T + 3, xbT_hi, xbT_lo, t_parts())
            pe.wait_ge(tr_copied, c1 + 4)
            for q in range(2):
                rope_transpose(6 + q, qb_blocks[q], 16)
            pair_count[0] = OB_T
            attend(ITEMS_B, kmT_b, vm_b, len(ITEMS_A))
            base_n = done["N"]
            for h in range(BH):
                if h == 4:
                    pe.wait_ge(o_lo, items_done[0])
                pe.wait_ge(on_scaled, h + 1)
                for c in range(2):
                    for t in range(TT):
                        o0 = 256 * c + P * t
                        mm = nc.tensor.transpose(ps[:, SUB_BANKS[h], o0:o0 + P],
                                                 o_nat[:, h, t, P * c:P * (c + 1)], ident[:, :])
                mm.then_inc(tr_ready, 1)
            done["N"] += BH
            wide_product(OB, OB_T, DSTEPS, xT_hi, xT_lo,
                         [(MH // 2 + h, tr_lo, base_n + h + 1) for h in range(BH)], MEM_CHUNK)
            ffn(IN1, IN1_T, OUT1, OUT1_T, 7)

        @blk.scalar
        def _(act):
            act.dma_start(gain_rows[0:N_GAIN, :], vec["gains"]).then_inc(small_landed, 16)
            act.dma_start(conv_rows[:, :, :, :].rearrange("c l j p -> c (l j p)"), vec["conv"])\
                .then_inc(small_landed, 16)
            act.dma_start(lam_rows[:, :, :].rearrange("p k n -> p (k n)"),
                          vec["lambda"].partition_broadcast(P)).then_inc(rope_landed, 16)
            act.dma_start(freq[:, :], inv_freq.partition_broadcast(P)).then_inc(rope_landed, 16)
            for t in range(TT):
                act.dma_start(pos_i[:, t:t + 1],
                              positions[t * P:(t + 1) * P].rearrange("(p a) -> p a", a=1))\
                    .then_inc(rope_landed, 16)

            n_split = [0]
            count = {"C": 0, "N": 0, "tr": 0, "sq": 0, "std": 0}

            def split(s, per=0, i=None):
                width = 1024
                if i is None and KVLAT <= s < QMEM:
                    width = KVW
                if i is None and UQ <= s < UKV:
                    width = 2 * 384
                act.wait_ge(w_landed[s % R], val(16 * (s // R + 1), 16 * per // R, i))
                if s >= R:
                    act.wait_ge(step_used, val(s - R + 1, per, i))
                nc.scalar.activation(w_hi[:, s % R, 0:width], w_raw[:, s % R, 0:width], ACT.Copy)\
                    .then_inc(hi_ready, 1)

            def splits_to(s):
                for k in range(n_split[0], min(s, STEPS)):
                    split(k)
                n_split[0] = max(n_split[0], min(s, STEPS))

            def root(n, width):
                count["std"] += 1
                act.wait_ge(ss_ready, count["std"])
                nc.scalar.activation(nrm[:, 2:4], nrm[:, 0:2], ACT.Sqrt, bias=eps[:, :],
                                     scale=1.0 / width).then_inc(std_ready, 1)

            squared = scratch[:, :, :, :].rearrange("p a b c -> p (a b c)").bitcast(BF16)
            unused = lambda k, n: squared[:, 1024 * k:1024 * k + n]

            def squares(pieces):
                for k, (src, col) in enumerate(pieces):
                    a = nc.scalar.activation(unused(2 * k, src.free_size()), src, ACT.Square,
                                             accum_out=col)
                a.then_inc(sq_ready, 1)
                count["sq"] += 1

            def split_transposes(chunks, targets, following=None):
                for g in range(chunks // 2):
                    count["tr"] += 1
                    act.wait_ge(tr_ready, count["tr"])
                    for g0, hi in targets:
                        for c in range(2):
                            ch = 2 * g + c
                            a = nc.scalar.activation(hi[:, ch, :], ps[:, 4 + g % 4, 256 * c:256 * c + S],
                                                     ACT.Copy, scale=gcol[:, g0 + ch:g0 + ch + 1])
                    a.then_inc(tr_hi, 1)
                    if following is not None and g >= 3:
                        splits_to(following + min(g + 1, CUT))

            def copy_transposed(dst, bank):
                count["tr"] += 1
                act.wait_ge(tr_ready, count["tr"])
                nc.scalar.activation(dst, ps[:, bank, 0:dst.free_size()], ACT.Copy)\
                    .then_inc(tr_copied, 1)

            act.wait_ge(consts_ready, 4)
            act.wait_ge(mem_landed[0], 16)
            squares([(mem[:, 0, :], ssp[:, 0, 0:1])])
            copy_transposed(gcol[:, 0:N_GAIN], 4)
            for layer in range(2):
                copy_transposed(conv[:, layer].rearrange("p j c -> p (j c)"), 5 + layer)
            root(1, D)
            splits_to(MEMA + AHEAD)
            split_transposes(KC, [(GAIN_ROWS["a_mem"], mTa_hi), (GAIN_ROWS["b_mem"], mTb_hi)], MEMA)

            def kv_epilogue(t, kT, heads, s_end):
                act.wait_ge(step_used, s_end)
                nc.scalar.activation(kT[:, heads, :].rearrange("p h s -> p (h s)"),
                                     ps[:, 2 * (t % 2), :], ACT.Copy).then_inc(pair_act, 1)

            splits_to(MEMA + DSTEPS + AHEAD)
            kv_epilogue(MEMA_T, kmT_a, slice(0, 2), MEMA + DSTEPS)
            act.wait_ge(range_ready, 1)
            nc.scalar.activation(cosine[:, :, :], rope_k[:, 0], ACT.Sin)
            nc.scalar.activation(sine[:, :, :], rope_k[:, 1], ACT.Sin).then_inc(trig_ready, 1)
            act.wait_ge(lam_prod, 1)
            nc.scalar.activation(neglam[:, 2:4], neglam[:, 0:2], ACT.Exp).then_inc(lam_exp, 1)
            for t in range(TT):
                act.wait_ge(x_landed[t], 16)
            squares([(x[:, t, :], ssp[:, t, 0:1]) for t in range(TT)])
            root(1, D)
            splits_to(MEMB + AHEAD)
            kv_epilogue(MEMA_T + 1, kmT_a, slice(2, 4), MEMB)
            split_transposes(KC, [(GAIN_ROWS["a_pre"], xT_hi)])
            splits_to(MEMB + DSTEPS + AHEAD)
            kv_epilogue(MEMB_T, kmT_b, slice(0, 2), MEMB + DSTEPS)
            splits_to(QLAT + AHEAD)
            kv_epilogue(MEMB_T + 1, kmT_b, slice(2, 4), QLAT)

            def latent_epilogue(k, t, s_end):
                act.wait_ge(step_used, s_end)
                pr = 2 * (t % 2)
                nc.scalar.activation(lat[:, k, 0, :], ps[:, pr, :], ACT.Copy).then_inc(pair_act, 1)
                act.wait_ge(pair_act, t + 1)
                act.wait_ge(pair_dve, t + 1)
                squares([(lat[:, k, u, :], ssp[:, u, 0:1]) for u in range(TT)])
                root(1, LORA)

            def to_scratch(dst, src):
                return nc.scalar.activation(dst, src, ACT.Copy).then_inc(raw_ready, 1)

            def raw_epilogue(t, width, s_end):
                act.wait_ge(step_used, s_end)
                pr = 2 * (t % 2)
                nc.scalar.activation(rawv[:, :, 0:width], ps[:, pr:pr + 2, 0:width], ACT.Copy)\
                    .then_inc(pair_act, 1)

            rawv = scratch[:, 0].rearrange("p a b -> p (a b)").rearrange("p (t n) -> p t n", t=TT)
            raw_a = scratch[:, 0].rearrange("p a b -> p (a b)")[:, 0:256]\
                .rearrange("p (t n) -> p t n", t=TT)

            splits_to(KVLAT + AHEAD)
            latent_epilogue(0, QLAT_T, KVLAT)
            splits_to(QMEM + AHEAD)
            latent_epilogue(1, KVLAT_T, QMEM)
            to_scratch(raw_a[:, :, 0:RD], ps[:, 7, 0:P].rearrange("p (t n) -> p t n", t=TT))
            split_transposes(4, [(GAIN_ROWS["q_norm"], latq_hi)])
            splits_to(UQ + AHEAD)
            act.wait_ge(step_used, UQ)
            nc.scalar.activation(qmT_a[:, 0:2, :].rearrange("p h s -> p (h s)"),
                                 ps[:, 2 * (QMEM_T % 2), :], ACT.Copy).then_inc(pair_act, 1)
            split_transposes(4, [(GAIN_ROWS["kv_norm"], latk_hi)])
            copy_transposed(kpT[:, :], 6)
            for j in range(6):
                splits_to(UQ + (j + 1) * LSTEPS + AHEAD)
                if j:
                    copy_transposed(qpT[:, j - 1, :], 4 + (j - 1) % 2)
                act.wait_ge(step_used, UQ + (j + 1) * LSTEPS)
                pr = 2 * ((UQ_T + j) % 2)
                to_scratch(raw_a, ps[:, pr + 1, 0:256].rearrange("p (t n) -> p t n", t=TT))
                nc.scalar.activation(qnT[:, 2 * j:2 * j + 2, :].rearrange("p h s -> p (h s)"),
                                     ps[:, pr, :], ACT.Copy).then_inc(pair_act, 1)
            for j in range(6):
                splits_to(UKV + (j + 1) * LSTEPS + AHEAD)
                if j == 0:
                    copy_transposed(qpT[:, 5, :], 5)
                kv_epilogue(UKV_T + j, kT_a, slice(2 * j, 2 * j + 2), UKV + (j + 1) * LSTEPS)

            def attend(items, first_item, scale):
                t0 = first_item
                is_b = first_item > 0

                def exps(t):
                    kind, h = items[t]
                    act.wait_ge(max_ready, t0 + t + 1)
                    if t >= 2:
                        act.wait_ge(pT_ready, t0 + t - 1)
                    sc = scale if kind != "mem" else SCALE_B
                    for j in range(2 if kind == "diff" else 1):
                        b = 2 * (t % 2) + j if is_b else t % 4
                        cuts = ((0, 256), (256, 512)) if kind == "mem" else ((0, P), (P, 3 * P))
                        for q, (a, z) in enumerate(cuts):
                            e = nc.scalar.activation(
                                probs[:, t % 2, j, a:z], ps[:, b, a:z], ACT.Exp, scale=sc,
                                bias=stat[:, t % 4, 2 * j + q:2 * j + q + 1],
                                accum_out=sums[:, t % 4, 2 * j + q:2 * j + q + 1])
                    e.then_inc(e_ready, 1)

                def copy_pT(t):
                    kind, h = items[t]
                    act.wait_ge(pT_ready, t0 + t + 1)
                    if t >= 2:
                        act.wait_ge(o_ready, t0 + t - 1)
                    n = 512 if kind == "mem" else 3 * P
                    nc.scalar.activation(pT[:, t % 2, 0:n], ps[:, 4 + t % 2, 0:n], ACT.Copy)\
                        .then_inc(pT_copied, 1)

                def output(t):
                    kind, h = items[t]
                    act.wait_ge(o_ready, t0 + t + 1)
                    src = ps[:, 6 + t % 2, :]
                    if kind == "diff":
                        for q in range(TT):
                            a = nc.scalar.activation(
                                unused(2 * (t % 2) + q, VD), src[:, VD * q:VD * (q + 1)], ACT.Square,
                                accum_out=osum[:, 0, 2 * h + q:2 * h + q + 1])
                        a.then_inc(o_hi, 1)
                    else:
                        ch = h if kind == "mla" else 12 + h
                        nc.scalar.activation(xT_hi[:, ch, :], src[:, 0:S], ACT.Copy).then_inc(o_hi, 1)

                for t in range(len(items) + 2):
                    if t < len(items):
                        exps(t)
                    if 1 <= t <= len(items):
                        copy_pT(t - 1)
                    if t >= 2:
                        output(t - 2)
                    if is_b and t == len(items) - 1:
                        act.wait_ge(o_hi, t0 + BH)
                        nc.scalar.activation(osum[:, 1, :], osum[:, 0, :], ACT.Sqrt, bias=eps[:, :],
                                             scale=1.0 / VD).then_inc(ostd_ready, 1)

            sums = stat[:, :, 4:8]
            attend(ITEMS_A, 0, SCALE_A)

            def wide_epilogue(s0, t0, steps):
                splits_to(s0 + AHEAD)
                lead, end = n_split[0] - s0, min(s0 + 4 * steps + AHEAD, STEPS)

                def turn(i, static=False):
                    for j in range(2):
                        for k in range(steps):
                            if not static or s0 + (2 * i + j) * steps + k + lead < end:
                                split(s0 + j * steps + k + lead, 2 * steps, i)
                            if k + lead + 1 - steps != AHEAD:
                                continue
                            act.wait_ge(step_used, val(s0 + (j + 1) * steps, 2 * steps, i))
                            for u in range(TT):
                                a = nc.scalar.activation(
                                    unused(2 * j + u, 512), ps[:, 2 * ((t0 + j) % 2) + u, :],
                                    ACT.Square, accum_out=ssp[:, u, bass.ds(i * 2 + j, 1)])
                            a.then_inc(pair_act, 1)

                if lead == AHEAD and end < STEPS:
                    with act.Fori(0, 2) as i:
                        turn(i)
                else:
                    for i in range(2):
                        turn(i, static=True)
                n_split[0] = end

            pieces = [0]

            def residual_norm(last=False):
                root(4, D)
                if last:
                    return
                cols = []
                for q in range(4):
                    pieces[0] += 1
                    act.wait_ge(x_piece, pieces[0])
                    t, half = q // 2, q % 2
                    a = nc.scalar.activation(unused(q, 1024), x[:, t, half * 1024:(half + 1) * 1024], ACT.Square,
                                             accum_out=ssp[:, t, half:half + 1])
                a.then_inc(sq_ready, 1)
                root(2, D)

            def ffn_epilogues(layer, s_in, t_in, g_count):
                splits_to(s_in + CUT)

                def first_tap(i, j):
                    act.wait_ge(step_used, val(s_in + (j + 1) * DSTEPS, 2 * DSTEPS, i))
                    for m4 in range(4):
                        ch = i * 4 + (m4 + j * FC)
                        a = nc.scalar.activation(
                            scratch[:, j, m4, :],
                            ps[:, 2 * ((t_in + j) % 2) + m4 // 2, 256 * (m4 % 2):256 * (m4 % 2) + S],
                            ACT.Identity, scale=conv[:, layer, 2, bass.ds(ch, 1)],
                            bias=conv[:, layer, 3, bass.ds(ch, 1)])
                    a.then_inc(pair_act, 1)

                def gate(i):
                    act.wait_ge(pair_dve, val(t_in + 1, 2, i))
                    nc.scalar.activation(scratch[:, 0], scratch[:, 0],
                                         ACT.Gelu_apprx_tanh).then_inc(gate_ready, 1)

                def hi_half(i):
                    act.wait_ge(h_ready, val(g_count + 1, 1, i))
                    nc.scalar.activation(hT_hi[:, bass.ds(i * 4, 4), :], scratch[:, 1],
                                         ACT.Copy).then_inc(h_hi, 1)

                with act.Fori(0, FJ) as i:
                    for j in range(2):
                        for k in range(DSTEPS):
                            split(s_in + j * DSTEPS + k + CUT, 2 * DSTEPS, i)
                            ahead = k + CUT + 1 - DSTEPS
                            if ahead == 3:
                                first_tap(i, j)
                            if ahead == 5 and j == 0:
                                gate(i)
                            if ahead == 6 and j == 1:
                                hi_half(i)
                n_split[0] = s_in + 2 * FJ * DSTEPS + CUT

            wide_epilogue(OA, OA_T, DSTEPS)
            residual_norm()
            splits_to(IN0 + AHEAD)
            split_transposes(KC, [(GAIN_ROWS["ffn_pre"], xT_hi)], IN0)
            ffn_epilogues(0, IN0, IN0_T, 0)
            wide_epilogue(OUT0, OUT0_T, FSTEPS)
            residual_norm()
            split_transposes(KC, [(GAIN_ROWS["shared"], xT_hi), (GAIN_ROWS["b_pre"], xbT_hi)], SKV)
            for j in range(BH):
                splits_to(SKV + (j + 1) * DSTEPS + AHEAD)
                if j:
                    copy_transposed(kT_b[:, 2 * j - 2:2 * j, :].rearrange("p h s -> p (h s)"),
                                    4 + (j - 1) % 2)
                raw_epilogue(SKV_T + j, 256, SKV + (j + 1) * DSTEPS)
            for j in range(3):
                splits_to(BQ + (j + 1) * DSTEPS + AHEAD)
                if j == 0:
                    copy_transposed(kT_b[:, 10:12, :].rearrange("p h s -> p (h s)"), 5)
                else:
                    for q in range(2):
                        h0 = 4 * (j - 1) + 2 * q
                        copy_transposed(qT_b[:, h0:h0 + 2, :].rearrange("p h s -> p (h s)"), 6 + q)
                raw_epilogue(BQ_T + j, 512, BQ + (j + 1) * DSTEPS)
            splits_to(OB + AHEAD)
            act.wait_ge(step_used, OB)
            nc.scalar.activation(qmT_b[:, 0:2, :].rearrange("p h s -> p (h s)"),
                                 ps[:, 2 * ((BQ_T + 3) % 2), :], ACT.Copy).then_inc(pair_act, 1)
            for q in range(2):
                copy_transposed(qT_b[:, 8 + 2 * q:10 + 2 * q, :].rearrange("p h s -> p (h s)"), 6 + q)
            attend(ITEMS_B, len(ITEMS_A), SCALE_B)
            for h in range(BH):
                count["tr"] += 1
                act.wait_ge(tr_ready, count["tr"])
                for c in range(2):
                    g0 = GAIN_ROWS["subln"] + c
                    a = nc.scalar.activation(xT_hi[:, 2 * h + c, :],
                                             ps[:, SUB_BANKS[h], 256 * c:256 * c + S], ACT.Copy, scale=gcol[:, g0:g0 + 1])
                a.then_inc(tr_hi, 1)
            wide_epilogue(OB, OB_T, DSTEPS)
            residual_norm()
            split_transposes(KC, [(GAIN_ROWS["ffn_pre"] + KC, xT_hi)], IN1)
            ffn_epilogues(1, IN1, IN1_T, FJ)
            wide_epilogue(OUT1, OUT1_T, FSTEPS)
            residual_norm(last=True)

        @blk.vector
        def _(dve):
            linked = [0]

            def link(ins, base=0):
                linked[0] += 1
                ins.then_inc(dve_link, 1)
                dve.wait_ge(dve_link, base + linked[0])

            n_split = [0]
            count = {"N": 0, "sq": 0, "std": 0, "gain": 0, "rope": 0}

            def split(s, per=0, i=None):
                width = 1024
                if i is None and KVLAT <= s < QMEM:
                    width = KVW
                if i is None and UQ <= s < UKV:
                    width = 2 * 384
                dve.wait_ge(hi_ready, val(s + 1, per, i))
                nc.vector.tensor_tensor(w_lo[:, s % R, 0:width], w_raw[:, s % R, 0:width],
                                        w_hi[:, s % R, 0:width].bitcast(F32), ALU.subtract)\
                    .then_inc(lo_ready, 1)

            def splits_to(s):
                for k in range(n_split[0], min(s, STEPS)):
                    split(k)
                n_split[0] = max(n_split[0], min(s, STEPS))

            def sums(parts):
                nc.vector.reduce_sum(nrm[:, 0:2], ssp[:, :, 0:parts], axis=AX).then_inc(ss_ready, 1)

            def inverse_std():
                count["std"] += 1
                dve.wait_ge(std_ready, count["std"])
                link(nc.vector.reciprocal(nrm[:, 4:6], nrm[:, 2:4]))

            def diagonal(dst):
                for t in range(TT):
                    d = nc.vector.tensor_scalar(dst[:, t, :], ident[:, :], nrm[:, 4 + t:5 + t], None,
                                                ALU.mult)
                d.then_inc(diag_ready, 1)

            def norm(parts, dst=diag):
                count["sq"] += 1
                dve.wait_ge(sq_ready, count["sq"])
                sums(parts)
                inverse_std()
                diagonal(dst)

            def split_transposes(chunks, targets, following=None):
                for g in range(chunks // 2):
                    count["N"] += 1
                    dve.wait_ge(tr_hi, count["N"])
                    for g0, hi, lo in targets:
                        for c in range(2):
                            ch = 2 * g + c
                            d = nc.vector.scalar_tensor_tensor(
                                out=lo[:, ch, :], in0=ps[:, 4 + g % 4, 256 * c:256 * c + S],
                                scalar=gcol[:, g0 + ch:g0 + ch + 1], in1=hi[:, ch, :].bitcast(F32),
                                op0=ALU.mult, op1=ALU.subtract)
                    d.then_inc(tr_lo, 1)
                    if following is not None and g >= 3:
                        splits_to(following + min(g + 1, CUT))

            def angles_and_lambda():
                dve.wait_ge(rope_landed, 16 * N_ROPE)
                link(nc.vector.tensor_copy(pos_f[:, :], pos_i[:, :]))
                for t in range(TT):
                    d = nc.vector.tensor_scalar(angle[:, t, :], freq[:, :], pos_f[:, t:t + 1], None,
                                                ALU.mult)
                link(d)
                for k, quarter in ((0, 0.25), (1, 0.0)):
                    d = nc.vector.tensor_scalar(turns[:, k], angle[:, :, :], 1.0 / (2 * math.pi), quarter,
                                                ALU.mult, ALU.add)
                link(d)
                link(nc.vector.tensor_scalar(turns[:, :], turns[:, :], ROUND, ROUND, ALU.add,
                                             ALU.subtract))
                for k in range(2):
                    d = nc.vector.scalar_tensor_tensor(
                        out=rope_k[:, k], in0=turns[:, k], scalar=-TWO_PI[0], in1=angle[:, :, :],
                        op0=ALU.mult, op1=ALU.add)
                link(d)
                for part in TWO_PI[1:]:
                    link(nc.vector.scalar_tensor_tensor(
                        out=rope_k[:, :], in0=turns[:, :], scalar=-part, in1=rope_k[:, :],
                        op0=ALU.mult, op1=ALU.add))
                link(nc.vector.tensor_scalar_add(rope_k[:, 0], rope_k[:, 0], math.pi / 2))
                nc.vector.tensor_scalar(rope_k[:, :], rope_k[:, :], SIN_MAX, -SIN_MAX, ALU.min, ALU.max)\
                    .then_inc(range_ready, 1)
                lr = lam_rows[:, :, :].rearrange("p (a b) n -> p a b n", a=2)
                link(nc.vector.tensor_tensor(lr[:, :, 0, :], lr[:, :, 0, :], lr[:, :, 1, :], ALU.mult))
                nc.vector.reduce_sum(neglam[:, 0:2], lr[:, :, 0, :], axis=AX).then_inc(lam_prod, 1)

            squared = scratch[:, 1].rearrange("p a b -> p (a b)").bitcast(BF16)
            dve.wait_ge(mem_landed[1], 16)
            nc.vector.tensor_tensor_reduce(
                out=squared, in0=mem[:, 1, :], in1=mem[:, 1, :], scale=1.0, scalar=0.0,
                op0=ALU.mult, op1=ALU.add, accum_out=ssp[:, 1, 0:1]).then_inc(sq_dve, 1)
            dve.wait_ge(sq_dve, 1)
            norm(1)
            splits_to(MEMA + AHEAD)
            dve.wait_ge(tr_copied, 3)
            g0 = GAIN_ROWS["subln"]
            link(nc.vector.tensor_scalar(gcol[:, g0:g0 + 2], gcol[:, g0:g0 + 2], 1.0 - LAMBDA_INIT,
                                         None, ALU.mult))
            split_transposes(KC, [(GAIN_ROWS["a_mem"], mTa_hi, mTa_lo),
                                  (GAIN_ROWS["b_mem"], mTb_hi, mTb_lo)], MEMA)

            def v_epilogue(t, v, heads, s_end):
                dve.wait_ge(step_used, s_end)
                nc.vector.tensor_copy(v[:, :, heads, :].rearrange("p t h n -> p t (h n)"),
                                      ps[:, 2 * (t % 2) + 1, :].rearrange("p (t n) -> p t n", t=2))\
                    .then_inc(pair_dve, 1)

            splits_to(MEMA + DSTEPS + AHEAD)
            angles_and_lambda()
            v_epilogue(MEMA_T, vm_a, slice(0, 2), MEMA + DSTEPS)
            dve.wait_ge(lam_exp, 1)
            link(nc.vector.tensor_tensor(neglam[:, 0:1], neglam[:, 3:4], neglam[:, 2:3], ALU.subtract))
            link(nc.vector.tensor_scalar_add(neglam[:, 0:1], neglam[:, 0:1], -LAMBDA_INIT))
            norm(1)
            splits_to(MEMB + AHEAD)
            v_epilogue(MEMA_T + 1, vm_a, slice(2, 4), MEMB)
            split_transposes(KC, [(GAIN_ROWS["a_pre"], xT_hi, xT_lo)])
            splits_to(MEMB + DSTEPS + AHEAD)
            v_epilogue(MEMB_T, vm_b, slice(0, 2), MEMB + DSTEPS)
            splits_to(QLAT + AHEAD)
            v_epilogue(MEMB_T + 1, vm_b, slice(2, 4), QLAT)

            raw = scratch[:, 0].rearrange("p a b -> p (a b)")
            tmp = scratch[:, 1].rearrange("p a b -> p (a b)")

            def rotate(semaphore, value, row, width, c0, half, twice=False):
                dve.wait_ge(semaphore, value)
                v4 = lambda a: a[:, 0:TT * row].rearrange("p (t n) -> p t n", t=TT)[:, :, 0:width]\
                    .rearrange("p t (g d) -> p t g d", d=2 * half)
                xr, tr = v4(raw), v4(tmp)
                g = width // (2 * half)
                wide = [P, TT, g, half]
                cos = cosine[:, :, c0:c0 + half].unsqueeze(2).to_broadcast(wide)
                sin = sine[:, :, c0:c0 + half].unsqueeze(2).to_broadcast(wide)
                a, b = (slice(0, half), slice(half, 2 * half))
                d = nc.vector.tensor_tensor(tr[:, :, :, a], xr[:, :, :, b], sin, ALU.mult)
                if not twice:
                    d.then_inc(pair_dve, 1)
                nc.vector.tensor_tensor(tr[:, :, :, b], xr[:, :, :, a], sin, ALU.mult)
                nc.vector.tensor_tensor(xr[:, :, :, a], xr[:, :, :, a], cos, ALU.mult)
                link(nc.vector.tensor_tensor(xr[:, :, :, b], xr[:, :, :, b], cos, ALU.mult))
                nc.vector.tensor_tensor(xr[:, :, :, a], xr[:, :, :, a], tr[:, :, :, a], ALU.subtract)
                d = nc.vector.tensor_tensor(xr[:, :, :, b], xr[:, :, :, b], tr[:, :, :, b], ALU.add)
                if twice:
                    link(d)
                    rows = raw[:, 0:TT * row].rearrange("p (t n) -> p t n", t=TT)
                    d = nc.vector.tensor_copy(rows[:, :, width:2 * width], rows[:, :, 0:width])
                d.then_inc(rope_ready, 1)

            def latent_epilogue(k, t, s_end, dst):
                dve.wait_ge(step_used, s_end)
                nc.vector.tensor_copy(lat[:, k, 1, :], ps[:, 2 * (t % 2) + 1, :]).then_inc(pair_dve, 1)
                norm(1, dst)

            splits_to(KVLAT + AHEAD)
            latent_epilogue(0, QLAT_T, KVLAT, diag)
            splits_to(QMEM + AHEAD)
            latent_epilogue(1, KVLAT_T, QMEM, diag_kv)
            rotate(raw_ready, 1, P, RD, 0, RD // 2, twice=True)
            split_transposes(4, [(GAIN_ROWS["q_norm"], latq_hi, latq_lo)])
            splits_to(UQ + AHEAD)
            dve.wait_ge(step_used, UQ)
            nc.vector.tensor_copy(qmT_a[:, 2:4, :].rearrange("p h s -> p (h s)"),
                                  ps[:, 2 * (QMEM_T % 2) + 1, :]).then_inc(pair_dve, 1)
            split_transposes(4, [(GAIN_ROWS["kv_norm"], latk_hi, latk_lo)])
            for j in range(6):
                splits_to(UQ + (j + 1) * LSTEPS + AHEAD)
                rotate(raw_ready, 2 + j, P, P, 0, RD // 2)
            for j in range(6):
                splits_to(UKV + (j + 1) * LSTEPS + AHEAD)
                v_epilogue(UKV_T + j, v_a, slice(2 * j, 2 * j + 2), UKV + (j + 1) * LSTEPS)

            def attend(items, first_item, scale):
                t0 = first_item
                is_b = first_item > 0

                def maxima(t):
                    kind, h = items[t]
                    dve.wait_ge(s_ready, t0 + t + 1)
                    m4 = stat[:, t % 4, :]
                    if kind == "mem":
                        b = 2 * (t % 2) if is_b else t % 4
                        n = 2
                        d = nc.vector.reduce_max(
                            m4[:, 0:2], ps[:, b, :].rearrange("p (q n) -> p q n", q=2), axis=AX)
                    else:
                        n = 4 if kind == "diff" else 2
                        for j in range(n // 2):
                            b = 2 * (t % 2) + j if is_b else t % 4
                            for q, (a, z) in enumerate(((0, P), (P, 3 * P))):
                                d = nc.vector.reduce_max(m4[:, 2 * j + q:2 * j + q + 1],
                                                         ps[:, b, a:z], axis=AX)
                    link(d)
                    sc = SCALE_B if kind == "mem" else scale
                    nc.vector.tensor_scalar(m4[:, 0:n], m4[:, 0:n], -sc, None, ALU.mult)\
                        .then_inc(max_ready, 1)

                def normalise(t):
                    kind, h = items[t]
                    dve.wait_ge(e_ready, t0 + t + 1)
                    m4 = stat[:, t % 4, :]
                    n = 4 if kind == "diff" else 2
                    link(nc.vector.reciprocal(m4[:, 4:4 + n], m4[:, 4:4 + n]))
                    p = probs[:, t % 2]
                    cuts = ((0, 256), (256, 512)) if kind == "mem" else ((0, P), (P, 3 * P))
                    if kind == "diff":
                        nc.vector.tensor_scalar(m4[:, 6:8], m4[:, 6:8], neglam[:, 0:1], None, ALU.mult)
                    for q, (a, z) in enumerate(cuts):
                        d = nc.vector.tensor_scalar(p[:, 0, a:z], p[:, 0, a:z], m4[:, 4 + q:5 + q],
                                                    None, ALU.mult)
                    if kind == "diff":
                        link(d)
                        for q, (a, z) in enumerate(cuts):
                            d = nc.vector.scalar_tensor_tensor(
                                out=p[:, 0, a:z], in0=p[:, 1, a:z], scalar=m4[:, 6 + q:7 + q],
                                in1=p[:, 0, a:z], op0=ALU.mult, op1=ALU.add)
                    d.then_inc(p_ready, 1)

                def output(t):
                    kind, h = items[t]
                    dve.wait_ge(o_hi, t0 + t + 1)
                    src = ps[:, 6 + t % 2, :]
                    if kind == "diff":
                        nc.vector.tensor_copy(o_nat[:, h].rearrange("p t n -> p (t n)"), src)\
                            .then_inc(o_lo, 1)
                    else:
                        ch = h if kind == "mla" else 12 + h
                        nc.vector.tensor_tensor(xT_lo[:, ch, :], src[:, 0:S],
                                                xT_hi[:, ch, :].bitcast(F32), ALU.subtract)\
                            .then_inc(o_lo, 1)

                for t in range(len(items) + 3):
                    if t < len(items):
                        maxima(t)
                    if 1 <= t <= len(items):
                        normalise(t - 1)
                    if t >= 3:
                        output(t - 3)
                    if is_b and t >= len(items):
                        if t == len(items):
                            dve.wait_ge(ostd_ready, 1)
                            link(nc.vector.reciprocal(osum[:, 2, :], osum[:, 1, :]))
                        for h in range(2 * (t - len(items)), 2 * (t - len(items)) + 2):
                            rstd = osum[:, 2, 2 * h:2 * h + 2].unsqueeze(2)
                            nc.vector.tensor_tensor(o_nat[:, h], o_nat[:, h],
                                                    rstd.to_broadcast([P, TT, VD]), ALU.mult)\
                                .then_inc(on_scaled, 1)

            attend(ITEMS_A, 0, SCALE_A)

            def wide_epilogue(s0, t0, steps, y, gain):
                splits_to(s0 + AHEAD)
                lead, end = n_split[0] - s0, min(s0 + 4 * steps + AHEAD, STEPS)
                count["gain"] += 1

                def turn(i, static=False):
                    for j in range(2):
                        for k in range(steps):
                            if not static or s0 + (2 * i + j) * steps + k + lead < end:
                                split(s0 + j * steps + k + lead, 2 * steps, i)
                            if k + lead + 1 - steps != AHEAD:
                                continue
                            if j == 0:
                                dve.wait_ge(gain_landed, 16 * count["gain"])
                            dve.wait_ge(pair_act, val(t0 + j + 1, 2, i))
                            pr = 2 * ((t0 + j) % 2)
                            cols = bass.ds(i * 1024 + 512 * j, 512)
                            nc.vector.tensor_tensor(
                                y[:, :, cols], ps[:, pr:pr + 2, :],
                                gain[:, cols].unsqueeze(1).to_broadcast([P, TT, 512]), ALU.mult)\
                                .then_inc(pair_dve, 1)

                if lead == AHEAD and end < STEPS:
                    with dve.Fori(0, 2) as i:
                        turn(i)
                else:
                    for i in range(2):
                        turn(i, static=True)
                n_split[0] = end

            def residual(y, t_end):
                dve.wait_ge(pair_dve, t_end)
                sums(4)
                inverse_std()
                for q in range(4):
                    t, half = q // 2, q % 2
                    cols = slice(half * 1024, (half + 1) * 1024)
                    nc.vector.scalar_tensor_tensor(
                        out=x[:, t, cols], in0=y[:, t, cols], scalar=nrm[:, 4 + t:5 + t],
                        in1=x[:, t, cols], op0=ALU.mult, op1=ALU.add).then_inc(x_piece, 1)

            def ffn_epilogues(layer, s_in, t_in, g_count):
                splits_to(s_in + CUT)
                before = linked[0]

                def other_taps(i, j):
                    dve.wait_ge(pair_act, val(t_in + j + 1, 2, i))
                    for shift in (1, 2):
                        for m4 in range(4):
                            ch = i * 4 + (m4 + j * FC)
                            u = ps[:, 2 * ((t_in + j) % 2) + m4 // 2,
                                   256 * (m4 % 2):256 * (m4 % 2) + S - shift]
                            c = scratch[:, j, m4, shift:S]
                            d = nc.vector.scalar_tensor_tensor(
                                out=c, in0=u, scalar=conv[:, layer, 2 - shift, bass.ds(ch, 1)],
                                in1=c, op0=ALU.mult, op1=ALU.add)
                        if shift == 1:
                            link(d, i * 2)
                    d.then_inc(pair_dve, 1)

                def gate_times_value(i):
                    dve.wait_ge(pair_dve, val(t_in + 2, 2, i))
                    dve.wait_ge(gate_ready, val(g_count + 1, 1, i))
                    nc.vector.tensor_tensor(scratch[:, 1], scratch[:, 0], scratch[:, 1], ALU.mult)\
                        .then_inc(h_ready, 1)

                def lo_half(i):
                    dve.wait_ge(h_hi, val(g_count + 1, 1, i))
                    hs = bass.ds(i * 4, 4)
                    nc.vector.tensor_tensor(hT_lo[:, hs, :], scratch[:, 1], hT_hi[:, hs, :].bitcast(F32),
                                            ALU.subtract).then_inc(h_lo, 1)

                with dve.Fori(0, FJ) as i:
                    for j in range(2):
                        for k in range(DSTEPS):
                            split(s_in + j * DSTEPS + k + CUT, 2 * DSTEPS, i)
                            ahead = k + CUT + 1 - DSTEPS
                            if ahead == 3:
                                other_taps(i, j)
                            if ahead == 4 and j == 1:
                                gate_times_value(i)
                            if ahead == 7 and j == 1:
                                lo_half(i)
                assert linked[0] - before == 2
                linked[0] = before + 2 * FJ
                n_split[0] = s_in + 2 * FJ * DSTEPS + CUT

            wide_epilogue(OA, OA_T, DSTEPS, y_o, gain_o)
            residual(y_o, OA_T + 4)
            norm(2)
            split_transposes(KC, [(GAIN_ROWS["ffn_pre"], xT_hi, xT_lo)], IN0)
            ffn_epilogues(0, IN0, IN0_T, 0)
            wide_epilogue(OUT0, OUT0_T, FSTEPS, y_f, gain_f)
            residual(y_f, OUT0_T + 4)
            norm(2)
            split_transposes(KC, [(GAIN_ROWS["shared"], xT_hi, xT_lo),
                                  (GAIN_ROWS["b_pre"], xbT_hi, xbT_lo)], SKV)
            for j in range(BH):
                splits_to(SKV + (j + 1) * DSTEPS + AHEAD)
                dve.wait_ge(pair_act, SKV_T + j + 1)
                pr = 2 * ((SKV_T + j) % 2)
                nc.vector.tensor_copy(v_b[:, :, j, :], ps[:, pr:pr + 2, 256:512])
                rotate(pair_act, SKV_T + j + 1, 512, 256, 32, HD // 2)
            for j in range(3):
                splits_to(BQ + (j + 1) * DSTEPS + AHEAD)
                rotate(pair_act, BQ_T + j + 1, 512, 512, 32, HD // 2)
            splits_to(OB + AHEAD)
            dve.wait_ge(step_used, OB)
            nc.vector.tensor_copy(qmT_b[:, 2:4, :].rearrange("p h s -> p (h s)"),
                                  ps[:, 2 * ((BQ_T + 3) % 2) + 1, :]).then_inc(pair_dve, 1)
            attend(ITEMS_B, len(ITEMS_A), SCALE_B)
            for h in range(BH):
                count["N"] += 1
                dve.wait_ge(tr_hi, count["N"])
                for c in range(2):
                    g0 = GAIN_ROWS["subln"] + c
                    d = nc.vector.scalar_tensor_tensor(
                        out=xT_lo[:, 2 * h + c, :], in0=ps[:, SUB_BANKS[h], 256 * c:256 * c + S],
                        scalar=gcol[:, g0:g0 + 1], in1=xT_hi[:, 2 * h + c, :].bitcast(F32),
                        op0=ALU.mult, op1=ALU.subtract)
                d.then_inc(tr_lo, 1)
            wide_epilogue(OB, OB_T, DSTEPS, y_o, gain_o)
            residual(y_o, OB_T + 4)
            norm(2)
            split_transposes(KC, [(GAIN_ROWS["ffn_pre"] + KC, xT_hi, xT_lo)], IN1)
            ffn_epilogues(1, IN1, IN1_T, FJ)
            wide_epilogue(OUT1, OUT1_T, FSTEPS, y_f, gain_f)
            residual(y_f, OUT1_T + 4)


_INS = ["x", "mem", "positions", "a_attn_norm_pre", "a_w_in", "a_q_norm", "a_w_uq", "a_kv_norm",
        "a_w_ukv", "a_mem_norm", "a_w_mem_kv", "a_w_o", "a_attn_norm_post", "shared_kv_norm",
        "shared_w_kv", "b_attn_norm_pre", "b_w_in", "b_lambda_q1", "b_lambda_k1", "b_lambda_q2",
        "b_lambda_k2", "b_subln", "b_mem_norm", "b_w_mem_kv", "b_w_o", "b_attn_norm_post",
        "ffn_norm_pre", "ffn_w_in", "ffn_conv_w", "ffn_conv_b", "ffn_w_out", "ffn_norm_post"]


_GAINS = ["a_attn_norm_pre", "a_mem_norm", "b_mem_norm", "b_attn_norm_pre", "shared_kv_norm",
          "ffn_norm_pre", "a_q_norm", "a_kv_norm", "b_subln"]
_LAMBDAS = ["b_lambda_q1", "b_lambda_k1", "b_lambda_q2", "b_lambda_k2"]
_PACKED = _GAINS + _LAMBDAS + ["ffn_conv_w", "ffn_conv_b"]


def build(nc, a, inv_freq, out):
    w = {n: a[n][0] for n in ("a_w_in", "a_w_uq", "a_w_ukv", "a_w_mem_kv", "a_w_o", "b_w_in",
                              "b_w_mem_kv", "b_w_o")}
    w["shared_w_kv"] = a["shared_w_kv"]
    for layer in range(2):
        w[f"ffn_w_in{layer}"] = a["ffn_w_in"][layer]
        w[f"ffn_w_out{layer}"] = a["ffn_w_out"][layer]
    vec = {
        "gains": a["gains"], "conv": a["conv"], "lambda": a["lambda"],
        "a_post": a["a_attn_norm_post"][0], "b_post": a["b_attn_norm_post"][0],
        "ffn_post0": a["ffn_norm_post"][0], "ffn_post1": a["ffn_norm_post"][1],
    }
    program(nc, a["x"][0], a["mem"][0], a["positions"][0], inv_freq, w, vec, out[0])


def kernel(**inputs):
    import concourse.bacc as bacc
    from concourse.bass_utils import run_bass_kernel_spmd

    nc = bacc.Bacc("TRN2", target_bir_lowering=False, num_devices=1)
    arrays, aps = {}, {}

    def give(name, v):
        arrays[f"in_{name}"] = np.ascontiguousarray(v)
        aps[name] = nc.dram_tensor(f"in_{name}", v.shape, mybir.dt.from_np(v.dtype),
                                   kind="ExternalInput").ap()

    given = {name: np.asarray(inputs[name]) for name in _INS}
    for name in _INS:
        if name not in _PACKED:
            give(name, given[name])
    rows = [given[n].reshape(-1, P) for n in _GAINS]
    give("gains", np.concatenate(rows))
    taps = np.concatenate([given["ffn_conv_w"], given["ffn_conv_b"][:, None]], axis=1)
    give("conv", taps.reshape(2, 4, 2 * FC, P).transpose(2, 0, 1, 3).reshape(2 * FC, 8 * P))
    give("lambda", np.concatenate([given[n].reshape(-1) for n in _LAMBDAS]))
    freq = np.concatenate([np.exp(np.float32(-math.log(THETA)) * np.arange(n, dtype=np.float32)
                                  * np.float32(1.0 / n)).astype(np.float32)
                           for n in (RD // 2, HD // 2)])
    arrays["in_freq"] = freq
    f = nc.dram_tensor("in_freq", freq.shape, F32, kind="ExternalInput").ap()
    out = nc.dram_tensor("out_0", (1, S, D), F32, kind="ExternalOutput").ap()
    build(nc, aps, f, out)
    r = run_bass_kernel_spmd(nc, [arrays], core_ids=[0])
    return r.results[0]["out_0"]
```

```python
import math
from contextlib import ExitStack

import numpy as np

import concourse.bass as bass
from concourse import mybir

P = 128
F32 = mybir.dt.float32
F32R = mybir.dt.float32r
BF16 = mybir.dt.bfloat16
I32 = mybir.dt.int32
ALU = mybir.AluOpType
ACT = mybir.ActivationFunctionType
AX = mybir.AxisListType.X

S = 256
M = 256
TT = S // P
D = 2048
KC = D // P
AH, NOPE, RD = 12, 128, 64
LORA = 512
BH, HD, VD = 6, 128, 256
MH = 4
F = 5632
FC = F // P
EPS = 1e-6
LAMBDA_INIT = 0.8 - 0.6 * math.exp(-0.3)
THETA = 10000.0
SCALE_A = float(NOPE + RD) ** -0.5
SCALE_B = float(HD) ** -0.5
NEG = -3.0e38

R = 4
X_PIECES = ((0, 1024), (1024, 1536), (1536, 2048))
HOLD = R
AHEAD = 3
CUT = 7
DSTEPS = KC // 2
LSTEPS = LORA // P // 2
FSTEPS = FC // 2
FJ = F // 512

MEMA, MEMA_T = 0, 0
MEMB, MEMB_T = MEMA + 2 * DSTEPS, MEMA_T + 2
QLAT, QLAT_T = MEMB + 2 * DSTEPS, MEMB_T + 2
KVLAT, KVLAT_T = QLAT + DSTEPS, QLAT_T + 1
KVW = LORA + RD
QMEM, QMEM_T = KVLAT + KC, KVLAT_T + 1
UQ, UQ_T = QMEM + DSTEPS, QMEM_T + 1
UKV, UKV_T = UQ + 6 * LSTEPS, UQ_T + 6
OA, OA_T = UKV + 6 * LSTEPS, UKV_T + 6
IN0, IN0_T = OA + 4 * DSTEPS, OA_T + 4
OUT0, OUT0_T = IN0 + 2 * FJ * DSTEPS, IN0_T + 2 * FJ
SKV, SKV_T = OUT0 + 4 * FSTEPS, OUT0_T + 4
BQ, BQ_T = SKV + BH * DSTEPS, SKV_T + BH
OB, OB_T = BQ + 4 * DSTEPS, BQ_T + 4
IN1, IN1_T = OB + 4 * DSTEPS, OB_T + 4
OUT1, OUT1_T = IN1 + 2 * FJ * DSTEPS, IN1_T + 2 * FJ
STEPS = OUT1 + 4 * FSTEPS

GROUPS = [("C", 3), ("N", 8), ("N", 8), ("N", 2), ("N", 2), ("C", 1), ("C", 6), ("N", 8),
          ("N", 8), ("C", 6), ("C", 6), ("N", 6), ("N", 8)]
T_QPE, T_KB, T_QB = 6, 9, 10

GAIN_ROWS = {}
_row = 0
for _name, _n in (("a_pre", KC), ("a_mem", KC), ("b_mem", KC), ("b_pre", KC), ("shared", KC),
                  ("ffn_pre", 2 * KC), ("q_norm", 4), ("kv_norm", 4), ("subln", 2)):
    GAIN_ROWS[_name] = _row
    _row += _n
N_GAIN = _row


MEM_CHUNK = KC - MH
N_SMALL, N_ROPE = 2, 2 + TT
ROUND = 1.5 * 2.0 ** 23
TWO_PI = (6.28125, float(np.float32(np.round((2 * math.pi - 6.28125) * 2 ** 20) / 2 ** 20)), None)
TWO_PI = TWO_PI[:2] + (2 * math.pi - TWO_PI[0] - TWO_PI[1],)
SIN_MAX = 3.1415925


SUB_BANKS = (4, 5, 2 - 2 * (OB_T % 2), 3 - 2 * (OB_T % 2), 6, 7)


def groups_before(phase, kind=None):
    return sum(n for k, n in GROUPS[:phase] if kind in (None, k))


def val(const, per, i):
    return const if i is None else i * per + const


def program(nc, x_in, mem_in, positions, inv_freq, w, vec, out):
    with ExitStack() as ctx:
        sem = lambda name: ctx.enter_context(nc.semaphore(name))
        base = 16512

        def at(name, shape, dt, offset):
            return nc.alloc_sbuf_tensor_at(name, shape, dt, offset=base + offset)

        KB = 1024
        X0, XT0, RING0, KVB0, H0, M0 = 0, 16 * KB, 48 * KB, 96 * KB, 104 * KB, 192 * KB
        x = at("x", [P, TT, D], F32, X0)
        xT_hi = at("xT_hi", [P, KC, S], F32R, XT0)
        xT_lo = at("xT_lo", [P, KC, S], F32R, XT0 + 16 * KB)
        w_raw = at("w_raw", [P, R, 1024], F32, RING0)
        w_hi = at("w_hi", [P, R, 1024], F32R, RING0 + 16 * KB)
        w_lo = at("w_lo", [P, R, 1024], F32R, RING0 + 32 * KB)
        y_f = at("y_f", [P, TT, D], F32, XT0)
        gain_f = at("gain_f", [P, D], F32, XT0 + 16 * KB)
        kmT_b = at("kmT_b", [P, MH, M], F32, KVB0)
        vm_b = at("vm_b", [P, 2, MH, P], F32, KVB0 + 4 * KB)
        mTa_hi = at("mTa_hi", [P, KC, M], F32R, H0)
        mTa_lo = at("mTa_lo", [P, KC, M], F32R, H0 + 16 * KB)
        mTb_hi = at("mTb_hi", [P, KC, M], F32R, H0 + 32 * KB)
        mTb_lo = at("mTb_lo", [P, KC, M], F32R, H0 + 48 * KB)
        mem = at("mem", [P, 2, D], F32, H0 + 64 * KB)
        gain_rows = at("gain_rows", [P, P], F32, H0 + 80 * KB)
        conv_rows = at("conv_rows", [2 * FC, 2, 4, P], F32, H0 + 81 * KB)
        lam_rows = at("lam_rows", [P, 4, P], F32, H0 + 85 * KB)
        freq = at("freq", [P, 96], F32, H0 + 87 * KB)
        angle = at("angle", [P, TT, 96], F32, KVB0)
        turns = at("turns", [P, 2, TT, 96], F32, KVB0 + KB)
        rope_k = at("rope_k", [P, 2, TT, 96], F32, KVB0 + 3 * KB)
        latq_hi = at("latq_hi", [P, 4, S], F32R, H0)
        latq_lo = at("latq_lo", [P, 4, S], F32R, H0 + 4 * KB)
        latk_hi = at("latk_hi", [P, 4, S], F32R, H0 + 8 * KB)
        latk_lo = at("latk_lo", [P, 4, S], F32R, H0 + 12 * KB)
        lat = at("lat", [P, 2, TT, LORA], F32, H0 + 16 * KB)
        qnT = at("qnT", [P, AH, S], F32, H0 + 24 * KB)
        kT_a = at("kT_a", [P, AH, S], F32, H0 + 36 * KB)
        v_a = at("v_a", [P, TT, AH, P], F32, H0 + 48 * KB)
        qmT_a = at("qmT_a", [P, MH, S], F32, H0 + 60 * KB)
        kmT_a = at("kmT_a", [P, MH, M], F32, H0 + 64 * KB)
        vm_a = at("vm_a", [P, 2, MH, P], F32, H0 + 68 * KB)
        qpT = at("qpT", [P, AH // 2, S], F32, H0 + 72 * KB)
        kpT = at("kpT", [P, S], F32, H0 + 78 * KB)
        diag_kv = at("diag_kv", [P, TT, P], F32, H0 + 79 * KB)
        xbT_hi = at("xbT_hi", [P, KC, S], F32R, H0)
        xbT_lo = at("xbT_lo", [P, KC, S], F32R, H0 + 16 * KB)
        kT_b = at("kT_b", [P, 2 * BH, S], F32, H0 + 32 * KB)
        v_b = at("v_b", [P, TT, BH, VD], F32, H0 + 44 * KB)
        qT_b = at("qT_b", [P, 2 * BH, S], F32, H0 + 56 * KB)
        qmT_b = at("qmT_b", [P, MH, S], F32, H0 + 68 * KB)
        o_nat = at("o_nat", [P, BH, TT, VD], F32, H0)
        probs = at("probs", [P, 2, 2, 512], F32, H0 + 12 * KB)
        pT = at("pT", [P, 2, 512], F32, H0 + 20 * KB)
        y_o = at("y_o", [P, TT, D], F32, H0 + 24 * KB)
        gain_o = at("gain_o", [P, D], F32, H0 + 80 * KB)
        hT_hi = at("hT_hi", [P, FC, S], F32R, H0)
        hT_lo = at("hT_lo", [P, FC, S], F32R, H0 + 44 * KB)
        scratch = at("scratch", [P, 2, 4, S], F32, M0)
        conv = at("conv", [P, 2, 4, 2 * FC], F32, M0 + 8 * KB)
        pe_raw = at("pe_raw", [P, 2, S], F32, M0 + 2 * KB)
        m = M0 + 8 * KB + 2816
        gcol = at("gcol", [P, P], F32, m)
        ident = at("ident", [P, P], F32, m + 512)
        diag = at("diag", [P, TT, P], F32, m + 1024)
        cosine = at("cosine", [P, TT, 96], F32, m + 2048)
        sine = at("sine", [P, TT, 96], F32, m + 2816)
        ident_b = at("ident_b", [P, P], BF16, m + 3584)
        mask_b = at("mask_b", [P, P], BF16, m + 3840)
        stat = at("stat", [P, 4, 8], F32, m + 4096)
        ssp = at("ssp", [P, 2, 8], F32, m + 4224)
        nrm = at("nrm", [P, 8], F32, m + 4288)
        osum = at("osum", [P, 3, 12], F32, m + 4320)
        neglam = at("neglam", [P, 4], F32, m + 4480)
        eps = at("eps", [P, 1], F32, m + 4512)
        pos_i = at("pos_i", [P, TT], I32, m + 4544)
        pos_f = at("pos_f", [P, TT], F32, m + 4576)
        inv_sum = at("inv_sum", [P, BH, 4], F32, m + 4608)
        assert m + 4704 + base <= 229344

        def uq_columns(buffer, s, rotary, sorted_):
            a = buffer[:, s % R, 0:768].rearrange("p (c n) -> p c n", c=2)
            if sorted_:
                a = a[:, :, 256:384] if rotary else a[:, :, 0:256]
                return a.rearrange("p c (h n) -> p c h n", h=2)
            a = a.rearrange("p c (h n) -> p c h n", h=2)
            return a[:, :, :, P:P + RD] if rotary else a[:, :, :, 0:P]

        ps = ctx.enter_context(nc.psum_tensor("ps", [P, 8, 512], F32))

        w_landed = [sem(f"w_landed{k}") for k in range(R)]
        small_landed = sem("small_landed")
        rope_landed = sem("rope_landed")
        mem_landed = [sem(f"mem_landed{t}") for t in range(2)]
        x_landed = [sem(f"x_landed{t}") for t in range(TT)]
        gain_landed = sem("gain_landed")
        out_stored = sem("out_stored")
        hi_ready = sem("hi_ready")
        lo_ready = sem("lo_ready")
        step_used = sem("step_used")
        first_bank_done = sem("first_bank_done")
        bank_squared = sem("bank_squared")
        pair_act = sem("pair_act")
        pair_dve = sem("pair_dve")
        eps_ready = sem("eps_ready")
        consts_ready = sem("consts_ready")
        pool_step = sem("pool_step")
        tr_ready = sem("tr_ready")
        tr_copied = sem("tr_copied")
        tr_hi = sem("tr_hi")
        tr_lo = sem("tr_lo")
        sq_ready = sem("sq_ready")
        sq_dve = sem("sq_dve")
        ss_ready = sem("ss_ready")
        std_ready = sem("std_ready")
        diag_ready = sem("diag_ready")
        x_piece = sem("x_piece")
        raw_ready = sem("raw_ready")
        unrotated = sem("unrotated")
        rope_ready = sem("rope_ready")
        range_ready = sem("range_ready")
        trig_ready = sem("trig_ready")
        lam_prod = sem("lam_prod")
        lam_exp = sem("lam_exp")
        s_ready = sem("s_ready")
        max_ready = sem("max_ready")
        e_ready = sem("e_ready")
        p_ready = sem("p_ready")
        pT_ready = sem("pT_ready")
        pT_copied = sem("pT_copied")
        o_ready = sem("o_ready")
        o_hi = sem("o_hi")
        o_lo = sem("o_lo")
        on_scaled = sem("on_scaled")
        dve_link = sem("dve_link")
        gate_ready = sem("gate_ready")
        h_ready = sem("h_ready")
        h_hi = sem("h_hi")
        h_lo = sem("h_lo")
        ostd_ready = sem("ostd_ready")

        ITEMS_A = [("mla", h) for h in range(AH)] + [("mem", h) for h in range(MH)]
        ITEMS_B = [("diff", h) for h in range(BH)] + [("mem", h) for h in range(MH)]

        view = {k: v.rearrange("(c p) n -> p c n", p=P) for k, v in w.items()}

        blk = ctx.enter_context(nc.Block())

        @blk.sync
        def _(sp):
            def load(s, src, per=0, i=None, width=1024):
                if s >= R:
                    sp.wait_ge(lo_ready, val(s - R + 1, per, i))
                dst = w_raw[:, s % R, 0:width]
                sp.dma_start(dst.rearrange("p (c n) -> p c n", c=src.shape[1]), src)\
                    .then_inc(w_landed[s % R], 16)

            def tile(s0, name, steps, n0, per=0, i=None, width=512, first=0):
                cols = slice(n0, n0 + width) if i is None else bass.ds(n0, width)
                for k in range(steps):
                    c = (first + 2 * k) % (2 * steps)
                    load(s0 + k, view[name][:, c:c + 2, cols], per, i, 2 * width)
                    if s0 + k == MEMA + R - 1:
                        for t in range(TT):
                            sp.dma_start(x[:, t, :], x_in[t * P:(t + 1) * P, :])\
                                .then_inc(x_landed[t], 16)

            for t in range(2):
                sp.dma_start(mem[:, t, :], mem_in[t * P:(t + 1) * P, :]).then_inc(mem_landed[t], 16)
            for j in range(2):
                tile(MEMA + j * DSTEPS, "a_w_mem_kv", DSTEPS, 512 * j)
            for j in range(2):
                tile(MEMB + j * DSTEPS, "b_w_mem_kv", DSTEPS, 512 * j)
            tile(QLAT, "a_w_in", DSTEPS, 0)
            for c in range(KC):
                load(KVLAT + c, view["a_w_in"][:, c:c + 1, LORA:LORA + KVW], width=KVW)
            tile(QMEM, "a_w_in", DSTEPS, 2 * LORA + RD)
            for j in range(6):
                tile(UQ + j * LSTEPS, "a_w_uq", LSTEPS, 384 * j, width=384)
            for j in range(6):
                tile(UKV + j * LSTEPS, "a_w_ukv", LSTEPS, 512 * j)
            with sp.Fori(0, 2) as i:
                for j in range(2):
                    tile(OA + j * DSTEPS, "a_w_o", DSTEPS, i * 1024 + 512 * j, 2 * DSTEPS, i)
            for layer, s_in, s_out in ((0, IN0, OUT0), (1, IN1, OUT1)):
                if layer == 1:
                    with sp.Fori(0, BH // 2) as i:
                        for j in range(2):
                            tile(SKV + j * DSTEPS, "shared_w_kv", DSTEPS, i * 1024 + 512 * j,
                                 2 * DSTEPS, i)
                    with sp.Fori(0, 2) as i:
                        for j in range(2):
                            tile(BQ + j * DSTEPS, "b_w_in", DSTEPS, i * 1024 + 512 * j,
                                 2 * DSTEPS, i)
                    for j in range(4):
                        tile(OB + j * DSTEPS, "b_w_o", DSTEPS, 512 * j, first=MEM_CHUNK)
                with sp.Fori(0, FJ) as i:
                    tile(s_in, f"ffn_w_in{layer}", DSTEPS, i * 512, 2 * DSTEPS, i)
                    tile(s_in + DSTEPS, f"ffn_w_in{layer}", DSTEPS, i * 512 + F, 2 * DSTEPS, i)
                with sp.Fori(0, 2) as i:
                    for j in range(2):
                        tile(s_out + j * FSTEPS, f"ffn_w_out{layer}", FSTEPS,
                             i * 1024 + 512 * j, 2 * FSTEPS, i)
            n = len(X_PIECES)
            for t in range(TT):
                for k, (a, z) in enumerate(X_PIECES):
                    sp.wait_ge(x_piece, 3 * TT * n + t * n + k + 1)
                    sp.dma_start(out[t * P:(t + 1) * P, a:z], x[:, t, a:z])\
                        .then_inc(out_stored, 16)
            sp.wait_ge(out_stored, 16 * TT * n)

        @blk.gpsimd
        def _(pool):
            nc.gpsimd.memset(eps[:, :], EPS).then_inc(eps_ready, 1)
            nc.gpsimd.memset(ident[:, :], 0.0).then_inc(pool_step, 1)
            nc.gpsimd.memset(ident_b[:, :], 0.0).then_inc(pool_step, 1)
            nc.gpsimd.memset(mask_b[:, :], 0.0).then_inc(pool_step, 1)
            pool.wait_ge(pool_step, 3)
            for t in (ident, ident_b):
                nc.gpsimd.affine_select(out=t[:, :], in_=t[:, :], compare_op=ALU.not_equal,
                                        fill=1.0, base=0, pattern=[[-1, P]], channel_multiplier=1)\
                    .then_inc(consts_ready, 1)
            nc.gpsimd.affine_select(out=mask_b[:, :], in_=mask_b[:, :], compare_op=ALU.is_ge,
                                    fill=NEG, base=0, pattern=[[-1, P]], channel_multiplier=1)\
                .then_inc(consts_ready, 1)
            pool.wait_ge(tr_copied, 3)
            pool.wait_ge(trig_ready, 1)
            pool.wait_ge(lam_prod, 1)
            pool.dma_start(gain_o[:, :], vec["a_post"].partition_broadcast(P))\
                .then_inc(gain_landed, 16)
            for k, (name, dst, step) in enumerate((("ffn_post0", gain_f, OUT0),
                                                   ("b_post", gain_o, OUT0),
                                                   ("ffn_post1", gain_f, OUT1))):
                if dst is gain_f:
                    pool.wait_ge(step_used, step)
                else:
                    pool.wait_ge(step_used, SKV)
                pool.dma_start(dst[:, :], vec[name].partition_broadcast(P)).then_inc(gain_landed, 16)

        @blk.tensor
        def _(pe):
            def release(tile_no, per=0, i=None):
                if tile_no >= 2:
                    pe.wait_ge(pair_act, val(tile_no - 1, per, i))
                    pe.wait_ge(pair_dve, val(tile_no - 1, per, i))

            def product(s0, steps, tile_no, xhi, xlo, parts, width=512, chunks=2, per=0, i=None,
                        per_t=0, first_chunk=0, late=(), after=None, hold=0):
                release(tile_no, per_t, i)
                pair = 2 * (tile_no % 2)
                held = range(steps - hold, steps)
                turns = [(k, parts) for k in range(steps - hold)]
                turns += [(k, [part]) for part in parts for k in held] if hold else []
                for k, parts_now in turns:
                    if k not in held or parts_now[0] is parts[0]:
                        pe.wait_ge(lo_ready, val(s0 + k + 1, per, i))
                    for step, semaphore, value in late:
                        if k == step:
                            pe.wait_ge(semaphore, value)
                    slot = (s0 + k) % R
                    for c in range(chunks):
                        wh = w_hi[:, slot, c * width:(c + 1) * width]
                        wl = w_lo[:, slot, c * width:(c + 1) * width]
                        n_ch = k * chunks + c
                        ch = (first_chunk + n_ch) % (steps * chunks)
                        seen = set()
                        for mode, bank, o0, on, tok, cols in parts_now:
                            rows = RD if bank >= 4 else P
                            dst = ps[0:rows, bank if bank >= 4 else pair + bank, o0:o0 + on]
                            first = n_ch == 0 and bank not in seen
                            seen.add(bank)
                            last = n_ch == steps * chunks - 1
                            a_hi, a_lo = xhi[:, ch, tok], xlo[:, ch, tok]
                            pairs = [(a_hi, cols(wh)), (a_hi, cols(wl)), (a_lo, cols(wh))]
                            if mode == "T":
                                pairs = [(b, a) for a, b in (pairs[0], pairs[2], pairs[1])]
                            for q, (st, mv) in enumerate(pairs):
                                mm = nc.tensor.matmul(dst, st, mv, start=first and q == 0,
                                                      stop=last and q == 2, skip_group_check=True)
                    if k not in held or parts_now[0] is parts[-1]:
                        mm.then_inc(step_used, 1)
                    elif k == steps - 1:
                        mm.then_inc(first_bank_done, 1)
                    if after:
                        after(k)

            whole = lambda n: (lambda a: a[:, 0:n])
            every = slice(0, S)
            tok_t = [slice(0, P), slice(P, S)]

            def n_parts(width=512):
                return [("N", t, 0, width, tok_t[t], whole(width)) for t in range(TT)]

            def t_parts():
                return [("T", k // 2, 256 * (k % 2), 256, every,
                         (lambda a, k=k: a[:, k * P:(k + 1) * P])) for k in range(4)]

            def kv_parts():
                ks = [("T", 0, 256 * h, 256, every,
                       (lambda a, h=h: a[:, 256 * h:256 * h + P])) for h in range(2)]
                pick = lambda a: a.rearrange("p (h n) -> p h n", h=2)[:, :, P:2 * P]
                return ks + [("N", 1, 256 * t, 256, tok_t[t], pick) for t in range(TT)]

            def uq_parts():
                return [("T", k // 2, 256 * (k % 2), 256, every,
                         (lambda a, k=k: a[:, k * P:(k + 1) * P])) for k in range(3)]

            done = {"C": 0, "N": 0}
            items_done = [0]

            def phase_free():
                if done["N"]:
                    pe.wait_ge(tr_lo, done["N"])
                if done["C"]:
                    pe.wait_ge(tr_copied, done["C"])
                if items_done[0]:
                    pe.wait_ge(o_lo, items_done[0])

            def norm_group(src, g, diag=diag, tiles=range(TT)):
                for c in range(2):
                    for t in tiles:
                        f0 = (2 * g + c) * P
                        mm = nc.tensor.matmul(ps[:, 4 + g % 4, 256 * c + P * t:256 * c + P * t + P],
                                              src[:, t, f0:f0 + P], diag[:, t, :],
                                              start=True, stop=True, skip_group_check=True)
                if TT - 1 in tiles:
                    mm.then_inc(tr_ready, 1)

            def norm_transpose(src, chunks, diag_no, diag=diag):
                phase_free()
                pe.wait_ge(diag_ready, diag_no)
                for g in range(chunks // 2):
                    if g >= 4:
                        pe.wait_ge(tr_lo, done["N"] + g - 3)
                    norm_group(src, g, diag)
                done["N"] += chunks // 2

            def norm_product(src, diag_no, *args):
                phase_free()
                if src is x:
                    for t in range(TT):
                        pe.wait_ge(diag_ready, diag_no + t)
                        for g in range(4):
                            norm_group(src, g, tiles=[t])
                else:
                    pe.wait_ge(diag_ready, diag_no)
                    for g in range(4):
                        norm_group(src, g)
                base_n = done["N"]
                late = [(k, tr_lo, base_n + k + 1) for k in range(DSTEPS)]
                product(*args, late=late, after=lambda k: k < 4 and norm_group(src, 4 + k))
                done["N"] += DSTEPS

            def rope_transpose(bank, blocks, rope_no):
                pe.wait_ge(rope_ready, rope_no)
                for k, src in enumerate(blocks):
                    mm = nc.tensor.transpose(ps[:, bank, P * k:P * (k + 1)], src, ident[:, :])
                mm.then_inc(tr_ready, 1)
                done["C"] += 1

            rot = scratch[:, 0].rearrange("p a b -> p (a b)")

            def unrotated_transpose(bank, buffer, rows, raw_no):
                pe.wait_ge(raw_ready, raw_no)
                for t in range(TT):
                    mm = nc.tensor.transpose(ps[:, bank, P * t:P * t + rows],
                                             pe_raw[0:rows, buffer, P * t:P * (t + 1)],
                                             ident[0:rows, 0:rows])
                mm.then_inc(unrotated, 1)

            def attend(items, km, vm, first_item, tiles_before):
                phase_free()
                pe.wait_ge(pair_act, tiles_before)
                pe.wait_ge(pair_dve, tiles_before)
                t0 = first_item

                def scores(t):
                    kind, h = items[t]
                    lag = 2 if is_b else 4
                    if t >= lag:
                        pe.wait_ge(e_ready, t0 + t - lag + 1)
                    if kind == "mem":
                        b = 2 * (t % 2) if is_b else t % 4
                        for q in range(TT):
                            mm = nc.tensor.matmul(ps[:, b, 256 * q:256 * q + M],
                                                  qm[:, h, q * P:(q + 1) * P], km[:, h, :],
                                                  start=q == 0, stop=True, skip_group_check=True)
                    else:
                        for j in range(2 if kind == "diff" else 1):
                            b = 2 * (t % 2) + j if is_b else t % 4
                            for q in range(TT):
                                dst = ps[:, b, P * q:P * q + (q + 1) * P]
                                n = (q + 1) * P
                                if kind == "diff":
                                    g = 2 * h + j
                                    nc.tensor.matmul(dst, qT_b[:, g, q * P:(q + 1) * P],
                                                     kT_b[:, g, 0:n], start=q == 0, stop=False,
                                                     skip_group_check=True)
                                else:
                                    nc.tensor.matmul(dst, qnT[:, h, q * P:(q + 1) * P],
                                                     kT_a[:, h, 0:n], start=q == 0, stop=False,
                                                     skip_group_check=True)
                                    r0 = RD * (h % 2)
                                    nc.tensor.matmul(dst, qpT[r0:r0 + RD, h // 2, q * P:(q + 1) * P],
                                                     kpT[r0:r0 + RD, 0:n], start=False, stop=False,
                                                     skip_group_check=True)
                                mm = nc.tensor.matmul(ps[:, b, P * 2 * q:P * 2 * q + P],
                                                      ident_b[:, :], mask_b[:, :], start=False,
                                                      stop=True, skip_group_check=True)
                    mm.then_inc(s_ready, 1)

                def transposes(t):
                    kind, h = items[t]
                    pe.wait_ge(p_ready, t0 + t + 1)
                    if t >= 2:
                        pe.wait_ge(pT_copied, t0 + t - 1)
                    src = probs[:, t % 2, 0, :]
                    dst = ps[:, 4 + t % 2, :]
                    if kind == "mem":
                        moves = [(256 * q + P * k, 256 * k + P * q) for q in range(2) for k in range(2)]
                    else:
                        moves = [(0, 0), (P, P), (2 * P, 2 * P)]
                    for a, b in moves:
                        mm = nc.tensor.transpose(dst[:, b:b + P], src[:, a:a + P], ident[:, :])
                    mm.then_inc(pT_ready, 1)

                def outputs(t):
                    kind, h = items[t]
                    pe.wait_ge(pT_copied, t0 + t + 1)
                    if t >= 2:
                        pe.wait_ge(o_lo, t0 + t - 1)
                    p = pT[:, t % 2, :]
                    dst = ps[:, 6 + t % 2, :]
                    if kind == "mem":
                        for k in range(2):
                            mm = nc.tensor.matmul(dst[:, 0:S], vm[:, k, h, :],
                                                  p[:, 256 * k:256 * k + S], start=k == 0, stop=k == 1)
                    elif kind == "mla":
                        nc.tensor.matmul(dst[:, 0:S], v_a[:, 0, h, :], p[:, 0:S], start=True,
                                         stop=False, skip_group_check=True)
                        mm = nc.tensor.matmul(dst[:, P:S], v_a[:, 1, h, :], p[:, 2 * P:3 * P],
                                              start=False, stop=True, skip_group_check=True)
                    else:
                        nc.tensor.matmul(dst[:, 0:VD], p[:, 0:P], v_b[:, 0, h, :], start=True,
                                         stop=True, skip_group_check=True)
                        nc.tensor.matmul(dst[:, VD:2 * VD], p[:, P:2 * P], v_b[:, 0, h, :],
                                         start=False, stop=False, skip_group_check=True)
                        mm = nc.tensor.matmul(dst[:, VD:2 * VD], p[:, 2 * P:3 * P], v_b[:, 1, h, :],
                                              start=False, stop=True, skip_group_check=True)
                    mm.then_inc(o_ready, 1)

                is_b = first_item > 0
                qm = qmT_b if is_b else qmT_a
                n = len(items)
                lead = 2 if is_b else 3
                for t in range(lead):
                    scores(t)
                for t in range(n + 1):
                    if t + lead < n:
                        scores(t + lead)
                    if t < n:
                        transposes(t)
                    if t >= 1:
                        outputs(t - 1)
                items_done[0] += n

            pe.wait_ge(small_landed, 16 * N_SMALL)
            pe.wait_ge(consts_ready, 3)
            nc.tensor.transpose(ps[:, 4, 0:N_GAIN], gain_rows[0:N_GAIN, :],
                                ident[0:N_GAIN, 0:N_GAIN]).then_inc(tr_ready, 1)
            for layer in range(2):
                for k in range(4):
                    mm = nc.tensor.transpose(ps[:, 5 + layer, 88 * k:88 * (k + 1)],
                                             conv_rows[:, layer, k, :], ident[0:2 * FC, 0:2 * FC])
                mm.then_inc(tr_ready, 1)
            done["C"] = 3

            norm_product(mem, 1, MEMA, DSTEPS, MEMA_T, mTa_hi, mTa_lo, kv_parts())
            product(MEMA + DSTEPS, DSTEPS, MEMA_T + 1, mTa_hi, mTa_lo, kv_parts())
            product(MEMB, DSTEPS, MEMB_T, mTb_hi, mTb_lo, kv_parts())
            phase_free()
            pe.wait_ge(diag_ready, 2)
            base_n = done["N"]

            def x_group(g):
                if g >= 4:
                    pe.wait_ge(tr_lo, base_n + g - 3)
                norm_group(x, g)

            product(MEMB + DSTEPS, DSTEPS, MEMB_T + 1, mTb_hi, mTb_lo, kv_parts(), after=x_group)
            done["N"] += DSTEPS
            product(QLAT, DSTEPS, QLAT_T, xT_hi, xT_lo, n_parts(),
                    late=[(k, tr_lo, base_n + k + 1) for k in range(DSTEPS)])
            kpe_parts = [("T", 7, 0, 256, every, (lambda a: a[:, LORA:KVW]))]
            product(KVLAT, KC, KVLAT_T, xT_hi, xT_lo, n_parts() + kpe_parts, width=KVW, chunks=1)
            norm_transpose(lat[:, 0], 4, 3)
            product(QMEM, DSTEPS, QMEM_T, xT_hi, xT_lo, t_parts(),
                    after=lambda k: k == 1 and unrotated_transpose(6, 0, RD, 1))
            norm_transpose(lat[:, 1], 4, 4, diag_kv)
            rope_transpose(6, [rot[:, P * t:P * (t + 1)] for t in range(TT)], 1)
            qpe_blocks = [rot[:, P * t:P * (t + 1)] for t in range(TT)]
            for j in range(6):
                product(UQ + j * LSTEPS, LSTEPS, UQ_T + j, latq_hi, latq_lo, uq_parts(), width=384,
                        after=lambda k: k == 0 and j > 0 and
                        unrotated_transpose(7, (j - 1) % 2, P, 1 + j))
                if j == 0:
                    phase_free()
                else:
                    if j >= 3:
                        pe.wait_ge(tr_copied, groups_before(T_QPE, "C") + j - 2)
                    rope_transpose(4 + (j - 1) % 2, qpe_blocks, 1 + j)
            for j in range(6):
                product(UKV + j * LSTEPS, LSTEPS, UKV_T + j, latk_hi, latk_lo, kv_parts(),
                        after=lambda k: k == 0 and j == 0 and unrotated_transpose(7, 1, P, 7))
                if j == 0:
                    pe.wait_ge(tr_copied, groups_before(T_QPE, "C") + 4)
                    rope_transpose(5, qpe_blocks, 7)
            pe.wait_ge(tr_lo, done["N"])
            attend(ITEMS_A, kmT_a, vm_a, 0, OA_T)

            def wide_product(s0, t0, steps, xhi, xlo, late=(), first_chunk=0):
                with pe.Fori(0, 2) as i:
                    for j in range(2):
                        product(s0 + j * steps, steps, t0 + j, xhi, xlo, n_parts(),
                                per=2 * steps, i=i, per_t=2, late=late if j == 0 else (),
                                first_chunk=first_chunk, hold=HOLD if j == 1 else 0)

            h_count = [0]

            def ffn(s_in, t_in, s_out, t_out, diag_no):
                tiles = lambda j, **kw: product(s_in + j * DSTEPS, DSTEPS, t_in + j, xT_hi, xT_lo,
                                                t_parts(), **kw)
                norm_product(x, diag_no, s_in, DSTEPS, t_in, xT_hi, xT_lo, t_parts())
                with pe.Fori(0, FJ - 1) as i:
                    for j in (1, 2):
                        tiles(j, per=2 * DSTEPS, i=i, per_t=2)
                tiles(2 * FJ - 1)
                h_count[0] += FJ
                pe.wait_ge(h_lo, h_count[0] - 1)
                wide_product(s_out, t_out, FSTEPS, hT_hi, hT_lo, [(FSTEPS - 2, h_lo, h_count[0])])

            pe.wait_ge(o_lo, items_done[0] - 2)
            wide_product(OA, OA_T, DSTEPS, xT_hi, xT_lo, [(DSTEPS - 1, o_lo, items_done[0])])
            ffn(IN0, IN0_T, OUT0, OUT0_T, 5)

            kb_blocks = [rot[:, 512 * t + P * g:512 * t + P * (g + 1)]
                         for g in range(2) for t in range(TT)]
            skv_tile = lambda j, **kw: product(SKV + j * DSTEPS, DSTEPS, SKV_T + j, xT_hi, xT_lo,
                                               n_parts(), **kw)
            c0 = groups_before(T_KB, "C")
            norm_product(x, 7, SKV, DSTEPS, SKV_T, xT_hi, xT_lo, n_parts())
            for j in range(1, BH):
                skv_tile(j)
                if j >= 3:
                    pe.wait_ge(tr_copied, c0 + j - 2)
                rope_transpose(4 + (j - 1) % 2, kb_blocks, 7 + j)
            qb_blocks = [[rot[:, 512 * t + P * g:512 * t + P * (g + 1)]
                          for g in (2 * q, 2 * q + 1) for t in range(TT)] for q in range(2)]
            c1 = groups_before(T_QB, "C")
            for j in range(3):
                product(BQ + j * DSTEPS, DSTEPS, BQ_T + j, xbT_hi, xbT_lo, n_parts())
                if j == 0:
                    pe.wait_ge(tr_copied, c0 + 4)
                    rope_transpose(5, kb_blocks, 13)
                else:
                    pe.wait_ge(tr_copied, c1 + 2 * (j - 1))
                    for q in range(2):
                        rope_transpose(6 + q, qb_blocks[q], 13 + j)
            product(BQ + 3 * DSTEPS, DSTEPS, BQ_T + 3, xbT_hi, xbT_lo, t_parts())
            pe.wait_ge(tr_copied, c1 + 4)
            for q in range(2):
                rope_transpose(6 + q, qb_blocks[q], 16)
            attend(ITEMS_B, kmT_b, vm_b, len(ITEMS_A), OB_T)
            base_n = done["N"]
            for h in range(BH):
                if h == 4:
                    pe.wait_ge(o_lo, items_done[0])
                pe.wait_ge(on_scaled, h + 1)
                for c in range(2):
                    for t in range(TT):
                        o0 = 256 * c + P * t
                        mm = nc.tensor.transpose(ps[:, SUB_BANKS[h], o0:o0 + P],
                                                 o_nat[:, h, t, P * c:P * (c + 1)], ident[:, :])
                mm.then_inc(tr_ready, 1)
            done["N"] += BH
            wide_product(OB, OB_T, DSTEPS, xT_hi, xT_lo,
                         [(MH // 2 + h, tr_lo, base_n + h + 1) for h in range(BH)], MEM_CHUNK)
            ffn(IN1, IN1_T, OUT1, OUT1_T, 9)

        @blk.scalar
        def _(act):
            act.dma_start(gain_rows[0:N_GAIN, :], vec["gains"]).then_inc(small_landed, 16)
            act.dma_start(conv_rows[:, :, :, :].rearrange("c l j p -> c (l j p)"), vec["conv"])\
                .then_inc(small_landed, 16)
            act.dma_start(lam_rows[:, :, :].rearrange("p k n -> p (k n)"),
                          vec["lambda"].partition_broadcast(P)).then_inc(rope_landed, 16)
            act.dma_start(freq[:, :], inv_freq.partition_broadcast(P)).then_inc(rope_landed, 16)
            for t in range(TT):
                act.dma_start(pos_i[:, t:t + 1],
                              positions[t * P:(t + 1) * P].rearrange("(p a) -> p a", a=1))\
                    .then_inc(rope_landed, 16)

            n_split = [0]
            count = {"tr": 0, "std": 0, "held": 0}

            def split(s, per=0, i=None):
                width = 1024
                if i is None and KVLAT <= s < QMEM:
                    width = KVW
                act.wait_ge(w_landed[s % R], val(16 * (s // R + 1), 16 * per // R, i))
                if s >= R:
                    act.wait_ge(step_used, val(s - R + 1, per, i))
                if i is None and UQ <= s < UKV:
                    for rotary in (False, True):
                        a = nc.scalar.activation(uq_columns(w_hi, s, rotary, True),
                                                 uq_columns(w_raw, s, rotary, False), ACT.Copy)
                    a.then_inc(hi_ready, 1)
                    return
                nc.scalar.activation(w_hi[:, s % R, 0:width], w_raw[:, s % R, 0:width], ACT.Copy)\
                    .then_inc(hi_ready, 1)

            def splits_to(s):
                for k in range(n_split[0], min(s, STEPS)):
                    split(k)
                n_split[0] = max(n_split[0], min(s, STEPS))

            def root(width, t0=0, t1=TT):
                count["std"] += 1
                act.wait_ge(ss_ready, count["std"])
                nc.scalar.activation(nrm[:, 2 + t0:2 + t1], nrm[:, t0:t1], ACT.Sqrt,
                                     bias=eps[:, :], scale=1.0 / width).then_inc(std_ready, 1)

            squared = scratch[:, :, :, :].rearrange("p a b c -> p (a b c)").bitcast(BF16)
            unused = lambda k, n: squared[:, 1024 * k:1024 * k + n]

            def squares(pieces):
                for k, (src, col) in enumerate(pieces):
                    a = nc.scalar.activation(unused(2 * k, src.free_size()), src, ACT.Square,
                                             accum_out=col)
                a.then_inc(sq_ready, 1)

            def split_transposes(chunks, targets, following=None, start=3):
                for g in range(chunks // 2):
                    count["tr"] += 1
                    act.wait_ge(tr_ready, count["tr"])
                    for g0, hi in targets:
                        for c in range(2):
                            ch = 2 * g + c
                            a = nc.scalar.activation(hi[:, ch, :], ps[:, 4 + g % 4, 256 * c:256 * c + S],
                                                     ACT.Copy, scale=gcol[:, g0 + ch:g0 + ch + 1])
                    a.then_inc(tr_hi, 1)
                    if following is not None and g >= start:
                        splits_to(following + min(g + 1, CUT))

            def copy_transposed(dst, bank):
                count["tr"] += 1
                act.wait_ge(tr_ready, count["tr"])
                nc.scalar.activation(dst, ps[:, bank, 0:dst.free_size()], ACT.Copy)\
                    .then_inc(tr_copied, 1)

            def load_table(func):
                nc.scalar.activation(nrm[:, 6:7], eps[:, :], func)

            act.wait_ge(eps_ready, 1)
            load_table(ACT.Sqrt)
            for t in range(2):
                act.wait_ge(mem_landed[t], 16)
                a = nc.scalar.activation(unused(t, 1024), mem[:, t, 0:1024], ACT.Square,
                                         accum_out=ssp[:, t, 0:1])
            a.then_inc(sq_ready, 1)
            root(D)
            copy_transposed(gcol[:, 0:N_GAIN], 4)
            for layer in range(2):
                copy_transposed(conv[:, layer].rearrange("p j c -> p (j c)"), 5 + layer)
            splits_to(MEMA + AHEAD)
            split_transposes(KC, [(GAIN_ROWS["a_mem"], mTa_hi), (GAIN_ROWS["b_mem"], mTb_hi)], MEMA)

            def kv_epilogue(t, kT, heads, s_end):
                act.wait_ge(step_used, s_end)
                nc.scalar.activation(kT[:, heads, :].rearrange("p h s -> p (h s)"),
                                     ps[:, 2 * (t % 2), :], ACT.Copy).then_inc(pair_act, 1)

            splits_to(MEMA + DSTEPS + AHEAD)
            kv_epilogue(MEMA_T, kmT_a, slice(0, 2), MEMA + DSTEPS)
            splits_to(MEMA + DSTEPS + AHEAD + 2)
            act.wait_ge(range_ready, 1)
            nc.scalar.activation(cosine[:, :, :], rope_k[:, 0], ACT.Sin)
            nc.scalar.activation(sine[:, :, :], rope_k[:, 1], ACT.Sin).then_inc(trig_ready, 1)
            splits_to(MEMA + DSTEPS + AHEAD + 4)
            act.wait_ge(lam_prod, 1)
            nc.scalar.activation(neglam[:, 2:4], neglam[:, 0:2], ACT.Exp).then_inc(lam_exp, 1)
            splits_to(MEMB + AHEAD)
            kv_epilogue(MEMA_T + 1, kmT_a, slice(2, 4), MEMB)
            for t in range(TT):
                act.wait_ge(x_landed[t], 16)
            squares([(x[:, t, :], ssp[:, t, 0:1]) for t in range(TT)])
            splits_to(MEMB + AHEAD + 3)
            root(D)
            splits_to(MEMB + DSTEPS + AHEAD)
            kv_epilogue(MEMB_T, kmT_b, slice(0, 2), MEMB + DSTEPS)
            split_transposes(KC, [(GAIN_ROWS["a_pre"], xT_hi)], MEMB + DSTEPS + AHEAD, 0)
            splits_to(QLAT + AHEAD)
            kv_epilogue(MEMB_T + 1, kmT_b, slice(2, 4), QLAT)

            def latent_epilogue(k, t, s_end):
                act.wait_ge(step_used, s_end)
                pr = 2 * (t % 2)
                nc.scalar.activation(lat[:, k, 0, :], ps[:, pr, :], ACT.Copy).then_inc(pair_act, 1)
                act.wait_ge(pair_act, t + 1)
                act.wait_ge(pair_dve, t + 1)
                squares([(lat[:, k, u, :], ssp[:, u, 0:1]) for u in range(TT)])
                root(LORA)

            def to_turn(dst, src):
                return nc.scalar.activation(dst, src, ACT.Copy).then_inc(raw_ready, 1)

            def raw_epilogue(t, width, s_end):
                act.wait_ge(step_used, s_end)
                pr = 2 * (t % 2)
                nc.scalar.activation(rawv[:, :, 0:width], ps[:, pr:pr + 2, 0:width], ACT.Copy)\
                    .then_inc(pair_act, 1)

            rawv = scratch[:, 0].rearrange("p a b -> p (a b)").rearrange("p (t n) -> p t n", t=TT)

            splits_to(KVLAT + AHEAD)
            latent_epilogue(0, QLAT_T, KVLAT)
            splits_to(QMEM + AHEAD)
            latent_epilogue(1, KVLAT_T, QMEM)
            to_turn(pe_raw[0:RD, 0, :], ps[0:RD, 7, 0:S])
            split_transposes(4, [(GAIN_ROWS["q_norm"], latq_hi)])
            splits_to(UQ + AHEAD)
            act.wait_ge(step_used, UQ)
            nc.scalar.activation(qmT_a[:, 0:2, :].rearrange("p h s -> p (h s)"),
                                 ps[:, 2 * (QMEM_T % 2), :], ACT.Copy).then_inc(pair_act, 1)
            split_transposes(4, [(GAIN_ROWS["kv_norm"], latk_hi)])
            copy_transposed(kpT[:, :], 6)
            for j in range(6):
                splits_to(UQ + (j + 1) * LSTEPS + AHEAD)
                if j:
                    copy_transposed(qpT[:, j - 1, :], 4 + (j - 1) % 2)
                act.wait_ge(step_used, UQ + (j + 1) * LSTEPS)
                pr = 2 * ((UQ_T + j) % 2)
                if j != 1:
                    act.wait_ge(unrotated, max(j, 1))
                to_turn(pe_raw[:, j % 2, :], ps[:, pr + 1, 0:S])
                nc.scalar.activation(qnT[:, 2 * j:2 * j + 2, :].rearrange("p h s -> p (h s)"),
                                     ps[:, pr, :], ACT.Copy).then_inc(pair_act, 1)
            for j in range(6):
                splits_to(UKV + (j + 1) * LSTEPS + AHEAD)
                if j == 0:
                    copy_transposed(qpT[:, 5, :], 5)
                kv_epilogue(UKV_T + j, kT_a, slice(2 * j, 2 * j + 2), UKV + (j + 1) * LSTEPS)

            def attend(items, first_item, scale):
                t0 = first_item
                is_b = first_item > 0

                def exps(t):
                    kind, h = items[t]
                    act.wait_ge(max_ready, t0 + t + 1)
                    if t >= 2:
                        act.wait_ge(pT_ready, t0 + t - 1)
                    sc = scale if kind != "mem" else SCALE_B
                    for j in range(2 if kind == "diff" else 1):
                        b = 2 * (t % 2) + j if is_b else t % 4
                        cuts = ((0, 256), (256, 512)) if kind == "mem" else ((0, P), (P, 3 * P))
                        for q, (a, z) in enumerate(cuts):
                            e = nc.scalar.activation(
                                probs[:, t % 2, j, a:z], ps[:, b, a:z], ACT.Exp, scale=sc,
                                bias=stat[:, t % 4, 2 * j + q:2 * j + q + 1],
                                accum_out=sums[:, t % 4, 2 * j + q:2 * j + q + 1])
                    e.then_inc(e_ready, 1)

                def copy_pT(t):
                    kind, h = items[t]
                    act.wait_ge(pT_ready, t0 + t + 1)
                    if t >= 2:
                        act.wait_ge(o_ready, t0 + t - 1)
                    n = 512 if kind == "mem" else 3 * P
                    nc.scalar.activation(pT[:, t % 2, 0:n], ps[:, 4 + t % 2, 0:n], ACT.Copy)\
                        .then_inc(pT_copied, 1)

                def output(t):
                    kind, h = items[t]
                    act.wait_ge(o_ready, t0 + t + 1)
                    src = ps[:, 6 + t % 2, :]
                    if kind == "diff":
                        for q in range(TT):
                            a = nc.scalar.activation(
                                unused(2 * (t % 2) + q, VD), src[:, VD * q:VD * (q + 1)], ACT.Square,
                                scale=inv_sum[:, h, q:q + 1],
                                accum_out=osum[:, 0, 2 * h + q:2 * h + q + 1])
                        a.then_inc(o_hi, 1)
                    else:
                        ch = h if kind == "mla" else 12 + h
                        nc.scalar.activation(xT_hi[:, ch, :], src[:, 0:S], ACT.Copy).then_inc(o_hi, 1)

                for t in range(len(items) + 2):
                    if t < len(items):
                        exps(t)
                    if 1 <= t <= len(items):
                        copy_pT(t - 1)
                    if t >= 2:
                        output(t - 2)
                    if is_b and t == len(items) - 1:
                        act.wait_ge(o_hi, t0 + BH)
                        nc.scalar.activation(osum[:, 1, :], osum[:, 0, :], ACT.Sqrt, bias=eps[:, :],
                                             scale=1.0 / VD).then_inc(ostd_ready, 1)

            sums = stat[:, :, 4:8]
            load_table(ACT.Exp)
            attend(ITEMS_A, 0, SCALE_A)

            pieces = [0]

            def wide_epilogue(s0, t0, steps, last=False):
                end = s0 + 4 * steps
                load_table(ACT.Sqrt)
                for j in range(3):
                    splits_to(s0 + (j + 1) * steps + AHEAD)
                    act.wait_ge(step_used, s0 + (j + 1) * steps)
                    for u in range(TT):
                        a = nc.scalar.activation(
                            unused(2 * (j % 2) + u, 512), ps[:, 2 * ((t0 + j) % 2) + u, :],
                            ACT.Square, accum_out=ssp[:, u, j:j + 1])
                    a.then_inc(pair_act, 1)
                splits_to(end)

                def last_tile(t):
                    return nc.scalar.activation(squared[:, 512 * t:512 * (t + 1)],
                                                ps[:, 2 * ((t0 + 3) % 2) + t, :],
                                                ACT.Square, accum_out=ssp[:, t, 3:4])

                def updated(t):
                    for k, (a, z) in enumerate(X_PIECES):
                        pieces[0] += 1
                        act.wait_ge(x_piece, pieces[0])
                        ins = nc.scalar.activation(unused(1 + k, z - a), x[:, t, a:z], ACT.Square,
                                                   accum_out=ssp[:, t, k:k + 1])
                    ins.then_inc(sq_ready, 1)

                count["held"] += 2
                act.wait_ge(first_bank_done, count["held"])
                last_tile(0).then_inc(bank_squared, 1)
                root(D, 0, 1)
                if not last:
                    splits_to(end + 1)
                    updated(0)
                act.wait_ge(step_used, end)
                last_tile(1).then_inc(pair_act, 1)
                if not last:
                    root(D, 0, 1)
                root(D, 1, 2)
                if not last:
                    splits_to(end + 2)
                    updated(1)
                    root(D, 1, 2)
                    splits_to(end + AHEAD)

            def ffn_epilogues(layer, s_in, t_in, g_count):
                splits_to(s_in + CUT)

                def first_tap(i, j):
                    act.wait_ge(step_used, val(s_in + (j + 1) * DSTEPS, 2 * DSTEPS, i))
                    for m4 in range(4):
                        ch = i * 4 + (m4 + j * FC)
                        a = nc.scalar.activation(
                            scratch[:, j, m4, :],
                            ps[:, 2 * ((t_in + j) % 2) + m4 // 2, 256 * (m4 % 2):256 * (m4 % 2) + S],
                            ACT.Identity, scale=conv[:, layer, 2, bass.ds(ch, 1)],
                            bias=conv[:, layer, 3, bass.ds(ch, 1)])
                    a.then_inc(pair_act, 1)

                def gate(i):
                    act.wait_ge(pair_dve, val(t_in + 1, 2, i))
                    nc.scalar.activation(scratch[:, 0], scratch[:, 0],
                                         ACT.Gelu_apprx_tanh).then_inc(gate_ready, 1)

                def hi_half(i):
                    act.wait_ge(h_ready, val(g_count + 1, 1, i))
                    nc.scalar.activation(hT_hi[:, bass.ds(i * 4, 4), :], scratch[:, 1],
                                         ACT.Copy).then_inc(h_hi, 1)

                with act.Fori(0, FJ) as i:
                    for j in range(2):
                        for k in range(DSTEPS):
                            split(s_in + j * DSTEPS + k + CUT, 2 * DSTEPS, i)
                            ahead = k + CUT + 1 - DSTEPS
                            if ahead == 3:
                                first_tap(i, j)
                            if ahead == 5 and j == 0:
                                gate(i)
                            if ahead == 6 and j == 1:
                                hi_half(i)
                n_split[0] = s_in + 2 * FJ * DSTEPS + CUT

            wide_epilogue(OA, OA_T, DSTEPS)
            split_transposes(KC, [(GAIN_ROWS["ffn_pre"], xT_hi)], IN0)
            ffn_epilogues(0, IN0, IN0_T, 0)
            wide_epilogue(OUT0, OUT0_T, FSTEPS)
            split_transposes(KC, [(GAIN_ROWS["shared"], xT_hi), (GAIN_ROWS["b_pre"], xbT_hi)], SKV)
            for j in range(BH):
                splits_to(SKV + (j + 1) * DSTEPS + AHEAD)
                if j:
                    copy_transposed(kT_b[:, 2 * j - 2:2 * j, :].rearrange("p h s -> p (h s)"),
                                    4 + (j - 1) % 2)
                raw_epilogue(SKV_T + j, 256, SKV + (j + 1) * DSTEPS)
            for j in range(3):
                splits_to(BQ + (j + 1) * DSTEPS + AHEAD)
                if j == 0:
                    copy_transposed(kT_b[:, 10:12, :].rearrange("p h s -> p (h s)"), 5)
                else:
                    for q in range(2):
                        h0 = 4 * (j - 1) + 2 * q
                        copy_transposed(qT_b[:, h0:h0 + 2, :].rearrange("p h s -> p (h s)"), 6 + q)
                raw_epilogue(BQ_T + j, 512, BQ + (j + 1) * DSTEPS)
            splits_to(OB + AHEAD)
            act.wait_ge(step_used, OB)
            nc.scalar.activation(qmT_b[:, 0:2, :].rearrange("p h s -> p (h s)"),
                                 ps[:, 2 * ((BQ_T + 3) % 2), :], ACT.Copy).then_inc(pair_act, 1)
            for q in range(2):
                copy_transposed(qT_b[:, 8 + 2 * q:10 + 2 * q, :].rearrange("p h s -> p (h s)"), 6 + q)
            load_table(ACT.Exp)
            attend(ITEMS_B, len(ITEMS_A), SCALE_B)
            for h in range(BH):
                count["tr"] += 1
                act.wait_ge(tr_ready, count["tr"])
                for c in range(2):
                    g0 = GAIN_ROWS["subln"] + c
                    a = nc.scalar.activation(xT_hi[:, 2 * h + c, :],
                                             ps[:, SUB_BANKS[h], 256 * c:256 * c + S], ACT.Copy, scale=gcol[:, g0:g0 + 1])
                a.then_inc(tr_hi, 1)
            wide_epilogue(OB, OB_T, DSTEPS)
            split_transposes(KC, [(GAIN_ROWS["ffn_pre"] + KC, xT_hi)], IN1)
            ffn_epilogues(1, IN1, IN1_T, FJ)
            wide_epilogue(OUT1, OUT1_T, FSTEPS, last=True)

        @blk.vector
        def _(dve):
            linked = [0]

            def link(ins, base=0):
                linked[0] += 1
                ins.then_inc(dve_link, 1)
                dve.wait_ge(dve_link, base + linked[0])

            n_split = [0]
            count = {"N": 0, "sq": 0, "std": 0, "gain": 0, "bank": 0}

            def split(s, per=0, i=None):
                width = 1024
                if i is None and KVLAT <= s < QMEM:
                    width = KVW
                dve.wait_ge(hi_ready, val(s + 1, per, i))
                if i is None and UQ <= s < UKV:
                    for rotary in (False, True):
                        d = nc.vector.tensor_tensor(
                            uq_columns(w_lo, s, rotary, True), uq_columns(w_raw, s, rotary, False),
                            uq_columns(w_hi, s, rotary, True).bitcast(F32), ALU.subtract)
                    d.then_inc(lo_ready, 1)
                    return
                nc.vector.tensor_tensor(w_lo[:, s % R, 0:width], w_raw[:, s % R, 0:width],
                                        w_hi[:, s % R, 0:width].bitcast(F32), ALU.subtract)\
                    .then_inc(lo_ready, 1)

            def splits_to(s):
                for k in range(n_split[0], min(s, STEPS)):
                    split(k)
                n_split[0] = max(n_split[0], min(s, STEPS))

            def sums(parts, t0=0, t1=TT):
                nc.vector.reduce_sum(nrm[:, t0:t1], ssp[:, t0:t1, 0:parts], axis=AX)\
                    .then_inc(ss_ready, 1)

            def inverse_std(t0=0, t1=TT):
                count["std"] += 1
                dve.wait_ge(std_ready, count["std"])
                link(nc.vector.reciprocal(nrm[:, 4 + t0:4 + t1], nrm[:, 2 + t0:2 + t1]))

            def diagonal(dst, tiles=range(TT)):
                for t in tiles:
                    d = nc.vector.tensor_scalar(dst[:, t, :], ident[:, :], nrm[:, 4 + t:5 + t], None,
                                                ALU.mult)
                d.then_inc(diag_ready, 1)

            def norm(parts, dst=diag):
                count["sq"] += 1
                dve.wait_ge(sq_ready, count["sq"])
                sums(parts)
                inverse_std()
                diagonal(dst)

            def split_transposes(chunks, targets, following=None, start=3):
                for g in range(chunks // 2):
                    count["N"] += 1
                    dve.wait_ge(tr_hi, count["N"])
                    for g0, hi, lo in targets:
                        for c in range(2):
                            ch = 2 * g + c
                            d = nc.vector.scalar_tensor_tensor(
                                out=lo[:, ch, :], in0=ps[:, 4 + g % 4, 256 * c:256 * c + S],
                                scalar=gcol[:, g0 + ch:g0 + ch + 1], in1=hi[:, ch, :].bitcast(F32),
                                op0=ALU.mult, op1=ALU.subtract)
                    d.then_inc(tr_lo, 1)
                    if following is not None and g >= start:
                        splits_to(following + min(g + 1, CUT))

            def angles_and_lambda():
                dve.wait_ge(rope_landed, 16 * N_ROPE)
                link(nc.vector.tensor_copy(pos_f[:, :], pos_i[:, :]))
                for t in range(TT):
                    d = nc.vector.tensor_scalar(angle[:, t, :], freq[:, :], pos_f[:, t:t + 1], None,
                                                ALU.mult)
                link(d)
                for k, quarter in ((0, 0.25), (1, 0.0)):
                    d = nc.vector.tensor_scalar(turns[:, k], angle[:, :, :], 1.0 / (2 * math.pi), quarter,
                                                ALU.mult, ALU.add)
                link(d)
                link(nc.vector.tensor_scalar(turns[:, :], turns[:, :], ROUND, ROUND, ALU.add,
                                             ALU.subtract))
                for k in range(2):
                    d = nc.vector.scalar_tensor_tensor(
                        out=rope_k[:, k], in0=turns[:, k], scalar=-TWO_PI[0], in1=angle[:, :, :],
                        op0=ALU.mult, op1=ALU.add)
                link(d)
                for part in TWO_PI[1:]:
                    link(nc.vector.scalar_tensor_tensor(
                        out=rope_k[:, :], in0=turns[:, :], scalar=-part, in1=rope_k[:, :],
                        op0=ALU.mult, op1=ALU.add))
                link(nc.vector.tensor_scalar_add(rope_k[:, 0], rope_k[:, 0], math.pi / 2))
                nc.vector.tensor_scalar(rope_k[:, :], rope_k[:, :], SIN_MAX, -SIN_MAX, ALU.min, ALU.max)\
                    .then_inc(range_ready, 1)
                lr = lam_rows[:, :, :].rearrange("p (a b) n -> p a b n", a=2)
                link(nc.vector.tensor_tensor(lr[:, :, 0, :], lr[:, :, 0, :], lr[:, :, 1, :], ALU.mult))
                nc.vector.reduce_sum(neglam[:, 0:2], lr[:, :, 0, :], axis=AX).then_inc(lam_prod, 1)

            squared = scratch[:, 1].rearrange("p a b -> p (a b)").bitcast(BF16)
            for t in range(2):
                dve.wait_ge(mem_landed[t], 16)
                nc.vector.tensor_tensor_reduce(
                    out=squared[:, 1024 * t:1024 * (t + 1)], in0=mem[:, t, 1024:2048],
                    in1=mem[:, t, 1024:2048], scale=1.0, scalar=0.0, op0=ALU.mult, op1=ALU.add,
                    accum_out=ssp[:, t, 1:2]).then_inc(sq_dve, 1)
            dve.wait_ge(sq_dve, 2)
            dve.wait_ge(consts_ready, 3)
            norm(2)
            splits_to(MEMA + AHEAD)
            dve.wait_ge(tr_copied, 3)
            g0 = GAIN_ROWS["subln"]
            link(nc.vector.tensor_scalar(gcol[:, g0:g0 + 2], gcol[:, g0:g0 + 2], 1.0 - LAMBDA_INIT,
                                         None, ALU.mult))
            split_transposes(KC, [(GAIN_ROWS["a_mem"], mTa_hi, mTa_lo),
                                  (GAIN_ROWS["b_mem"], mTb_hi, mTb_lo)], MEMA)

            def v_epilogue(t, v, heads, s_end):
                dve.wait_ge(step_used, s_end)
                nc.vector.tensor_copy(v[:, :, heads, :].rearrange("p t h n -> p t (h n)"),
                                      ps[:, 2 * (t % 2) + 1, :].rearrange("p (t n) -> p t n", t=2))\
                    .then_inc(pair_dve, 1)

            splits_to(MEMA + DSTEPS + AHEAD)
            v_epilogue(MEMA_T, vm_a, slice(0, 2), MEMA + DSTEPS)
            angles_and_lambda()
            splits_to(MEMB + AHEAD)
            dve.wait_ge(lam_exp, 1)
            link(nc.vector.tensor_tensor(neglam[:, 0:1], neglam[:, 3:4], neglam[:, 2:3], ALU.subtract))
            link(nc.vector.tensor_scalar_add(neglam[:, 0:1], neglam[:, 0:1], -LAMBDA_INIT))
            v_epilogue(MEMA_T + 1, vm_a, slice(2, 4), MEMB)
            splits_to(MEMB + AHEAD + 2)
            norm(1)
            splits_to(MEMB + DSTEPS + AHEAD)
            v_epilogue(MEMB_T, vm_b, slice(0, 2), MEMB + DSTEPS)
            split_transposes(KC, [(GAIN_ROWS["a_pre"], xT_hi, xT_lo)], MEMB + DSTEPS + AHEAD, 0)
            splits_to(QLAT + AHEAD)
            v_epilogue(MEMB_T + 1, vm_b, slice(2, 4), QLAT)

            raw = scratch[:, 0].rearrange("p a b -> p (a b)")
            tmp = scratch[:, 1].rearrange("p a b -> p (a b)")

            def rotate(semaphore, value, row, width, c0, half, twice=False, src=None):
                dve.wait_ge(semaphore, value)
                v4 = lambda a: a[:, 0:TT * row].rearrange("p (t n) -> p t n", t=TT)[:, :, 0:width]\
                    .rearrange("p t (g d) -> p t g d", d=2 * half)
                xr, tr = v4(raw), v4(tmp)
                xs = xr if src is None else v4(src)
                g = width // (2 * half)
                wide = [P, TT, g, half]
                cos = cosine[:, :, c0:c0 + half].unsqueeze(2).to_broadcast(wide)
                sin = sine[:, :, c0:c0 + half].unsqueeze(2).to_broadcast(wide)
                a, b = (slice(0, half), slice(half, 2 * half))
                d = nc.vector.tensor_tensor(tr[:, :, :, a], xs[:, :, :, b], sin, ALU.mult)
                if not twice:
                    d.then_inc(pair_dve, 1)
                nc.vector.tensor_tensor(tr[:, :, :, b], xs[:, :, :, a], sin, ALU.mult)
                nc.vector.tensor_tensor(xr[:, :, :, a], xs[:, :, :, a], cos, ALU.mult)
                link(nc.vector.tensor_tensor(xr[:, :, :, b], xs[:, :, :, b], cos, ALU.mult))
                nc.vector.tensor_tensor(xr[:, :, :, a], xr[:, :, :, a], tr[:, :, :, a], ALU.subtract)
                d = nc.vector.tensor_tensor(xr[:, :, :, b], xr[:, :, :, b], tr[:, :, :, b], ALU.add)
                if twice:
                    link(d)
                    rows = raw[:, 0:TT * row].rearrange("p (t n) -> p t n", t=TT)
                    d = nc.vector.tensor_copy(rows[:, :, width:2 * width], rows[:, :, 0:width])
                d.then_inc(rope_ready, 1)

            def latent_epilogue(k, t, s_end, dst):
                dve.wait_ge(step_used, s_end)
                nc.vector.tensor_copy(lat[:, k, 1, :], ps[:, 2 * (t % 2) + 1, :]).then_inc(pair_dve, 1)
                norm(1, dst)

            splits_to(KVLAT + AHEAD)
            latent_epilogue(0, QLAT_T, KVLAT, diag)
            splits_to(QMEM + AHEAD)
            latent_epilogue(1, KVLAT_T, QMEM, diag_kv)
            split_transposes(4, [(GAIN_ROWS["q_norm"], latq_hi, latq_lo)])
            rotate(unrotated, 1, P, RD, 0, RD // 2, twice=True, src=ps[:, 6, 0:TT * P])
            splits_to(UQ + AHEAD)
            dve.wait_ge(step_used, UQ)
            nc.vector.tensor_copy(qmT_a[:, 2:4, :].rearrange("p h s -> p (h s)"),
                                  ps[:, 2 * (QMEM_T % 2) + 1, :]).then_inc(pair_dve, 1)
            split_transposes(4, [(GAIN_ROWS["kv_norm"], latk_hi, latk_lo)])
            for j in range(6):
                splits_to(UQ + (j + 1) * LSTEPS + AHEAD)
                rotate(unrotated, 2 + j, P, P, 0, RD // 2, src=ps[:, 7, 0:TT * P])
            for j in range(6):
                splits_to(UKV + (j + 1) * LSTEPS + AHEAD)
                v_epilogue(UKV_T + j, v_a, slice(2 * j, 2 * j + 2), UKV + (j + 1) * LSTEPS)

            def attend(items, first_item, scale):
                t0 = first_item
                is_b = first_item > 0

                def maxima(t):
                    kind, h = items[t]
                    dve.wait_ge(s_ready, t0 + t + 1)
                    m4 = stat[:, t % 4, :]
                    if kind == "mem":
                        b = 2 * (t % 2) if is_b else t % 4
                        n = 2
                        d = nc.vector.reduce_max(
                            m4[:, 0:2], ps[:, b, :].rearrange("p (q n) -> p q n", q=2), axis=AX)
                    else:
                        n = 4 if kind == "diff" else 2
                        for j in range(n // 2):
                            b = 2 * (t % 2) + j if is_b else t % 4
                            for q, (a, z) in enumerate(((0, P), (P, 3 * P))):
                                d = nc.vector.reduce_max(m4[:, 2 * j + q:2 * j + q + 1],
                                                         ps[:, b, a:z], axis=AX)
                    link(d)
                    sc = SCALE_B if kind == "mem" else scale
                    nc.vector.tensor_scalar(m4[:, 0:n], m4[:, 0:n], -sc, None, ALU.mult)\
                        .then_inc(max_ready, 1)

                def normalise(t):
                    kind, h = items[t]
                    dve.wait_ge(e_ready, t0 + t + 1)
                    m4 = stat[:, t % 4, :]
                    p = probs[:, t % 2]
                    cuts = ((0, 256), (256, 512)) if kind == "mem" else ((0, P), (P, 3 * P))
                    if kind == "diff":
                        link(nc.vector.reciprocal(inv_sum[:, h, :], m4[:, 4:8]))
                        link(nc.vector.scalar_tensor_tensor(
                            out=m4[:, 6:8], in0=inv_sum[:, h, 2:4], scalar=neglam[:, 0:1],
                            in1=m4[:, 4:6], op0=ALU.mult, op1=ALU.mult))
                        for q, (a, z) in enumerate(cuts):
                            d = nc.vector.scalar_tensor_tensor(
                                out=p[:, 0, a:z], in0=p[:, 1, a:z], scalar=m4[:, 6 + q:7 + q],
                                in1=p[:, 0, a:z], op0=ALU.mult, op1=ALU.add)
                    else:
                        link(nc.vector.reciprocal(m4[:, 4:6], m4[:, 4:6]))
                        for q, (a, z) in enumerate(cuts):
                            d = nc.vector.tensor_scalar(p[:, 0, a:z], p[:, 0, a:z],
                                                        m4[:, 4 + q:5 + q], None, ALU.mult)
                    d.then_inc(p_ready, 1)

                def output(t):
                    kind, h = items[t]
                    dve.wait_ge(o_hi, t0 + t + 1)
                    src = ps[:, 6 + t % 2, :]
                    if kind == "diff":
                        for q in range(TT):
                            d = nc.vector.tensor_scalar(
                                o_nat[:, h, q, :], src[:, VD * q:VD * (q + 1)],
                                inv_sum[:, h, q:q + 1], None, ALU.mult)
                        d.then_inc(o_lo, 1)
                    else:
                        ch = h if kind == "mla" else 12 + h
                        nc.vector.tensor_tensor(xT_lo[:, ch, :], src[:, 0:S],
                                                xT_hi[:, ch, :].bitcast(F32), ALU.subtract)\
                            .then_inc(o_lo, 1)

                for t in range(len(items) + 3):
                    if t < len(items):
                        maxima(t)
                    if 1 <= t <= len(items):
                        normalise(t - 1)
                    if t >= 3:
                        output(t - 3)
                    if is_b and t >= len(items):
                        if t == len(items):
                            dve.wait_ge(ostd_ready, 1)
                            link(nc.vector.reciprocal(osum[:, 2, :], osum[:, 1, :]))
                        for h in range(2 * (t - len(items)), 2 * (t - len(items)) + 2):
                            rstd = osum[:, 2, 2 * h:2 * h + 2].unsqueeze(2)
                            nc.vector.tensor_tensor(o_nat[:, h], o_nat[:, h],
                                                    rstd.to_broadcast([P, TT, VD]), ALU.mult)\
                                .then_inc(on_scaled, 1)

            attend(ITEMS_A, 0, SCALE_A)

            def wide_epilogue(s0, t0, steps, y, gain, last=False):
                count["gain"] += 1
                end = s0 + 4 * steps
                for j in range(3):
                    splits_to(s0 + (j + 1) * steps + AHEAD)
                    if j == 0:
                        dve.wait_ge(gain_landed, 16 * count["gain"])
                    dve.wait_ge(pair_act, t0 + j + 1)
                    pr, cols = 2 * ((t0 + j) % 2), slice(512 * j, 512 * (j + 1))
                    nc.vector.tensor_tensor(
                        y[:, :, cols], ps[:, pr:pr + 2, :],
                        gain[:, cols].unsqueeze(1).to_broadcast([P, TT, 512]), ALU.mult)\
                        .then_inc(pair_dve, 1)
                splits_to(end)

                def last_tile(t):
                    return nc.vector.tensor_tensor(y[:, t, 1536:2048],
                                                   ps[:, 2 * ((t0 + 3) % 2) + t, :],
                                                   gain[:, 1536:2048], ALU.mult)

                def update(t):
                    inverse_std(t, t + 1)
                    for a, z in X_PIECES:
                        cols = slice(a, z)
                        nc.vector.scalar_tensor_tensor(
                            out=x[:, t, cols], in0=y[:, t, cols], scalar=nrm[:, 4 + t:5 + t],
                            in1=x[:, t, cols], op0=ALU.mult, op1=ALU.add).then_inc(x_piece, 1)

                def sum_updated(t):
                    count["sq"] += 1
                    dve.wait_ge(sq_ready, count["sq"])
                    sums(len(X_PIECES), t, t + 1)

                def next_diagonal(t):
                    inverse_std(t, t + 1)
                    diagonal(diag, [t])

                count["bank"] += 1
                dve.wait_ge(bank_squared, count["bank"])
                sums(4, 0, 1)
                link(last_tile(0))
                update(0)
                if not last:
                    splits_to(end + 1)
                    sum_updated(0)
                dve.wait_ge(pair_act, t0 + 4)
                sums(4, 1, 2)
                last_tile(1).then_inc(pair_dve, 1)
                if not last:
                    next_diagonal(0)
                dve.wait_ge(pair_dve, t0 + 4)
                update(1)
                if not last:
                    splits_to(end + 2)
                    sum_updated(1)
                    next_diagonal(1)
                    splits_to(end + AHEAD)

            def ffn_epilogues(layer, s_in, t_in, g_count):
                splits_to(s_in + CUT)
                before = linked[0]

                def other_taps(i, j):
                    dve.wait_ge(pair_act, val(t_in + j + 1, 2, i))
                    for shift in (1, 2):
                        for m4 in range(4):
                            ch = i * 4 + (m4 + j * FC)
                            u = ps[:, 2 * ((t_in + j) % 2) + m4 // 2,
                                   256 * (m4 % 2):256 * (m4 % 2) + S - shift]
                            c = scratch[:, j, m4, shift:S]
                            d = nc.vector.scalar_tensor_tensor(
                                out=c, in0=u, scalar=conv[:, layer, 2 - shift, bass.ds(ch, 1)],
                                in1=c, op0=ALU.mult, op1=ALU.add)
                        if shift == 1:
                            link(d, i * 2)
                    d.then_inc(pair_dve, 1)

                def gate_times_value(i):
                    dve.wait_ge(pair_dve, val(t_in + 2, 2, i))
                    dve.wait_ge(gate_ready, val(g_count + 1, 1, i))
                    nc.vector.tensor_tensor(scratch[:, 1], scratch[:, 0], scratch[:, 1], ALU.mult)\
                        .then_inc(h_ready, 1)

                def lo_half(i):
                    dve.wait_ge(h_hi, val(g_count + 1, 1, i))
                    hs = bass.ds(i * 4, 4)
                    nc.vector.tensor_tensor(hT_lo[:, hs, :], scratch[:, 1], hT_hi[:, hs, :].bitcast(F32),
                                            ALU.subtract).then_inc(h_lo, 1)

                with dve.Fori(0, FJ) as i:
                    for j in range(2):
                        for k in range(DSTEPS):
                            split(s_in + j * DSTEPS + k + CUT, 2 * DSTEPS, i)
                            ahead = k + CUT + 1 - DSTEPS
                            if ahead == 3:
                                other_taps(i, j)
                            if ahead == 4 and j == 1:
                                gate_times_value(i)
                            if ahead == 7 and j == 1:
                                lo_half(i)
                assert linked[0] - before == 2
                linked[0] = before + 2 * FJ
                n_split[0] = s_in + 2 * FJ * DSTEPS + CUT

            wide_epilogue(OA, OA_T, DSTEPS, y_o, gain_o)
            split_transposes(KC, [(GAIN_ROWS["ffn_pre"], xT_hi, xT_lo)], IN0)
            ffn_epilogues(0, IN0, IN0_T, 0)
            wide_epilogue(OUT0, OUT0_T, FSTEPS, y_f, gain_f)
            split_transposes(KC, [(GAIN_ROWS["shared"], xT_hi, xT_lo),
                                  (GAIN_ROWS["b_pre"], xbT_hi, xbT_lo)], SKV)
            for j in range(BH):
                splits_to(SKV + (j + 1) * DSTEPS + AHEAD)
                dve.wait_ge(pair_act, SKV_T + j + 1)
                pr = 2 * ((SKV_T + j) % 2)
                nc.vector.tensor_copy(v_b[:, :, j, :], ps[:, pr:pr + 2, 256:512])
                rotate(pair_act, SKV_T + j + 1, 512, 256, 32, HD // 2)
            for j in range(3):
                splits_to(BQ + (j + 1) * DSTEPS + AHEAD)
                rotate(pair_act, BQ_T + j + 1, 512, 512, 32, HD // 2)
            splits_to(OB + AHEAD)
            dve.wait_ge(step_used, OB)
            nc.vector.tensor_copy(qmT_b[:, 2:4, :].rearrange("p h s -> p (h s)"),
                                  ps[:, 2 * ((BQ_T + 3) % 2) + 1, :]).then_inc(pair_dve, 1)
            attend(ITEMS_B, len(ITEMS_A), SCALE_B)
            for h in range(BH):
                count["N"] += 1
                dve.wait_ge(tr_hi, count["N"])
                for c in range(2):
                    g0 = GAIN_ROWS["subln"] + c
                    d = nc.vector.scalar_tensor_tensor(
                        out=xT_lo[:, 2 * h + c, :], in0=ps[:, SUB_BANKS[h], 256 * c:256 * c + S],
                        scalar=gcol[:, g0:g0 + 1], in1=xT_hi[:, 2 * h + c, :].bitcast(F32),
                        op0=ALU.mult, op1=ALU.subtract)
                d.then_inc(tr_lo, 1)
            wide_epilogue(OB, OB_T, DSTEPS, y_o, gain_o)
            split_transposes(KC, [(GAIN_ROWS["ffn_pre"] + KC, xT_hi, xT_lo)], IN1)
            ffn_epilogues(1, IN1, IN1_T, FJ)
            wide_epilogue(OUT1, OUT1_T, FSTEPS, y_f, gain_f, last=True)


_INS = ["x", "mem", "positions", "a_attn_norm_pre", "a_w_in", "a_q_norm", "a_w_uq", "a_kv_norm",
        "a_w_ukv", "a_mem_norm", "a_w_mem_kv", "a_w_o", "a_attn_norm_post", "shared_kv_norm",
        "shared_w_kv", "b_attn_norm_pre", "b_w_in", "b_lambda_q1", "b_lambda_k1", "b_lambda_q2",
        "b_lambda_k2", "b_subln", "b_mem_norm", "b_w_mem_kv", "b_w_o", "b_attn_norm_post",
        "ffn_norm_pre", "ffn_w_in", "ffn_conv_w", "ffn_conv_b", "ffn_w_out", "ffn_norm_post"]


_GAINS = ["a_attn_norm_pre", "a_mem_norm", "b_mem_norm", "b_attn_norm_pre", "shared_kv_norm",
          "ffn_norm_pre", "a_q_norm", "a_kv_norm", "b_subln"]
_LAMBDAS = ["b_lambda_q1", "b_lambda_k1", "b_lambda_q2", "b_lambda_k2"]
_PACKED = _GAINS + _LAMBDAS + ["ffn_conv_w", "ffn_conv_b"]


def build(nc, a, inv_freq, out):
    w = {n: a[n][0] for n in ("a_w_in", "a_w_uq", "a_w_ukv", "a_w_mem_kv", "a_w_o", "b_w_in",
                              "b_w_mem_kv", "b_w_o")}
    w["shared_w_kv"] = a["shared_w_kv"]
    for layer in range(2):
        w[f"ffn_w_in{layer}"] = a["ffn_w_in"][layer]
        w[f"ffn_w_out{layer}"] = a["ffn_w_out"][layer]
    vec = {
        "gains": a["gains"], "conv": a["conv"], "lambda": a["lambda"],
        "a_post": a["a_attn_norm_post"][0], "b_post": a["b_attn_norm_post"][0],
        "ffn_post0": a["ffn_norm_post"][0], "ffn_post1": a["ffn_norm_post"][1],
    }
    program(nc, a["x"][0], a["mem"][0], a["positions"][0], inv_freq, w, vec, out[0])


def kernel(**inputs):
    import concourse.bacc as bacc
    from concourse.bass_utils import run_bass_kernel_spmd

    nc = bacc.Bacc("TRN2", target_bir_lowering=False, num_devices=1)
    arrays, aps = {}, {}

    def give(name, v):
        arrays[f"in_{name}"] = np.ascontiguousarray(v)
        aps[name] = nc.dram_tensor(f"in_{name}", v.shape, mybir.dt.from_np(v.dtype),
                                   kind="ExternalInput").ap()

    given = {name: np.asarray(inputs[name]) for name in _INS}
    for name in _INS:
        if name not in _PACKED:
            give(name, given[name])
    rows = [given[n].reshape(-1, P) for n in _GAINS]
    give("gains", np.concatenate(rows))
    taps = np.concatenate([given["ffn_conv_w"], given["ffn_conv_b"][:, None]], axis=1)
    give("conv", taps.reshape(2, 4, 2 * FC, P).transpose(2, 0, 1, 3).reshape(2 * FC, 8 * P))
    give("lambda", np.concatenate([given[n].reshape(-1) for n in _LAMBDAS]))
    freq = np.concatenate([np.exp(np.float32(-math.log(THETA)) * np.arange(n, dtype=np.float32)
                                  * np.float32(1.0 / n)).astype(np.float32)
                           for n in (RD // 2, HD // 2)])
    arrays["in_freq"] = freq
    f = nc.dram_tensor("in_freq", freq.shape, F32, kind="ExternalInput").ap()
    out = nc.dram_tensor("out_0", (1, S, D), F32, kind="ExternalOutput").ap()
    build(nc, aps, f, out)
    r = run_bass_kernel_spmd(nc, [arrays], core_ids=[0])
    return r.results[0]["out_0"]
```
